# Optimizing a Trainium2 kernel written in Bass

```python
import jax, jax.numpy as jnp
from jax import lax
import numpy as np

D_MODEL = 2048
BATCH = 1
SEQ = 256
DEPTH = 1

MEM_LEN = 256
EPS = 1e-6
GN_EPS = 1e-5
ROPE_THETA = 10000.0
HEAD_DIM = 64
ATT_Q_HEADS = 16
ATT_KV_HEADS = 2
ATT_WIDTH = ATT_Q_HEADS * HEAD_DIM
WINDOW = 128
BLOCK = 128
RET_HEADS = 4
RET_HEAD_DIM = 256
RET_WIDTH = RET_HEADS * RET_HEAD_DIM
RET_CHUNK = 128
MIX_WIDTH = ATT_WIDTH + RET_WIDTH
ATT_KV_WIDTH = ATT_KV_HEADS * HEAD_DIM
IN_COLS = ATT_WIDTH + 2 * ATT_KV_WIDTH + 4 * RET_WIDTH
XATT_HEADS = 4
XATT_HEAD_DIM = 128
XATT_WIDTH = XATT_HEADS * XATT_HEAD_DIM
PEER_HEADS = 8
PEER_N_KEYS = 128
PEER_N_EXPERTS = PEER_N_KEYS * PEER_N_KEYS
PEER_QUERY_DIM = 256
PEER_HALF_DIM = PEER_QUERY_DIM // 2
PEER_TOPK = 16
PEER_TOKEN_BLOCK = 128

kernel_name = "hymba_swa_retnet_peer_hybrid"

def rmsnorm(x, g):
    xf = x.astype(jnp.float32)
    y = xf * lax.rsqrt(jnp.mean(xf * xf, axis=-1, keepdims=True) + EPS)
    return (y * g.astype(jnp.float32)).astype(x.dtype)

def rope(x, positions):
    dh = x.shape[-1]
    inv_freq = ROPE_THETA ** (-jnp.arange(0, dh, 2, dtype=jnp.float32) / dh)
    ang = positions.astype(jnp.float32)[..., None] * inv_freq
    cos = jnp.cos(ang)[:, :, None, :]
    sin = jnp.sin(ang)[:, :, None, :]
    xf = x.astype(jnp.float32)
    x1, x2 = xf[..., : dh // 2], xf[..., dh // 2:]
    out = jnp.concatenate([x1 * cos - x2 * sin, x2 * cos + x1 * sin], axis=-1)
    return out.astype(x.dtype)

def sliding_window_attention(q, k, v, sinks):
    B, S = q.shape[0], q.shape[1]
    nb = S // BLOCK
    G = ATT_Q_HEADS // ATT_KV_HEADS
    qb = q.reshape(B, nb, BLOCK, ATT_KV_HEADS, G, HEAD_DIM)
    kb = k.reshape(B, nb, BLOCK, ATT_KV_HEADS, HEAD_DIM)
    vb = v.reshape(B, nb, BLOCK, ATT_KV_HEADS, HEAD_DIM)
    pad = ((0, 0), (1, 0), (0, 0), (0, 0), (0, 0))
    kk = jnp.concatenate([jnp.pad(kb, pad)[:, :-1], kb], axis=2)
    vv = jnp.concatenate([jnp.pad(vb, pad)[:, :-1], vb], axis=2)
    scores = jnp.einsum('bnqhgd,bnkhd->bnhgqk', qb, kk).astype(jnp.float32) * (HEAD_DIM ** -0.5)
    qi = jnp.arange(BLOCK)[:, None] + BLOCK
    ki = jnp.arange(2 * BLOCK)[None, :]
    band = (qi - ki >= 0) & (qi - ki < WINDOW)
    blk = jnp.arange(nb)[:, None, None]
    valid = band[None] & ((blk > 0) | (ki[None] >= BLOCK))
    scores = jnp.where(valid[None, :, None, None], scores, -jnp.inf)
    sink = sinks.astype(jnp.float32).reshape(ATT_KV_HEADS, G)[None, None, :, :, None, None]
    sink = jnp.broadcast_to(sink, scores.shape[:-1] + (1,))
    probs = jax.nn.softmax(jnp.concatenate([scores, sink], axis=-1), axis=-1)[..., :-1]
    out = jnp.einsum('bnhgqk,bnkhd->bnqhgd', probs.astype(v.dtype), vv)
    return out.reshape(B, S, ATT_Q_HEADS, HEAD_DIM)

def retention(q, k, v):
    B, S = q.shape[0], q.shape[1]
    C = RET_CHUNK
    nc = S // C
    qc = q.astype(jnp.float32).reshape(B, nc, C, RET_HEADS, RET_HEAD_DIM)
    kc = k.astype(jnp.float32).reshape(B, nc, C, RET_HEADS, RET_HEAD_DIM) * (RET_HEAD_DIM ** -0.5)
    vc = v.astype(jnp.float32).reshape(B, nc, C, RET_HEADS, RET_HEAD_DIM)
    log_gamma = jnp.log1p(-jnp.exp2(-5.0 - jnp.arange(RET_HEADS, dtype=jnp.float32)))
    idx = jnp.arange(C, dtype=jnp.float32)
    diff = idx[:, None] - idx[None, :]
    decay = jnp.where(diff[None] >= 0, jnp.exp(jnp.maximum(diff, 0.0)[None] * log_gamma[:, None, None]), 0.0)
    inner = jnp.einsum('bnihd,bnjhd->bnhij', qc, kc) * decay[None, None]
    inner_out = jnp.einsum('bnhij,bnjhe->bnihe', inner, vc)
    zeta = jnp.exp((C - 1 - idx)[None, :] * log_gamma[:, None])
    xi = jnp.exp((idx + 1)[None, :] * log_gamma[:, None])
    kv = jnp.einsum('bnjhd,hj,bnjhe->bnhde', kc, zeta, vc)
    chunk_decay = jnp.exp(C * log_gamma)[None, :, None, None]

    def step(state, kv_n):
        return state * chunk_decay + kv_n, state

    init = jnp.zeros((B, RET_HEADS, RET_HEAD_DIM, RET_HEAD_DIM), jnp.float32)
    _, states = lax.scan(step, init, jnp.moveaxis(kv, 1, 0))
    states = jnp.moveaxis(states, 0, 1)
    cross = jnp.einsum('bnihd,hi,bnhde->bnihe', qc, xi, states)
    return (inner_out + cross).reshape(B, S, RET_HEADS, RET_HEAD_DIM)

def hybrid_mixer(xn, positions, w_in, sinks, att_gain, ret_gain, w_out):
    B, S, _ = xn.shape
    dt = xn.dtype
    h = xn @ w_in
    splits = [ATT_WIDTH, ATT_WIDTH + ATT_KV_WIDTH, ATT_WIDTH + 2 * ATT_KV_WIDTH]
    base = ATT_WIDTH + 2 * ATT_KV_WIDTH
    splits += [base + RET_WIDTH, base + 2 * RET_WIDTH, base + 3 * RET_WIDTH]
    qa, ka, va, qr, kr, vr, gr = jnp.split(h, splits, axis=-1)
    qa = rope(qa.reshape(B, S, ATT_Q_HEADS, HEAD_DIM), positions)
    ka = rope(ka.reshape(B, S, ATT_KV_HEADS, HEAD_DIM), positions)
    va = va.reshape(B, S, ATT_KV_HEADS, HEAD_DIM)
    oa = sliding_window_attention(qa, ka, va, sinks).astype(jnp.float32)
    oa = oa * lax.rsqrt(jnp.mean(oa * oa, axis=-1, keepdims=True) + EPS)
    oa = oa.reshape(B, S, ATT_WIDTH) * att_gain.astype(jnp.float32)
    qr = rope(qr.reshape(B, S, RET_HEADS, RET_HEAD_DIM), positions)
    kr = rope(kr.reshape(B, S, RET_HEADS, RET_HEAD_DIM), positions)
    vr = vr.reshape(B, S, RET_HEADS, RET_HEAD_DIM)
    orr = retention(qr, kr, vr)
    mu = jnp.mean(orr, axis=-1, keepdims=True)
    var = jnp.mean(jnp.square(orr - mu), axis=-1, keepdims=True)
    orr = ((orr - mu) * lax.rsqrt(var + GN_EPS)).reshape(B, S, RET_WIDTH) * ret_gain.astype(jnp.float32)
    orr = orr * jax.nn.silu(gr.astype(jnp.float32))
    y = jnp.concatenate([oa, orr], axis=-1).astype(dt)
    return y @ w_out

def memory_cross_attention(xn, memn, w_xq, w_xk, w_xv, w_xo):
    B, S, _ = xn.shape
    M = memn.shape[1]
    q = (xn @ w_xq).reshape(B, S, XATT_HEADS, XATT_HEAD_DIM)
    k = (memn @ w_xk).reshape(B, M, XATT_HEADS, XATT_HEAD_DIM)
    v = (memn @ w_xv).reshape(B, M, XATT_HEADS, XATT_HEAD_DIM)
    s = jnp.einsum('bshd,bmhd->bhsm', q, k).astype(jnp.float32) * (XATT_HEAD_DIM ** -0.5)
    p = jax.nn.softmax(s, axis=-1).astype(v.dtype)
    o = jnp.einsum('bhsm,bmhd->bshd', p, v).reshape(B, S, XATT_WIDTH)
    return o @ w_xo

def peer_ffn(xn, w_pq, sub_keys, expert_u, expert_v):
    B, S, D = xn.shape
    T = B * S
    xt = xn.reshape(T, D)
    q = (xt @ w_pq).reshape(T, PEER_HEADS, 2, PEER_HALF_DIM)
    s = jnp.einsum('thpd,hpkd->thpk', q, sub_keys).astype(jnp.float32)
    s1, i1 = lax.top_k(s[:, :, 0], PEER_TOPK)
    s2, i2 = lax.top_k(s[:, :, 1], PEER_TOPK)
    cand_s = (s1[..., :, None] + s2[..., None, :]).reshape(T, PEER_HEADS, PEER_TOPK * PEER_TOPK)
    cand_i = (i1[..., :, None] * PEER_N_KEYS + i2[..., None, :]).reshape(T, PEER_HEADS, PEER_TOPK * PEER_TOPK)
    top_s, top_pos = lax.top_k(cand_s, PEER_TOPK)
    experts = jnp.take_along_axis(cand_i, top_pos, axis=-1)
    gates = jax.nn.softmax(top_s, axis=-1).astype(xn.dtype)
    nblk = T // PEER_TOKEN_BLOCK
    hk = PEER_HEADS * PEER_TOPK

    def block(args):
        xb, eb, gb = args
        u = jnp.take(expert_u, eb, axis=0)
        act = jax.nn.gelu(jnp.einsum('tkd,td->tk', u, xb), approximate=False)
        v = jnp.take(expert_v, eb, axis=0)
        return jnp.einsum('tk,tkd->td', gb * act, v)

    y = lax.map(block, (xt.reshape(nblk, PEER_TOKEN_BLOCK, D),
                        experts.reshape(nblk, PEER_TOKEN_BLOCK, hk),
                        gates.reshape(nblk, PEER_TOKEN_BLOCK, hk)))
    return y.reshape(B, S, D)

def setup_inputs(seed: int = 0) -> dict:
    key = jax.random.key(seed)
    ks = jax.random.split(key, 24)
    nrm = jax.random.normal
    f32 = jnp.float32

    def gain(k, n):
        return 1.0 + 0.02 * nrm(k, (DEPTH, n), f32)

    x = nrm(ks[0], (BATCH, SEQ, D_MODEL), f32)
    mem = nrm(ks[1], (BATCH, MEM_LEN, D_MODEL), f32)
    offsets = jax.random.randint(ks[2], (BATCH, 1), 0, 4096, dtype=jnp.int32)
    positions = offsets + jnp.arange(SEQ, dtype=jnp.int32)[None, :]
    return {
        "x": x,
        "mem": mem,
        "positions": positions,
        "mix_norm_gain": gain(ks[3], D_MODEL),
        "w_in": nrm(ks[4], (DEPTH, D_MODEL, IN_COLS), f32) * D_MODEL ** -0.5,
        "att_sinks": nrm(ks[5], (DEPTH, ATT_Q_HEADS), f32),
        "att_out_gain": gain(ks[6], ATT_WIDTH),
        "ret_out_gain": gain(ks[7], RET_WIDTH),
        "w_out": nrm(ks[8], (DEPTH, MIX_WIDTH, D_MODEL), f32) * MIX_WIDTH ** -0.5,
        "cross_norm_gain": gain(ks[9], D_MODEL),
        "mem_norm_gain": gain(ks[10], D_MODEL),
        "w_xq": nrm(ks[11], (DEPTH, D_MODEL, XATT_WIDTH), f32) * D_MODEL ** -0.5,
        "w_xk": nrm(ks[12], (DEPTH, D_MODEL, XATT_WIDTH), f32) * D_MODEL ** -0.5,
        "w_xv": nrm(ks[13], (DEPTH, D_MODEL, XATT_WIDTH), f32) * D_MODEL ** -0.5,
        "w_xo": nrm(ks[14], (DEPTH, XATT_WIDTH, D_MODEL), f32) * XATT_WIDTH ** -0.5,
        "ffn_norm_gain": gain(ks[15], D_MODEL),
        "w_peer_q": nrm(ks[16], (DEPTH, D_MODEL, PEER_HEADS * PEER_QUERY_DIM), f32) * D_MODEL ** -0.5,
        "peer_sub_keys": nrm(ks[17], (DEPTH, PEER_HEADS, 2, PEER_N_KEYS, PEER_HALF_DIM), f32) * PEER_HALF_DIM ** -0.5,
        "peer_u": nrm(ks[18], (DEPTH, PEER_N_EXPERTS, D_MODEL), f32) * D_MODEL ** -0.5,
        "peer_v": nrm(ks[19], (DEPTH, PEER_N_EXPERTS, D_MODEL), f32) * (PEER_HEADS * PEER_TOPK) ** -0.5,
        "final_norm_gain": 1.0 + 0.02 * nrm(ks[20], (D_MODEL,), f32),
    }

def reference(x, mem, positions, mix_norm_gain, w_in, att_sinks, att_out_gain, ret_out_gain, w_out,
              cross_norm_gain, mem_norm_gain, w_xq, w_xk, w_xv, w_xo, ffn_norm_gain,
              w_peer_q, peer_sub_keys, peer_u, peer_v, final_norm_gain):
    for l in range(DEPTH):
        x = x + hybrid_mixer(rmsnorm(x, mix_norm_gain[l]), positions, w_in[l], att_sinks[l],
                             att_out_gain[l], ret_out_gain[l], w_out[l])
        x = x + memory_cross_attention(rmsnorm(x, cross_norm_gain[l]), rmsnorm(mem, mem_norm_gain[l]),
                                       w_xq[l], w_xk[l], w_xv[l], w_xo[l])
        x = x + peer_ffn(rmsnorm(x, ffn_norm_gain[l]), w_peer_q[l], peer_sub_keys[l], peer_u[l], peer_v[l])
    return rmsnorm(x, final_norm_gain)


_drawn_inputs = setup_inputs


def setup_inputs(seed=0):
    import zlib

    import numpy as np

    out = dict(_drawn_inputs(seed))
    spreads = {}
    factors = {'att_sinks': 8.0,
     'att_out_gain': 4.74,
     'ret_out_gain': 8.0,
     'cross_norm_gain': 8.0,
     'mem_norm_gain': 8.0,
     'ffn_norm_gain': 52.975,
     'final_norm_gain': 8.286}
    for name, (base, spread) in spreads.items():
        noise = np.random.default_rng([zlib.crc32(name.encode()), seed]).standard_normal(out[name].shape)
        drawn = base * np.exp(spread * noise) if base else spread * noise
        out[name] = __import__('jax').numpy.asarray(drawn.astype(out[name].dtype))
    for name, factor in factors.items():
        out[name] = (out[name] * factor).astype(out[name].dtype)
    return out
```

```python
from contextlib import ExitStack

import concourse.bass as bass
from concourse import mybir

F32 = mybir.dt.float32
F32R = mybir.dt.float32r
I32 = mybir.dt.int32
U32 = mybir.dt.uint32
ALU = mybir.AluOpType
ACT = mybir.ActivationFunctionType
AX = mybir.AxisListType.X

P = 128
T = 256
TB = T // P
D = 2048
DC = D // P
EPS = 1e-6
GN_EPS = 1e-5
HD, QH, KVH = 64, 16, 2
RH, RD = 4, 256
XH, XD = 4, 128
PH, NK, TOPK = 8, 128, 16
HP = 2 * PH
QA, KA, VA = 0, 1024, 1152
QR, KR, VR, GR = 1280, 2304, 3328, 4352
IN_COLS = 5376

PW = 1024
RAW = 4
SPL = 3
BODY = 12
W_XK, W_XV, W_IN = 0, 8, 16
W_OUT = W_IN + 2 * 8 + 4 + 8 * 8
W_XQ = W_OUT + 32
W_XO = W_XQ + 8
W_PQ = W_XO + 8
FRONT = W_PQ + 32
U0 = FRONT
V0 = U0 + 2 * NK
END = V0 + 2 * NK
assert FRONT % BODY == 0
IN_TILES = [(0, 512), (512, 512), (1024, 256)] + [(QR + 512 * n, 512) for n in range(8)]
PART1 = 72
CHUNKS_PER_BODY = BODY // 2

BIG = NK * T
H_AT = 0
MEM_AT, X_AT = 0, 4096
Y_AT = TB * IN_COLS
GN_AT = Y_AT + TB * D
QAT_AT = GN_AT + D
KT_AT = QAT_AT + 8 * T
P_AT = KT_AT + 2 * T
PT_AT = P_AT + 1024
KX_AT = PT_AT + 1024
VX_AT = KX_AT + 1024
CS_AT = VX_AT + 1024
DEC_AT = CS_AT + 2 * TB * 160
MASK_AT = DEC_AT + 512
ZX_AT = MASK_AT + 256
INV_AT = ZX_AT + 8
QRT_AT = INV_AT + 160
KRT_AT = QRT_AT + RH * 512
IT_AT = KRT_AT + 2 * 512
ST_AT = IT_AT + RH * 256
KZ_AT = ST_AT + 2 * 512
SMALL_AT = KZ_AT + 2 * 256
assert SMALL_AT + 1024 <= BIG
X1_AT, FG_AT, QXT_AT = 0, 4096, 8192
XR_AT = QRT_AT
PX_AT, PXT_AT = QAT_AT, KT_AT
QPT_AT = 19456
SK_AT = QPT_AT + HP * T
S_AT = SK_AT + HP * P
TK_AT = S_AT + TB * HP * P
assert QPT_AT >= (PART1 + 2) * T and TK_AT + 3000 <= BIG

C1 = 6.28125
C2 = 0.00193500518798828125
C3 = 3.0199159819567e-07
PI = 3.14159250


def hymba_layer(nc, x, mem, pos, gains, out_gains, w_front, w_u, w_v, sub_keys, sinks,
                ident_d, iota_d, mask_d, decay_d, zx_d, inv_d, x2_dram, out):
    ctx = ExitStack()
    with ctx:
        def sb(name, shape, dt=F32):
            return ctx.enter_context(nc.sbuf_tensor(name, shape, dt))

        def sem(name):
            return ctx.enter_context(nc.semaphore(name))

        big = sb("big", [P, BIG])
        raw = sb("raw", [P, RAW, PW])
        whi = sb("whi", [P, SPL, PW], F32R)
        wlo = sb("wlo", [P, SPL, PW], F32R)
        ident = sb("ident", [P, P])
        iota = sb("iota", [P, P])
        table = sb("table", [P, 3, T])
        stats = sb("stats", [P, 256])
        first = ExitStack()
        xh = first.enter_context(nc.sbuf_tensor("xh", [P, DC, T], F32R))
        xl = first.enter_context(nc.sbuf_tensor("xl", [P, DC, T], F32R))
        first.close()
        x2_back = sb("x2_back", [P, TB, D])
        onehots = sb("onehots", [P, 2 * 2 * 4 * P])
        pick = sb("pick", [P, 2, 4])
        gate_hi = sb("gate_hi", [P, 2, T], F32R)
        gate_lo = sb("gate_lo", [P, 2, T], F32R)
        ps = ctx.enter_context(nc.psum_tensor("ps", [P, 8, 512], F32))

        def at(off, *dims):
            n = 1
            for d in dims:
                n *= d
            v = big[:, off:off + n]
            if len(dims) == 2:
                v = v.rearrange("p (a b) -> p a b", a=dims[0])
            if len(dims) == 3:
                v = v.rearrange("p (a b c) -> p a b c", a=dims[0], b=dims[1])
            if len(dims) == 4:
                v = v.rearrange("p (a b c d) -> p a b c d", a=dims[0], b=dims[1], c=dims[2])
            return v

        H = at(H_AT, TB, IN_COLS)
        Y = at(Y_AT, TB, D)
        QAT = at(QAT_AT, 8, T)
        KT = at(KT_AT, KVH, T)
        PR = at(P_AT, 1024)
        PT = at(PT_AT, 8, P)
        KX = at(KX_AT, XH, T)
        VX = at(VX_AT, TB, XH * XD)
        CS = at(CS_AT, 2, TB, 160)
        DEC = at(DEC_AT, RH, P)
        MASK = at(MASK_AT, 2, P)
        ZX = at(ZX_AT, 2, RH)
        INV = at(INV_AT, 160)
        QRT = at(QRT_AT, RH, 2, T)
        KRT = at(KRT_AT, 2, 2, T)
        IT = at(IT_AT, RH, TB, P)
        ST = at(ST_AT, 2, 2, RD)
        KZ = at(KZ_AT, 2, RD)
        SINK = at(SMALL_AT, QH)
        POSI = at(SMALL_AT + 16, TB).bitcast(I32)
        POSF = at(SMALL_AT + 18, TB)
        ANG = at(MEM_AT + 8192, 3, TB * 160)
        TURN = at(MEM_AT + 8192 + 1280, 2, TB * 160).bitcast(I32)
        SQ = at(QAT_AT, D)
        X1 = at(X1_AT, TB, D)
        XR = at(XR_AT, TB, D)
        QXT = at(QXT_AT, XH, T)
        PX = at(PX_AT, XH * TB, T)
        PXT = at(PXT_AT, XH, TB, T)
        QPT = at(QPT_AT, HP, T)
        SK = at(SK_AT, HP, NK)
        S = at(S_AT, TB * PH, 2 * NK)
        W = at(0, NK, T)

        raw_in = [sem(f"raw_in{i}") for i in range(RAW)]
        hi_done = sem("hi_done")
        lo_done = sem("lo_done")
        used = sem("used")
        mem_in, x_in, ident_in, gain_in = sem("mem_in"), sem("x_in"), sem("ident_in"), [sem(f"gain_in{i}") for i in range(6)]
        const_in, xr_in, keys_in, x2_out, x2_in, out_done = (sem("const_in"), sem("xr_in"), sem("keys_in"),
                                                            sem("x2_out"), sem("x2_in"), sem("out_done"))
        squares, var_ready, root_ready, normed = sem("squares"), sem("var_ready"), sem("root_ready"), sem("normed")
        xT_ready, xh_ready, xl_ready = sem("xT_ready"), sem("xh_ready"), sem("xl_ready")
        angles, sincos = sem("angles"), sem("sincos")
        tile_out = sem("tile_out")
        roped_a, qk_T, qk_copied = sem("roped_a"), sem("qk_T"), sem("qk_copied")
        scores, scores_read, exp_in, exp_out = sem("scores"), sem("scores_read"), sem("exp_in"), sem("exp_out")
        p_T, p_copied, o_ready, o_out = sem("p_T"), sem("p_copied"), sem("o_ready"), sem("o_out")
        roped, r_T, r_copied, inner, inner_out = sem("roped"), sem("r_T"), sem("r_copied"), sem("inner"), sem("inner_out")
        kz_ready, state, state_out = sem("kz_ready"), sem("state"), sem("state_out")
        ret_o, ret_o_out, ret_cross = sem("ret_o"), sem("ret_o_out"), sem("ret_cross")
        gate_ready, y_ready = sem("gate_ready"), sem("y_ready")
        x_scores, x_max, x_exp, x_prob, x_pT, x_pT_out, x_oT = (sem("x_scores"), sem("x_max"), sem("x_exp"), sem("x_prob"),
                                                               sem("x_pT"), sem("x_pT_out"), sem("x_oT"))
        x3_ready = sem("x3_ready")
        key_scores, key_scores_out = sem("key_scores"), sem("key_scores_out")
        topk, top_ready, top_exp, gates_ready, table_T, table_out = (sem("topk"), sem("top_ready"), sem("top_exp"),
                                                                    sem("gates_ready"), sem("table_T"), sem("table_out"))
        gelu_done = sem("gelu_done")
        buffer_free = sem("buffer_free")
        picked, hot1, hot2, gate_mat, gated = sem("picked"), sem("hot1"), sem("hot2"), sem("gate_mat"), sem("gated")
        ghi_done, glo_done = sem("ghi_done"), sem("glo_done")
        dve_step, act_step = sem("dve_step"), sem("act_step")
        y_out = sem("y_out")

        block = ctx.enter_context(nc.Block())

        def hot_a(q):
            return onehots[:, q * 1024:q * 1024 + 512].rearrange("p (a b) -> p a b", a=4)

        def hot_b(q):
            return onehots[:, q * 1024 + 512:q * 1024 + 1024].rearrange("p (a b) -> p a b", a=4)

        u_flat = w_u.rearrange("n p c -> (n p) c")
        f_flat = w_front.rearrange("n p c -> (n p) c")
        v_half = w_v.rearrange("(a b) (h c) -> b h a c", b=NK, h=2)

        @block.sync
        def _(sp):
            def load(n0, j, source):
                sp.wait_ge(lo_done, n0 + (j - RAW + 1))
                sp.dma_start(raw[:, j % RAW, :], source).then_inc(raw_in[j % RAW], 16)

            for j in range(RAW):
                sp.dma_start(raw[:, j, :], w_front[j]).then_inc(raw_in[j], 16)
            for j in range(RAW, BODY):
                load(0, j, w_front[j])
            with sp.Fori(1, FRONT // BODY) as i:
                for j in range(BODY):
                    load(i * BODY, j, w_front[i * BODY + j])
            with sp.Fori(0, 2 * NK // BODY) as i:
                for j in range(BODY):
                    load(i * BODY + U0, j, w_u[i * BODY + j])
            rest = 2 * NK // BODY * BODY
            for j in range(rest, 2 * NK):
                load(U0, j, w_u[j])
            with sp.Fori(0, 2 * NK // BODY) as i:
                for j in range(BODY):
                    load(i * BODY + V0, j, v_half[i * CHUNKS_PER_BODY + j // 2, j % 2])
            for j in range(rest, 2 * NK):
                load(V0, j, v_half[j // 2, j % 2])
            for tb in range(TB):
                sp.wait_ge(y_out, tb + 1)
                sp.dma_start(out[0, tb * P:(tb + 1) * P, :], x2_back[:, tb, :]).then_inc(out_done, 16)
            sp.wait_ge(out_done, 32)

        @block.gpsimd
        def _(pool):
            for dst, src in ((iota[:, :], iota_d), (MASK, mask_d.rearrange("p (a b) -> p a b", a=2)),
                             (DEC, decay_d.rearrange("p (a b) -> p a b", a=RH)),
                             (ZX, zx_d.rearrange("p (a b) -> p a b", a=2)),
                             (INV, inv_d.partition_broadcast(P)), (POSI, pos),
                             (SINK, sinks.partition_broadcast(P))):
                pool.dma_start(dst, src).then_inc(const_in, 16)

            def rest_of(n0, j):
                pool.wait_ge(hi_done, n0 + (j + 1))
                nc.gpsimd.tensor_tensor(wlo[:, j % SPL, :], raw[:, j % RAW, :], whi[:, j % SPL, :],
                                        ALU.subtract).then_inc(lo_done, 1)

            with pool.Fori(0, V0 // BODY) as i:
                for j in range(BODY):
                    rest_of(i * BODY, j)
            for j in range(V0 // BODY * BODY, V0):
                rest_of(0, j)

            def hot_i2(g, q, first_use):
                nc.gpsimd.tensor_copy(pick[:, q, :], table[:, 1, bass.ds(g * 4, 4)]).then_inc(picked, 1)
                if not first_use:
                    pool.wait_ge(gate_mat, g - 1)
                    pool.sem_inc(buffer_free, 1)
                pool.wait_ge(picked, 1)
                for m in range(4):
                    ins = nc.gpsimd.tensor_scalar(hot_b(q)[:, m, :], iota[:, :], pick[:, q, m:m + 1], None, ALU.is_equal)
                ins.then_inc(hot2, 1)
                pool.sem_clear(picked)

            pool.wait_ge(table_out, 1)
            pool.wait_ge(used, V0)
            for q in range(2):
                hot_i2(q, q, True)
            with pool.Fori(1, T // 8) as i:
                for q in range(2):
                    hot_i2(i * 2 + q, q, False)

        @block.scalar
        def _(act):
            steps = [0]

            act.dma_start(at(MEM_AT, TB, D), mem[0].rearrange("(b p) d -> p b d", p=P)).then_inc(mem_in, 16)
            act.dma_start(ident[:, :], ident_d).then_inc(ident_in, 16)
            act.dma_start(at(X_AT, TB, D), x[0].rearrange("(b p) d -> p b d", p=P)).then_inc(x_in, 16)
            act.dma_start(at(GN_AT, D), gains[0:1, :].partition_broadcast(P)).then_inc(gain_in[0], 16)
            act.dma_start(at(QRT_AT, D), gains[1:2, :].partition_broadcast(P)).then_inc(gain_in[1], 16)

            def square_sum(src, col):
                nc.scalar.activation(SQ, src, ACT.Square, accum_out=stats[:, col:col + 1]).then_inc(squares, 1)
                steps[0] += 1
                act.wait_ge(squares, steps[0])

            def root(n, cols):
                act.wait_ge(var_ready, n)
                nc.scalar.activation(stats[:, 80:80 + cols], stats[:, 40:40 + cols], ACT.Sqrt).then_inc(root_ready, 1)

            def high(j, n0=0):
                act.wait_ge(raw_in[j % RAW], (n0 + (j // RAW * RAW + RAW)) * (16 // RAW))
                if not (isinstance(n0, int) and n0 + j < SPL):
                    act.wait_ge(used, n0 + (j - SPL + 1))
                nc.scalar.activation(whi[:, j % SPL, :], raw[:, j % RAW, :], ACT.Copy).then_inc(hi_done, 1)

            def transposed_high(k):
                for b in range(8):
                    act.wait_ge(xT_ready, 8 * k + b + 1)
                    nc.scalar.activation(xh[:, 2 * b:2 * b + 2, :],
                                         ps[:, b, :].rearrange("p (a b) -> p a b", a=2), ACT.Copy).then_inc(xh_ready, 1)

            act.wait_ge(mem_in, 16)
            for tb in range(TB):
                square_sum(at(MEM_AT, TB, D)[:, tb, :], tb)
            act.wait_ge(x_in, 16)
            for tb in range(TB):
                square_sum(at(X_AT, TB, D)[:, tb, :], 2 + tb)
            root(1, 4)
            act.wait_ge(angles, 1)
            nc.scalar.activation(CS, ANG[:, 0:2, :].rearrange("p a (b c) -> p a b c", b=TB), ACT.Sin).then_inc(sincos, 1)
            transposed_high(0)
            for j in range(W_XK, W_IN):
                high(j)
            act.wait_ge(used, W_IN)
            transposed_high(1)

            def exps(b):
                act.wait_ge(exp_in, b + 1)
                n, k = BATCH[b][3] - BATCH[b][2], BATCH[b][4]
                nc.scalar.activation(PR[:, 0:n * k], PR[:, 0:n * k], ACT.Exp)
                nc.scalar.activation(stats[:, 128:128 + n], stats[:, 144:144 + n], ACT.Exp).then_inc(exp_out, 1)

            def inner_rows(r):
                act.wait_ge(ret_o, r + 1)
                nc.scalar.activation(Y[:, :, 1024 + r * RD:1024 + (r + 1) * RD],
                                     ps[:, 6, :].rearrange("p (a b) -> p a b", a=TB), ACT.Copy).then_inc(ret_o_out, 1)

            for j in range(W_IN, W_OUT):
                high(j)
                for what, k in ACT_POINTS.get(j, ()):
                    (exps if what == "exp" else inner_rows)(k)
            for k in ACT_LAST:
                inner_rows(k)
            act.wait_ge(roped, 6)
            act.dma_start(at(GN_AT, D), out_gains.partition_broadcast(P)).then_inc(gain_in[5], 16)
            act.wait_ge(tile_out, 2 + len(IN_TILES))
            for tb in range(TB):
                nc.scalar.activation(H[:, tb, GR:GR + 1024], H[:, tb, GR:GR + 1024], ACT.Silu).then_inc(gate_ready, 1)
            root(2, 40)
            act.wait_ge(ret_cross, RH)
            act.dma_start(XR, x[0].rearrange("(b p) d -> p b d", p=P)).then_inc(xr_in, 16)
            act.wait_ge(y_ready, 1)
            act.dma_start(at(GN_AT, D), gains[2:3, :].partition_broadcast(P)).then_inc(gain_in[2], 16)
            act.dma_start(at(FG_AT, D), gains[3:4, :].partition_broadcast(P)).then_inc(gain_in[3], 16)
            transposed_high(2)
            for j in range(W_OUT, W_XQ):
                high(j)
            act.wait_ge(tile_out, 17)
            for tb in range(TB):
                square_sum(X1[:, tb, :], tb)
            act.dma_start(SK, sub_keys.rearrange("p (a b) -> p a b", a=HP)).then_inc(keys_in, 16)
            root(3, 2)
            transposed_high(3)
            for j in range(W_XQ, W_XO):
                high(j)
            act.wait_ge(x_max, 1)
            for h in range(XH):
                for tb in range(TB):
                    k = h * TB + tb
                    nc.scalar.activation(PX[:, k, :], ps[:, 4 + h, tb * T:(tb + 1) * T], ACT.Exp,
                                         bias=stats[:, 208 + k:209 + k], scale=XD ** -0.5,
                                         accum_out=stats[:, 216 + k:217 + k]).then_inc(x_exp, 1)
            act.wait_ge(x_oT, 1)
            nc.scalar.activation(xh[:, 0:XH, :], ps[:, 4:8, 0:T], ACT.Copy).then_inc(xh_ready, 1)
            for j in range(W_XO, W_PQ):
                high(j)
            act.wait_ge(tile_out, 22)
            for tb in range(TB):
                square_sum(X1[:, tb, :], tb)
            act.dma_start(x2_dram.rearrange("(b p) d -> p b d", p=P), X1).then_inc(x2_out, 16)
            root(4, 2)
            for b in range(8):
                act.wait_ge(xT_ready, 8 * 4 + b + 1)
                nc.scalar.activation(xh[:, 2 * b:2 * b + 2, :],
                                     ps[:, b, :].rearrange("p (a b) -> p a b", a=2), ACT.Copy).then_inc(xh_ready, 1)
            for j in range(W_PQ, U0):
                high(j)

            act.wait_ge(x2_out, 16)
            act.wait_ge(xl_ready, 34)

            def gelu(k0, c):
                nc.scalar.activation(W[:, k0 + c, :], ps[:, c % 2, 0:T], ACT.Gelu).then_inc(gelu_done, 1)

            for j in range(BODY):
                high(j, U0)
                if j % 2 == 0 and j >= 4:
                    gelu(0, j // 2 - 2)

            def body(i):
                for j in range(BODY):
                    high(j, i * BODY + U0)
                    if j % 2 == 0:
                        gelu(i * CHUNKS_PER_BODY - 2, j // 2)

            with act.Fori(1, PART1 // CHUNKS_PER_BODY) as i:
                body(i)
            act.wait_ge(top_ready, 1)
            GE = at(TK_AT, TB * PH, TOPK)
            nc.scalar.activation(GE, GE, ACT.Exp).then_inc(top_exp, 1)
            act.wait_ge(table_out, 1)
            with act.Fori(PART1 // CHUNKS_PER_BODY, NK // CHUNKS_PER_BODY) as i:
                body(i)
            tail = NK // CHUNKS_PER_BODY * CHUNKS_PER_BODY
            for j in range(2 * tail, 2 * NK):
                high(j, U0)
                if j % 2 == 0:
                    gelu(0, j // 2 - 2)
            for k in range(NK - 2, NK):
                act.wait_ge(used, U0 + 2 * k + 2)
                gelu(0, k)
            act.wait_ge(used, V0)
            act.dma_start(x2_back[:, :, :], x2_dram.rearrange("(b p) d -> p b d", p=P)).then_inc(x2_in, 16)

            def v_body(n0, k0, js):
                for j in js:
                    act.wait_ge(raw_in[j % RAW], (n0 + (j // RAW * RAW + RAW + V0 // RAW * RAW)) * (16 // RAW))
                    act.wait_ge(used, n0 + (V0 + j - SPL + 1))
                    nc.scalar.activation(whi[:, (V0 + j) % SPL, :], raw[:, j % RAW, :], ACT.Copy).then_inc(hi_done, 1)
                    if j % 2 == 0:
                        nc.scalar.activation(gate_hi[:, j // 2 % 2, :], W[:, k0 + j // 2, :], ACT.Copy).then_inc(ghi_done, 1)

            assert V0 % RAW == 0
            act.wait_ge(gated, T // 4)
            with act.Fori(0, 2 * NK // BODY) as i:
                v_body(i * BODY, i * CHUNKS_PER_BODY, range(BODY))
            v_body(0, 0, range(2 * NK // BODY * BODY, 2 * NK))
            act.wait_ge(glo_done, NK)
            act.wait_ge(gated, T // 4)
            act.dma_start(onehots[:, 0:D], gains[4:5, :].partition_broadcast(P)).then_inc(gain_in[4], 16)
            for tb in range(TB):
                act.wait_ge(x3_ready, tb + 1)
                nc.scalar.activation(at(0, TB, D)[:, tb, :], x2_back[:, tb, :], ACT.Square,
                                     accum_out=stats[:, tb:tb + 1]).then_inc(squares, 1)
            root(5, 2)

        @block.vector
        def _(dve):
            n = [0]

            def step(ins):
                n[0] += 1
                ins.then_inc(dve_step, 1)
                dve.wait_ge(dve_step, n[0])

            def inverse_root(k, cols, eps):
                v, r, t = stats[:, 40:40 + cols], stats[:, 160:160 + cols], stats[:, 80:80 + cols]
                dve.wait_ge(root_ready, k)
                step(nc.vector.reciprocal(r, t))
                step(nc.vector.tensor_tensor(t, r, r, ALU.mult))
                step(nc.vector.tensor_tensor(t, t, v, ALU.mult))
                step(nc.vector.tensor_scalar(t, t, -0.5, 1.5, ALU.mult, ALU.add))
                step(nc.vector.tensor_tensor(r, r, t, ALU.mult))

            def variances(cols, squares_done):
                dve.wait_ge(squares, squares_done)
                nc.vector.tensor_scalar(stats[:, 40:40 + cols], stats[:, 0:cols], 1.0 / D, EPS,
                                        ALU.mult, ALU.add).then_inc(var_ready, 1)

            def norm_rows(src, gain, col):
                for tb in range(TB):
                    nc.vector.scalar_tensor_tensor(Y[:, tb, :], src[:, tb, :], stats[:, 160 + col + tb:161 + col + tb],
                                                   gain, ALU.mult, ALU.mult).then_inc(normed, 1)

            def transposed_low(first_count):
                for b in range(8):
                    dve.wait_ge(xh_ready, first_count + b + 1)
                    nc.vector.tensor_tensor(xl[:, 2 * b:2 * b + 2, :],
                                            ps[:, b, :].rearrange("p (a b) -> p a b", a=2),
                                            xh[:, 2 * b:2 * b + 2, :], ALU.subtract).then_inc(xl_ready, 1)

            variances(4, 4)
            dve.wait_ge(const_in, 7 * 16)
            TF = at(MEM_AT + 8192 + 1920, 2, TB * 160)
            step(nc.vector.tensor_copy(POSF, POSI))
            for tb in range(TB):
                step(nc.vector.tensor_scalar(ANG[:, 2, tb * 160:(tb + 1) * 160], INV, POSF[:, tb:tb + 1], None, ALU.mult))
            for k, shift in ((0, 0.0), (1, 0.25)):
                step(nc.vector.tensor_scalar(TF[:, k, :], ANG[:, 2, :], 0.15915494309189535, shift, ALU.mult, ALU.add))
                step(nc.vector.tensor_copy(TURN[:, k, :], TF[:, k, :]))
                step(nc.vector.tensor_copy(TF[:, k, :], TURN[:, k, :]))
                step(nc.vector.scalar_tensor_tensor(ANG[:, k, :], TF[:, k, :], -C1, ANG[:, 2, :], ALU.mult, ALU.add))
                step(nc.vector.scalar_tensor_tensor(ANG[:, k, :], TF[:, k, :], -C2, ANG[:, k, :], ALU.mult, ALU.add))
                step(nc.vector.scalar_tensor_tensor(ANG[:, k, :], TF[:, k, :], -C3, ANG[:, k, :], ALU.mult, ALU.add))
                if k:
                    step(nc.vector.tensor_scalar(ANG[:, k, :], ANG[:, k, :], PI / 2, None, ALU.add))
            nc.vector.tensor_scalar(ANG[:, 0:2, :], ANG[:, 0:2, :], PI, -PI, ALU.min, ALU.max).then_inc(angles, 1)
            inverse_root(1, 4, EPS)
            dve.wait_ge(gain_in[0], 16)
            norm_rows(at(MEM_AT, TB, D), at(GN_AT, D), 0)
            transposed_low(0)
            dve.wait_ge(gain_in[1], 16)
            dve.wait_ge(xT_ready, 8)
            norm_rows(at(X_AT, TB, D), at(QRT_AT, D), 2)
            dve.wait_ge(used, 8)
            nc.vector.tensor_copy(KX, ps[:, 0:4, 0:T]).then_inc(tile_out, 1)
            dve.wait_ge(used, 16)
            nc.vector.tensor_copy(VX, ps[:, 4:6, :]).then_inc(tile_out, 1)
            transposed_low(8)

            def in_tile(t):
                c0, w = IN_TILES[t]
                dve.wait_ge(used, TILE_END[t])
                b = 2 * (t % 2)
                nc.vector.tensor_copy(H[:, :, c0:c0 + w], ps[:, b:b + 2, 0:w]).then_inc(tile_out, 1)
                dve.wait_ge(tile_out, 3 + t)

            ropes = [0]

            def rope(tb, c0, heads, half, tab):
                v = H[:, tb, c0:c0 + heads * 2 * half].rearrange("p (n two f) -> p n two f", two=2, f=half)
                x1, x2 = v[:, :, 0, :], v[:, :, 1, :]
                m = heads * half
                t = [at(GN_AT + 576 * k, heads, half) if m > 512 else at(GN_AT + 512 * k, heads, half) for k in range(3)]
                sin, cos = (CS[:, k, tb, tab:tab + half].unsqueeze(1).broadcast_to([P, heads, half]) for k in range(2))
                nc.vector.tensor_tensor(t[0], x1, cos, ALU.mult)
                nc.vector.tensor_tensor(t[1], x2, sin, ALU.mult)
                step(nc.vector.tensor_tensor(t[2], x1, sin, ALU.mult))
                step(nc.vector.tensor_tensor(x1, t[0], t[1], ALU.subtract))
                step(nc.vector.tensor_tensor(t[0], x2, cos, ALU.mult))
                nc.vector.tensor_tensor(x2, t[0], t[2], ALU.add).then_inc(roped, 1)
                ropes[0] += 1
                dve.wait_ge(roped, ropes[0])

            def rope_a(_):
                dve.wait_ge(sincos, 1)
                for tb in range(TB):
                    rope(tb, QA, QH + KVH, HD // 2, 0)
                for tb in range(TB):
                    for g in range(KVH):
                        src = H[:, tb, KA + g * HD:KA + (g + 1) * HD].unsqueeze(1).broadcast_to([P, 2, HD])
                        nc.vector.tensor_copy(at(P_AT + (tb * KVH + g) * P, 2, HD), src).then_inc(roped_a, 1)

            def qk_copies(g):
                dve.wait_ge(qk_T, g + 1)
                b = 4 if g == 0 else 6
                if g == 0:
                    nc.vector.tensor_copy(KT, ps[:, 6, :].rearrange("p (a b) -> p a b", a=2))
                nc.vector.tensor_copy(QAT[:, 4 * g:4 * g + 4, :],
                                      ps[:, b:b + 2, :].rearrange("p a (b c) -> p (a b) c", b=2)).then_inc(qk_copied, 1)

            def softmax_in(b):
                g, tb, h0, h1, w = BATCH[b]
                m = h1 - h0
                pr = PR[:, 0:m * w].rearrange("p (a b) -> p a b", a=m)
                src = ps[:, 4:6, :].rearrange("p a b -> p (a b)")[:, 0:m * w].rearrange("p (a b) -> p a b", a=m)
                mask = MASK.rearrange("p a b -> p (a b)")[:, 2 * P - w:2 * P].unsqueeze(1).broadcast_to([P, m, w])
                dve.wait_ge(scores, b + 1)
                if b:
                    dve.wait_ge(p_T, b)
                nc.vector.scalar_tensor_tensor(pr, src, HD ** -0.5, mask, ALU.mult, ALU.add).then_inc(scores_read, 1)
                dve.wait_ge(scores_read, b + 1)
                mx = stats[:, 120:120 + m]
                step(nc.vector.reduce_max(mx, pr, AX))
                mx2 = mx.rearrange("p (b a) -> p b a", b=2)
                sink = SINK[:, h0:h1].rearrange("p (a b) -> p b a", b=2)
                step(nc.vector.tensor_tensor(mx2, mx2, sink, ALU.max))
                nc.vector.tensor_tensor(stats[:, 144:144 + m].rearrange("p (b a) -> p b a", b=2), sink, mx2, ALU.subtract)
                nc.vector.tensor_tensor(pr, pr, mx.unsqueeze(2).broadcast_to([P, m, w]), ALU.subtract).then_inc(exp_in, 1)

            def softmax_sum(b):
                g, tb, h0, h1, w = BATCH[b]
                m = h1 - h0
                dve.wait_ge(exp_out, b + 1)
                pr = PR[:, 0:m * w].rearrange("p (a b) -> p a b", a=m)
                r = stats[:, 200 + 8 * (b % 2):200 + 8 * (b % 2) + m]
                step(nc.vector.reduce_sum(r, pr, AX))
                step(nc.vector.tensor_tensor(r, r, stats[:, 128:128 + m], ALU.add))
                step(nc.vector.reciprocal(r, r))

            def o_rows(b):
                g, tb, h0, h1, w = BATCH[b]
                m = h1 - h0
                dve.wait_ge(o_ready, b + 1)
                r = stats[:, 200 + 8 * (b % 2):200 + 8 * (b % 2) + m]
                nc.vector.tensor_tensor(Y[:, tb, h0 * HD:h1 * HD].rearrange("p (a b d) -> p a b d", b=2, d=HD),
                                        ps[:, 6, 0:m * HD].rearrange("p (a b d) -> p a b d", b=2, d=HD),
                                        r.rearrange("p (b a) -> p a b", b=2).unsqueeze(3).broadcast_to([P, m // 2, 2, HD]),
                                        ALU.mult).then_inc(o_out, 1)

            def p_copies(b):
                dve.wait_ge(p_T, b + 1)
                nc.vector.tensor_copy(PT, ps[:, 6:8, :].rearrange("p a (b c) -> p (a b) c", b=4)).then_inc(p_copied, 1)

            def rope_r(c0):
                for tb in range(TB):
                    rope(tb, c0, RH, RD // 2, 32)

            def r_copies(r):
                dve.wait_ge(r_T, r + 1)
                nc.vector.tensor_copy(QRT[:, r], ps[:, 4, :].rearrange("p (a b) -> p a b", a=2))
                nc.vector.tensor_copy(KRT[:, r % 2], ps[:, 5, :].rearrange("p (a b) -> p a b", a=2)).then_inc(r_copied, 1)

            def inner_decay(r):
                dve.wait_ge(inner, r + 1)
                nc.vector.tensor_tensor(IT[:, r], ps[:, 6, 0:T].rearrange("p (a b) -> p a b", a=TB),
                                        DEC[:, r, :].unsqueeze(1).broadcast_to([P, TB, P]), ALU.mult).then_inc(inner_out, 1)

            def kz_rows(r):
                if r >= 2:
                    dve.wait_ge(state, r - 1)
                nc.vector.tensor_scalar(KZ[:, r % 2, :], H[:, 0, KR + r * RD:KR + (r + 1) * RD], ZX[:, 0, r:r + 1],
                                        None, ALU.mult).then_inc(kz_ready, 1)

            def state_copy(r):
                dve.wait_ge(state, r + 1)
                nc.vector.tensor_copy(ST[:, r % 2], ps[:, 7, :].rearrange("p (a b) -> p a b", a=2)).then_inc(state_out, 1)

            def cross_rows(r):
                dve.wait_ge(ret_o_out, r + 1)
                y = Y[:, 1, 1024 + r * RD:1024 + (r + 1) * RD]
                nc.vector.scalar_tensor_tensor(y, ps[:, 7, 0:RD], ZX[:, 1, r:r + 1], y, ALU.mult, ALU.add).then_inc(ret_cross, 1)

            do = {"tile": in_tile, "rope_a": rope_a, "qk": qk_copies, "sin": softmax_in, "ssum": softmax_sum,
                  "o": o_rows, "pt": p_copies, "rope_r": rope_r, "rc": r_copies, "dec": inner_decay, "kz": kz_rows,
                  "st": state_copy, "cross": cross_rows}
            for what, k in DVE_ORDER:
                do[what](k)

            dve.wait_ge(ret_cross, RH)
            dve.wait_ge(o_out, len(BATCH))
            SQA = at(P_AT, 2, 1024)
            ms = stats[:, 0:32].rearrange("p (a b) -> p a b", a=TB)
            step(nc.vector.tensor_tensor(SQA, Y[:, :, 0:1024], Y[:, :, 0:1024], ALU.mult))
            for tb in range(TB):
                step(nc.vector.reduce_sum(ms[:, tb, :], SQA[:, tb, :].rearrange("p (a b) -> p a b", a=QH), AX))
            step(nc.vector.tensor_scalar(stats[:, 40:72], stats[:, 0:32], 1.0 / HD, EPS, ALU.mult, ALU.add))
            BN = at(QAT_AT, TB * RH, 6)
            MV = at(QAT_AT + 64, TB * RH, 2)
            for tb in range(TB):
                for r in range(RH):
                    step(nc.vector.bn_stats(BN[:, tb * RH + r, :], Y[:, tb, 1024 + r * RD:1024 + (r + 1) * RD]))
                    step(nc.vector.bn_aggr(MV[:, tb * RH + r, :], BN[:, tb * RH + r, :]))
            nc.vector.tensor_scalar(stats[:, 72:80], MV[:, :, 1], GN_EPS, None, ALU.add).then_inc(var_ready, 1)
            inverse_root(2, 40, EPS)
            for tb in range(TB):
                ya = Y[:, tb, 0:1024].rearrange("p (a b) -> p a b", a=QH)
                nc.vector.tensor_tensor(ya, ya, stats[:, 160 + 16 * tb:176 + 16 * tb].unsqueeze(2).broadcast_to([P, QH, HD]), ALU.mult)
                for r in range(RH):
                    yr = Y[:, tb, 1024 + r * RD:1024 + (r + 1) * RD]
                    k = tb * RH + r
                    ins = nc.vector.tensor_scalar(yr, yr, MV[:, k, 0:1], stats[:, 192 + k:193 + k], ALU.subtract, ALU.mult)
                step(ins)
            dve.wait_ge(gain_in[5], 16)
            step(nc.vector.tensor_tensor(Y, Y, at(GN_AT, D).unsqueeze(1).broadcast_to([P, TB, D]), ALU.mult))
            dve.wait_ge(gate_ready, 2)
            nc.vector.tensor_tensor(Y[:, :, 1024:D], Y[:, :, 1024:D], H[:, :, GR:GR + 1024], ALU.mult).then_inc(y_ready, 1)
            transposed_low(16)

            dve.wait_ge(xr_in, 16)
            for t in range(4):
                dve.wait_ge(used, W_OUT + 8 * t + 8)
                b = 2 * (t % 2)
                ins = nc.vector.tensor_tensor(X1[:, :, 512 * t:512 * t + 512], ps[:, b:b + 2, :],
                                              XR[:, :, 512 * t:512 * t + 512], ALU.add).then_inc(tile_out, 1)
            variances(2, 6)
            inverse_root(3, 2, EPS)
            dve.wait_ge(gain_in[2], 16)
            dve.wait_ge(xT_ready, 24)
            norm_rows(X1, at(GN_AT, D), 0)
            transposed_low(24)

            dve.wait_ge(used, W_XO)
            nc.vector.tensor_copy(QXT, ps[:, 0:4, 0:T]).then_inc(tile_out, 1)
            dve.wait_ge(x_scores, 1)
            sc = ps[:, 4:8, :].rearrange("p a (b c) -> p (a b) c", b=TB)
            step(nc.vector.reduce_max(stats[:, 224:232], sc, AX))
            nc.vector.tensor_scalar(stats[:, 208:216], stats[:, 224:232], -XD ** -0.5, None, ALU.mult).then_inc(x_max, 1)
            dve.wait_ge(x_exp, 8)
            step(nc.vector.reciprocal(stats[:, 232:240], stats[:, 216:224]))
            nc.vector.tensor_tensor(PX, PX, stats[:, 232:240].unsqueeze(2).broadcast_to([P, 8, T]), ALU.mult).then_inc(x_prob, 1)
            dve.wait_ge(x_pT, 1)
            nc.vector.tensor_copy(PXT, ps[:, 0:4, :].rearrange("p a (b c) -> p a b c", b=TB)).then_inc(x_pT_out, 1)
            dve.wait_ge(xh_ready, 33)
            nc.vector.tensor_tensor(xl[:, 0:XH, :], ps[:, 4:8, 0:T], xh[:, 0:XH, :], ALU.subtract).then_inc(xl_ready, 1)
            for t in range(4):
                dve.wait_ge(used, W_XO + 2 * t + 2)
                b = 2 * (t % 2)
                dst = X1[:, :, 512 * t:512 * t + 512]
                nc.vector.tensor_tensor(dst, ps[:, b:b + 2, :], dst, ALU.add).then_inc(tile_out, 1)

            variances(2, 8)
            inverse_root(4, 2, EPS)
            dve.wait_ge(gain_in[3], 16)
            norm_rows(X1, at(FG_AT, D), 0)
            transposed_low(33)
            for t in range(4):
                dve.wait_ge(used, W_PQ + 8 * t + 8)
                b = 4 * (t % 2)
                nc.vector.tensor_copy(QPT[:, 4 * t:4 * t + 4, :], ps[:, b:b + 4, 0:T]).then_inc(tile_out, 1)
            for tb in range(TB):
                dve.wait_ge(key_scores, tb + 1)
                nc.vector.tensor_copy(S[:, tb * PH:(tb + 1) * PH, :],
                                      ps[:, 4 * tb:4 * tb + 4, :].rearrange("p a (b c) -> p (a b) c", b=2)).then_inc(key_scores_out, 1)
            dve.wait_ge(key_scores_out, 2)

            o = TK_AT
            def small(*dims):
                nonlocal o
                v = at(o, *dims)
                m = 1
                for d in dims:
                    m *= d
                o += m
                return v
            GE = small(TB * PH, TOPK)
            CH = small(2, TB * PH * TOPK)
            cur, cur2, v, ixf = small(2, NK), small(2, NK), small(2, TOPK), small(2, TOPK)
            ix = small(2, TOPK).bitcast(U32)
            cand, cand2, top = small(TOPK * TOPK), small(TOPK * TOPK), small(TOPK)
            where = small(TOPK).bitcast(U32)
            ab, abf = small(2, TOPK).bitcast(U32), small(2, TOPK)
            oh = small(2, TOPK, TOPK)
            assert o <= BIG
            LOW = -3.0e38
            with dve.Fori(0, TB * PH) as r:
                k = [0]

                def tick(ins):
                    k[0] += 1
                    ins.then_inc(topk, 1)
                    dve.wait_ge(topk, k[0])

                tick(nc.vector.tensor_copy(cur, S[:, bass.ds(r, 1), :].rearrange("p a (b c) -> p (a b) c", b=2)))
                for c, half in ((cur, 0), (cur2, 8)):
                    for p in range(2):
                        ins = nc.vector.max(v[:, p, half:half + 8], c[:, p, :])
                    tick(ins)
                    for p in range(2):
                        ins = nc.vector.max_index(ix[:, p, half:half + 8], v[:, p, half:half + 8], c[:, p, :])
                    if half == 0:
                        for p in range(2):
                            ins = nc.vector.match_replace(cur2[:, p, :], v[:, p, 0:8], cur[:, p, :], LOW)
                    tick(ins)
                tick(nc.vector.tensor_copy(ixf, ix))
                tick(nc.vector.tensor_tensor(cand.rearrange("p (a b) -> p a b", a=TOPK),
                                             v[:, 0, :].unsqueeze(2).broadcast_to([P, TOPK, TOPK]),
                                             v[:, 1, :].unsqueeze(1).broadcast_to([P, TOPK, TOPK]), ALU.add))
                tick(nc.vector.max(top[:, 0:8], cand))
                tick(nc.vector.max_index(where[:, 0:8], top[:, 0:8], cand))
                tick(nc.vector.match_replace(cand2, top[:, 0:8], cand, LOW))
                tick(nc.vector.max(top[:, 8:16], cand2))
                tick(nc.vector.max_index(where[:, 8:16], top[:, 8:16], cand2))
                tick(nc.vector.tensor_copy(GE[:, bass.ds(r, 1), :], top.unsqueeze(1)))
                tick(nc.vector.tensor_scalar(ab[:, 0, :], where, 4, None, ALU.logical_shift_right))
                tick(nc.vector.tensor_scalar(ab[:, 1, :], where, 15, None, ALU.bitwise_and))
                tick(nc.vector.tensor_copy(abf, ab))
                tick(nc.vector.tensor_tensor(oh, iota[:, 0:TOPK].unsqueeze(1).unsqueeze(1).broadcast_to([P, 2, TOPK, TOPK]),
                                             abf.unsqueeze(3).broadcast_to([P, 2, TOPK, TOPK]), ALU.is_equal))
                tick(nc.vector.tensor_tensor(oh, oh, ixf.unsqueeze(2).broadcast_to([P, 2, TOPK, TOPK]), ALU.mult))
                tick(nc.vector.reduce_sum(CH[:, :, bass.ds(r * TOPK, TOPK)], oh, AX))
                dve.sem_clear(topk)
            top1 = stats[:, 0:16]
            step(nc.vector.tensor_copy(top1.unsqueeze(2), GE[:, :, 0:1]))
            nc.vector.tensor_tensor(GE, GE, top1.unsqueeze(2).broadcast_to([P, 16, TOPK]), ALU.subtract).then_inc(top_ready, 1)
            dve.wait_ge(top_exp, 1)
            step(nc.vector.reduce_sum(top1, GE, AX))
            step(nc.vector.reciprocal(top1, top1))
            nc.vector.tensor_tensor(GE, GE, top1.unsqueeze(2).broadcast_to([P, 16, TOPK]), ALU.mult).then_inc(gates_ready, 1)
            dve.wait_ge(table_T, 1)
            nc.vector.tensor_copy(table[:, 0:2, :], ps[:, 4, :].rearrange("p (a b) -> p a b", a=2))
            nc.vector.tensor_copy(table[:, 2, :], ps[:, 5, 0:T]).then_inc(table_out, 1)
            dve.wait_ge(table_out, 1)

            def hot_i1(g, q, first_use):
                if not first_use:
                    dve.wait_ge(gate_mat, g - 1)
                for m in range(4):
                    ins = nc.vector.tensor_scalar(hot_a(q)[:, m, :], iota[:, :], table[:, 0, bass.ds(g * 4 + m, 1)],
                                                  table[:, 2, bass.ds(g * 4 + m, 1)], ALU.is_equal, ALU.mult)
                ins.then_inc(hot1, 1)

            def apply_gates(g, q):
                dve.wait_ge(gate_mat, g + 1)
                w = W[:, :, bass.ds(g * 4, 4)]
                nc.vector.tensor_tensor(w, ps[:, 2 + q, :].rearrange("p (m k) -> p k m", m=4), w, ALU.mult).then_inc(gated, 1)

            dve.wait_ge(used, V0)
            hot_i1(0, 0, True)
            hot_i1(1, 1, True)
            dve.wait_ge(gelu_done, NK)
            apply_gates(0, 0)
            with dve.Fori(0, T // 8 - 1) as i:
                hot_i1(i * 2 + 2, 0, False)
                apply_gates(i * 2 + 1, 1)
                hot_i1(i * 2 + 3, 1, False)
                apply_gates(i * 2 + 2, 0)
            apply_gates(T // 4 - 1, 1)

            def v_body(n0, k0, js):
                for j in js:
                    dve.wait_ge(hi_done, n0 + (V0 + j + 1))
                    s = (V0 + j) % SPL
                    nc.vector.tensor_tensor(wlo[:, s, :], raw[:, j % RAW, :], whi[:, s, :], ALU.subtract).then_inc(lo_done, 1)
                    if j % 2 == 0:
                        dve.wait_ge(ghi_done, k0 + (j // 2 + 1))
                        nc.vector.tensor_tensor(gate_lo[:, j // 2 % 2, :], W[:, k0 + j // 2, :],
                                                gate_hi[:, j // 2 % 2, :], ALU.subtract).then_inc(glo_done, 1)

            with dve.Fori(0, 2 * NK // BODY) as i:
                v_body(i * BODY, i * CHUNKS_PER_BODY, range(BODY))
            v_body(0, 0, range(2 * NK // BODY * BODY, 2 * NK))

            dve.wait_ge(x2_in, 16)
            dve.wait_ge(used, END)
            for tb in range(TB):
                nc.vector.tensor_tensor(x2_back[:, tb, :], ps[:, 4 * tb:4 * tb + 4, :].rearrange("p a b -> p (a b)"),
                                        x2_back[:, tb, :], ALU.add).then_inc(x3_ready, 1)
            variances(2, 10)
            inverse_root(5, 2, EPS)
            dve.wait_ge(gain_in[4], 16)
            for tb in range(TB):
                nc.vector.scalar_tensor_tensor(x2_back[:, tb, :], x2_back[:, tb, :], stats[:, 160 + tb:161 + tb],
                                               onehots[:, 0:D], ALU.mult, ALU.mult).then_inc(y_out, 1)

        @block.tensor
        def _(pe):
            def transposes(k):
                pe.wait_ge(normed if k != 2 else y_ready, {0: 2, 1: 4, 2: 1, 3: 6, 4: 8}[k])
                for b in range(8):
                    for c in range(2):
                        for tb in range(TB):
                            m = 2 * b + c
                            ins = nc.tensor.transpose(ps[:, b, (c * TB + tb) * P:(c * TB + tb + 1) * P],
                                                      Y[:, tb, m * P:(m + 1) * P], ident[:, :])
                    ins.then_inc(xT_ready, 1)

            def three(out_ap, sh, sl, mh, ml, start, stop):
                nc.tensor.matmul(out_ap, sh, mh, start=start, stop=False)
                nc.tensor.matmul(out_ap, sh, ml, start=False, stop=False)
                return nc.tensor.matmul(out_ap, sl, mh, start=False, stop=stop)

            def rows_piece(n, c0, width, last_chunk, banks):
                pe.wait_ge(lo_done, n + 1)
                s = n % SPL
                for tb in range(TB):
                    for c in range(PW // width):
                        m = c0 + c
                        t = slice(tb * P, (tb + 1) * P)
                        cols = slice(c * width, (c + 1) * width)
                        ins = three(ps[:, banks + tb, 0:width], xh[:, m, t], xl[:, m, t], whi[:, s, cols], wlo[:, s, cols],
                                    m == 0, m == last_chunk)
                ins.then_inc(used, 1)

            def cols_piece(n, c0, last_chunk, banks):
                pe.wait_ge(lo_done, n + 1)
                s = n % SPL
                for c in range(2):
                    for b in range(4):
                        m = c0 + c
                        cols = slice(c * 512 + b * P, c * 512 + (b + 1) * P)
                        ins = three(ps[:, banks + b, 0:T], whi[:, s, cols], wlo[:, s, cols], xh[:, m, :], xl[:, m, :],
                                    m == 0, m == last_chunk)
                ins.then_inc(used, 1)

            pe.wait_ge(ident_in, 16)
            transposes(0)
            pe.wait_ge(xl_ready, 8)
            for n in range(W_XK, W_XV):
                cols_piece(n, 2 * (n - W_XK), DC - 1, 0)
            for n in range(W_XV, W_IN):
                rows_piece(n, 2 * (n - W_XV), 512, DC - 1, 4)
            pe.wait_ge(tile_out, 2)
            transposes(1)
            pe.wait_ge(xl_ready, 16)

            def qk_transposes(g):
                if g == 0:
                    pe.wait_ge(roped_a, 4)
                    for k in range(KVH):
                        for tb in range(TB):
                            nc.tensor.transpose(ps[:, 6, (k * TB + tb) * P:(k * TB + tb + 1) * P],
                                                at(P_AT + (tb * KVH + k) * P, P), ident[:, :])
                else:
                    pe.wait_ge(qk_copied, 1)
                for c in range(4):
                    for tb in range(TB):
                        m = c * TB + tb
                        ins = nc.tensor.transpose(ps[:, (4 if g == 0 else 6) + m // 4, (m % 4) * P:(m % 4 + 1) * P],
                                                  H[:, tb, (4 * g + c) * P:(4 * g + c + 1) * P], ident[:, :])
                ins.then_inc(qk_T, 1)

            def head_scores(b):
                g, tb, h0, h1, w = BATCH[b]
                pe.wait_ge(qk_copied, 1 + g)
                if b:
                    pe.wait_ge(scores_read, b)
                for h in range(h0, h1):
                    lo = h % 2 * HD
                    col = (h - h0) // 2 * w
                    ins = nc.tensor.matmul(ps[:, 4 + h % 2, col:col + w],
                                           QAT[lo:lo + HD, h // 2, tb * P:(tb + 1) * P],
                                           KT[lo:lo + HD, g, 0:w], start=True, stop=True)
                ins.then_inc(scores, 1)

            def p_transposes(b):
                g, tb, h0, h1, w = BATCH[b]
                pe.wait_ge(exp_out, b + 1)
                pe.wait_ge(qk_copied, 2)
                if b:
                    pe.wait_ge(o_out, b)
                for m in range(8):
                    ins = nc.tensor.transpose(ps[:, 6 + m // 4, (m % 4) * P:(m % 4 + 1) * P], PR[:, m * P:(m + 1) * P],
                                              ident[:, :])
                ins.then_inc(p_T, 1)

            def head_outputs(b):
                g, tb, h0, h1, w = BATCH[b]
                pe.wait_ge(p_copied, b + 1)
                nk = w // P
                for k in range(h1 - h0):
                    for kc in range(nk):
                        q = k % 2 * ((h1 - h0) // 2) + k // 2
                        ins = nc.tensor.matmul(ps[:, 6, k * HD:(k + 1) * HD], PT[:, q * nk + kc, :],
                                               H[:, kc, VA + g * HD:VA + (g + 1) * HD], start=kc == 0, stop=kc == nk - 1)
                ins.then_inc(o_ready, 1)

            def r_transposes(r):
                pe.wait_ge(roped, 6)
                if r == 0:
                    pe.wait_ge(scores_read, len(BATCH))
                else:
                    pe.wait_ge(r_copied, r)
                for k, c0 in ((0, QR), (1, KR)):
                    for dc in range(2):
                        for tb in range(TB):
                            ins = nc.tensor.transpose(ps[:, 4 + k, (dc * TB + tb) * P:(dc * TB + tb + 1) * P],
                                                      H[:, tb, c0 + r * RD + dc * P:c0 + r * RD + (dc + 1) * P], ident[:, :])
                ins.then_inc(r_T, 1)

            def r_inner(r):
                pe.wait_ge(r_copied, r + 1)
                if r == 0:
                    pe.wait_ge(o_out, len(BATCH))
                else:
                    pe.wait_ge(ret_o_out, r)
                for tb in range(TB):
                    for dc in range(2):
                        ins = nc.tensor.matmul(ps[:, 6, tb * P:(tb + 1) * P], KRT[:, r % 2, dc, tb * P:(tb + 1) * P],
                                               QRT[:, r, dc, tb * P:(tb + 1) * P], start=dc == 0, stop=dc == 1)
                ins.then_inc(inner, 1)

            def r_state(r):
                pe.wait_ge(kz_ready, r + 1)
                pe.wait_ge(tile_out, 2 + 9)
                if r:
                    pe.wait_ge(ret_cross, r)
                for dc in range(2):
                    ins = nc.tensor.matmul(ps[:, 7, dc * RD:(dc + 1) * RD], KZ[:, r % 2, dc * P:(dc + 1) * P],
                                           H[:, 0, VR + r * RD:VR + (r + 1) * RD], start=True, stop=True)
                ins.then_inc(state, 1)

            def r_out(r):
                pe.wait_ge(inner_out, r + 1)
                pe.wait_ge(state_out, r + 1)
                for tb in range(TB):
                    nc.tensor.matmul(ps[:, 6, tb * RD:(tb + 1) * RD], IT[:, r, tb, :], H[:, tb, VR + r * RD:VR + (r + 1) * RD],
                                     start=True, stop=True)
                for dc in range(2):
                    ins = nc.tensor.matmul(ps[:, 7, 0:RD], QRT[:, r, dc, P:T], ST[:, r % 2, dc, :], start=dc == 0, stop=dc == 1)
                ins.then_inc(ret_o, 1)

            do = {"qk": qk_transposes, "s": head_scores, "pt": p_transposes, "o": head_outputs, "rt": r_transposes,
                  "ri": r_inner, "rs": r_state, "ro": r_out}
            n = W_IN
            for t, (c0, w) in enumerate(IN_TILES):
                if t >= 2:
                    pe.wait_ge(tile_out, 2 + t - 1)
                per = PW // w
                for j in range(DC // per):
                    rows_piece(n, j * per, w, DC - 1, 2 * (t % 2))
                    for what, k in PE_POINTS.get(n, ()):
                        do[what](k)
                    n += 1
            assert n == W_OUT
            for what, k in PE_LAST:
                do[what](k)
            pe.wait_ge(ret_cross, RH)
            transposes(2)
            pe.wait_ge(xl_ready, 24)
            for t in range(4):
                if t >= 2:
                    pe.wait_ge(tile_out, 13 + t - 1)
                for j in range(8):
                    rows_piece(W_OUT + 8 * t + j, 2 * j, 512, DC - 1, 2 * (t % 2))
            pe.wait_ge(tile_out, 17)
            transposes(3)
            pe.wait_ge(xl_ready, 32)
            for j in range(8):
                cols_piece(W_XQ + j, 2 * j, DC - 1, 0)
            pe.wait_ge(tile_out, 18)
            for h in range(XH):
                for tb in range(TB):
                    ins = nc.tensor.matmul(ps[:, 4 + h, tb * T:(tb + 1) * T], QXT[:, h, tb * P:(tb + 1) * P], KX[:, h, :],
                                           start=True, stop=True)
            ins.then_inc(x_scores, 1)
            pe.wait_ge(x_prob, 1)
            for h in range(XH):
                for mb in range(TB):
                    for tb in range(TB):
                        ins = nc.tensor.transpose(ps[:, h, mb * T + tb * P:mb * T + (tb + 1) * P],
                                                  PX[:, h * TB + tb, mb * P:(mb + 1) * P], ident[:, :])
            ins.then_inc(x_pT, 1)
            pe.wait_ge(x_pT_out, 1)
            for h in range(XH):
                for mb in range(TB):
                    ins = nc.tensor.matmul(ps[:, 4 + h, 0:T], VX[:, mb, h * XD:(h + 1) * XD], PXT[:, h, mb, :],
                                           start=mb == 0, stop=mb == 1)
            ins.then_inc(x_oT, 1)
            pe.wait_ge(xl_ready, 33)
            for t in range(4):
                if t >= 2:
                    pe.wait_ge(tile_out, 18 + t - 1)
                for j in range(2):
                    rows_piece(W_XO + 2 * t + j, 2 * j, 512, XH - 1, 2 * (t % 2))
            pe.wait_ge(tile_out, 22)
            transposes(4)
            pe.wait_ge(xl_ready, 41)
            for t in range(4):
                if t >= 2:
                    pe.wait_ge(tile_out, 22 + t - 1)
                for j in range(8):
                    cols_piece(W_PQ + 8 * t + j, 2 * j, DC - 1, 4 * (t % 2))
            pe.wait_ge(tile_out, 26)
            pe.wait_ge(keys_in, 16)
            for tb in range(TB):
                for hp in range(HP):
                    ins = nc.tensor.matmul(ps[:, 4 * tb + hp // 4, hp % 4 * NK:(hp % 4 + 1) * NK],
                                           QPT[:, hp, tb * P:(tb + 1) * P], SK[:, hp, :], start=True, stop=True)
                ins.then_inc(key_scores, 1)

            def u_piece(n0, j):
                pe.wait_ge(lo_done, n0 + (j + 1))
                s = j % SPL
                for c in range(8):
                    m = j % 2 * 8 + c
                    cols = slice(c * P, (c + 1) * P)
                    ins = three(ps[:, j // 2 % 2, 0:T], whi[:, s, cols], wlo[:, s, cols], xh[:, m, :], xl[:, m, :],
                                m == 0, m == DC - 1)
                ins.then_inc(used, 1)

            def u_body(i):
                for j in range(BODY):
                    if j % 2 == 0:
                        pe.wait_ge(gelu_done, i * CHUNKS_PER_BODY + (j // 2 - 1))
                    u_piece(i * BODY + U0, j)

            pe.wait_ge(key_scores_out, 2)
            for j in range(BODY):
                if j % 2 == 0 and j >= 4:
                    pe.wait_ge(gelu_done, j // 2 - 1)
                u_piece(U0, j)
            with pe.Fori(1, PART1 // CHUNKS_PER_BODY) as i:
                u_body(i)
            pe.wait_ge(gates_ready, 1)
            CH = at(TK_AT + 256, 2, T)
            GE = at(TK_AT, T)
            for k in range(3):
                for tb in range(TB):
                    src = (CH[:, k, :] if k < 2 else GE)[:, tb * P:(tb + 1) * P]
                    ins = nc.tensor.transpose(ps[:, 4 + k // 2, (k % 2 * TB + tb) * P:(k % 2 * TB + tb + 1) * P], src, ident[:, :])
            ins.then_inc(table_T, 1)
            with pe.Fori(PART1 // CHUNKS_PER_BODY, NK // CHUNKS_PER_BODY) as i:
                u_body(i)
            for j in range(NK // CHUNKS_PER_BODY * BODY, 2 * NK):
                if j % 2 == 0:
                    pe.wait_ge(gelu_done, j // 2 - 1)
                u_piece(U0, j)

            def gate_products(g, q, first_use):
                pe.wait_ge(hot1, g + 1)
                pe.wait_ge(hot2, g + 1)
                if not first_use:
                    pe.wait_ge(gated, g - 1)
                for m in range(4):
                    ins = nc.tensor.matmul(ps[:, 2 + q, m * P:(m + 1) * P], hot_a(q)[:, m, :], hot_b(q)[:, m, :],
                                           start=True, stop=True)
                ins.then_inc(gate_mat, 1)

            for q in range(2):
                gate_products(q, q, True)
            with pe.Fori(1, T // 8) as i:
                for q in range(2):
                    gate_products(i * 2 + q, q, False)

            def v_piece(n0, k0, j, first=False, last=False):
                if j % 2 == 0:
                    pe.wait_ge(glo_done, k0 + (j // 2 + 1))
                pe.wait_ge(lo_done, n0 + (V0 + j + 1))
                s, g = (V0 + j) % SPL, j // 2 % 2
                for tb in range(TB):
                    for c in range(2):
                        t = slice(tb * P, (tb + 1) * P)
                        cols = slice(c * 512, (c + 1) * 512)
                        ins = three(ps[:, 4 * tb + 2 * (j % 2) + c, :], gate_hi[:, g, t], gate_lo[:, g, t], whi[:, s, cols],
                                    wlo[:, s, cols], first, last)
                ins.then_inc(used, 1)

            pe.wait_ge(gated, T // 4)
            for j in range(BODY):
                v_piece(0, 0, j, first=j < 2)
            with pe.Fori(1, 2 * NK // BODY) as i:
                for j in range(BODY):
                    v_piece(i * BODY, i * CHUNKS_PER_BODY, j)
            for j in range(2 * NK // BODY * BODY, 2 * NK):
                v_piece(0, 0, j, last=j >= 2 * NK - 2)


BATCH = [(g, tb, h0, h1, w) for g in range(KVH) for tb, h0, h1, w in
         ((0, 8 * g, 8 * g + 8, P), (1, 8 * g, 8 * g + 4, 2 * P), (1, 8 * g + 4, 8 * g + 8, 2 * P))]
TILE_END = []
for _c, _w in IN_TILES:
    TILE_END.append((TILE_END[-1] if TILE_END else W_IN) + DC * _w // PW)


def _half(t, h):
    return TILE_END[t] - 8 + 4 * h + 3


PE_POINTS = {_half(3, 0): [("qk", 0)], _half(3, 1): [("qk", 1), ("s", 0)]}
for _b in range(7):
    _steps = ([("o", _b - 1)] if _b else []) + ([("s", _b + 1)] if _b < 5 else []) + ([("pt", _b)] if _b < 6 else [])
    PE_POINTS[_half(4 + _b // 2, _b % 2)] = _steps
PE_POINTS[_half(7, 1)] = [("rt", 0)]
for _r, _at in enumerate((_half(8, 1), _half(9, 0), _half(9, 1), _half(10, 0))):
    PE_POINTS[_at] = ([("ro", _r - 1)] if _r else []) + [("ri", _r), ("rs", _r)] + ([("rt", _r + 1)] if _r < 3 else [])
PE_LAST = [("ro", 3)]

ACT_POINTS = {}
for _b in range(6):
    ACT_POINTS.setdefault(_half(3 + (_b + 1) // 2, (_b + 1) % 2), []).append(("exp", _b))
for _r, _at in enumerate((_half(9, 0), _half(9, 1), _half(10, 0))):
    ACT_POINTS.setdefault(_at, []).append(("ret", _r))
ACT_LAST = [3]

DVE_ORDER = [("tile", 0), ("tile", 1), ("tile", 2), ("rope_a", 0), ("qk", 0), ("tile", 3), ("qk", 1), ("sin", 0)]
for _b in range(7):
    if _b < 6:
        DVE_ORDER.append(("ssum", _b))
    if _b:
        DVE_ORDER.append(("o", _b - 1))
    if _b < 6:
        DVE_ORDER.append(("pt", _b))
    if _b < 5:
        DVE_ORDER.append(("sin", _b + 1))
    if _b in (1, 3):
        DVE_ORDER.append(("tile", 4 + _b // 2))
    if _b == 2:
        DVE_ORDER.append(("rope_r", QR))
    if _b == 5:
        DVE_ORDER.append(("tile", 6))
DVE_ORDER += [("rope_r", KR), ("kz", 0), ("tile", 7), ("rc", 0), ("tile", 8)]
for _r in range(4):
    DVE_ORDER += ([("cross", _r - 1)] if _r else []) + [("dec", _r), ("st", _r)] + \
                 ([("rc", _r + 1), ("kz", _r + 1)] if _r < 3 else [])
    if _r == 2:
        DVE_ORDER.append(("tile", 9))
DVE_ORDER += [("cross", 3), ("tile", 10), ]


def _pieces(w, width):
    per = PW // width
    k = w.shape[0] // P // per
    return w.reshape(k, per, P, width).transpose(0, 2, 1, 3).reshape(k, P, PW)


def kernel(**inputs):
    import numpy as np
    import concourse.bacc as bacc
    from concourse.bass_utils import run_bass_kernel_spmd

    a = {k: np.asarray(v) for k, v in inputs.items()}

    def tiles(w):
        return [_pieces(w[:, c:c + 512], 512) for c in range(0, w.shape[1], 512)]

    w_in = a["w_in"][0]
    front = [_pieces(a["w_xk"][0], 512), _pieces(a["w_xv"][0], 512)]
    front += [_pieces(w_in[:, c:c + w], w) for c, w in IN_TILES]
    front += tiles(a["w_out"][0]) + tiles(a["w_xq"][0]) + tiles(a["w_xo"][0]) + tiles(a["w_peer_q"][0])
    u = a["peer_u"][0].reshape(NK, NK, 2, 8, P).transpose(1, 2, 4, 3, 0).reshape(2 * NK, P, PW)
    lg = np.log1p(-np.exp2(-5.0 - np.arange(RH)))
    i = np.arange(P)
    diff = i[None, :] - i[:, None]
    decay = np.where(diff[None] >= 0, np.exp(np.maximum(diff, 0)[None] * lg[:, None, None]), 0.0) * RD ** -0.5
    zeta = np.exp((P - 1 - i)[:, None] * lg[None, :]) * RD ** -0.5
    xi = np.exp((i + 1)[:, None] * lg[None, :])
    mask = np.stack([i[None, :] > i[:, None], i[None, :] <= i[:, None]], 1)
    theta = np.float32(10000.0)
    inv = np.concatenate([theta ** (-np.arange(0, d, 2, dtype=np.float32) / np.float32(d)) for d in (HD, RD)])
    arrays = {
        "x": a["x"], "mem": a["mem"], "pos": a["positions"].astype(np.int32).reshape(TB, P).T,
        "gains": np.stack([a["mem_norm_gain"][0], a["mix_norm_gain"][0], a["cross_norm_gain"][0],
                           a["ffn_norm_gain"][0], a["final_norm_gain"]]),
        "out_gains": np.concatenate([a["att_out_gain"][0], a["ret_out_gain"][0]])[None],
        "w_front": np.concatenate(front), "w_u": u, "w_v": a["peer_v"][0],
        "sub_keys": a["peer_sub_keys"][0].reshape(HP, NK, P).transpose(2, 0, 1).reshape(P, HP * NK),
        "sinks": a["att_sinks"].reshape(1, QH),
        "c_ident": np.eye(P, dtype=np.float32), "c_iota": np.tile(i.astype(np.float32), (P, 1)),
        "c_mask": np.where(mask, 0.0, -1e30).astype(np.float32).reshape(P, 2 * P),
        "c_decay": decay.astype(np.float32).transpose(1, 0, 2).reshape(P, RH * P),
        "c_zx": np.concatenate([zeta, xi], 1).astype(np.float32), "c_inv": inv.astype(np.float32)[None],
    }
    arrays = {k: np.ascontiguousarray(v) for k, v in arrays.items()}
    nc = bacc.Bacc("TRN2", target_bir_lowering=False, num_devices=1)
    args = [nc.dram_tensor(f"in_{k}", v.shape, mybir.dt.from_np(v.dtype), kind="ExternalInput").ap()
            for k, v in arrays.items()]
    x2_dram = nc.dram_tensor("x2_scratch", (T, D), F32, kind="Internal").ap()
    out = nc.dram_tensor("out_0", (1, T, D), F32, kind="ExternalOutput").ap()
    hymba_layer(nc, *args, x2_dram, out)
    r = run_bass_kernel_spmd(nc, [{f"in_{k}": v for k, v in arrays.items()}], core_ids=[0])
    return r.results[0]["out_0"]
```

```python
from contextlib import ExitStack

import concourse.bass as bass
from concourse import mybir

F32 = mybir.dt.float32
F32R = mybir.dt.float32r
BF16 = mybir.dt.bfloat16
I32 = mybir.dt.int32
U32 = mybir.dt.uint32
ALU = mybir.AluOpType
ACT = mybir.ActivationFunctionType
AX = mybir.AxisListType.X

P = 128
T = 256
TB = T // P
D = 2048
DC = D // P
EPS = 1e-6
GN_EPS = 1e-5
HD, QH, KVH = 64, 16, 2
RH, RD = 4, 256
XH, XD = 4, 128
PH, NK, TOPK = 8, 128, 16
HP = 2 * PH
QA, KA, VA = 0, 1024, 1152
QR, KR, VR, GR = 1280, 2304, 3328, 4352
IN_COLS = 5376

PW = 1024
RAW = 4
SPL = 3
BODY = 12
W_XK, W_XV, W_IN = 0, 8, 16
W_OUT = W_IN + 2 * 8 + 4 + 8 * 8
W_XQ = W_OUT + 32
W_XO = W_XQ + 8
W_PQ = W_XO + 8
FRONT = W_PQ + 32
U0 = FRONT
V0 = U0 + 2 * NK
END = V0 + 2 * NK
assert FRONT % BODY == 0
IN_TILES = [(0, 512), (512, 512), (1024, 256)] + [(QR + 512 * n, 512) for n in range(8)]
CHUNKS_PER_BODY = BODY // 2
C_TABLES, C_GATE = 54, 60
C_ONES = C_GATE - 2
TOK_PAIRS = T // 2
ACT_BANKS = 3
POOL_END = V0 + 8
assert POOL_END == V0 + BODY - RAW and POOL_END % BODY == 0 and CHUNKS_PER_BODY % ACT_BANKS == 0

BIG = NK * T
H_AT = 0
MEM_AT, X_AT = 0, 4096
Y_AT = TB * IN_COLS
GN_AT = Y_AT + TB * D
QAT_AT = GN_AT + D
KT_AT = QAT_AT + 8 * T
P_AT = KT_AT + 2 * T
PT_AT = P_AT + 1024
KX_AT = PT_AT + 1024
VX_AT = KX_AT + 1024
CS_AT = VX_AT + 1024
DEC_AT = CS_AT + 2 * TB * 160
MASK_AT = DEC_AT + 512
ZX_AT = MASK_AT + 256
INV_AT = ZX_AT + 8
QRT_AT = INV_AT + 160
KRT_AT = QRT_AT + RH * 512
IT_AT = KRT_AT + 2 * 512
ST_AT = IT_AT + RH * 256
KZ_AT = ST_AT + 2 * 512
SMALL_AT = KZ_AT + 2 * 256
IDENT_AT = BIG - P
IOTA_AT = IDENT_AT - P
assert SMALL_AT + 64 <= IOTA_AT
X1_AT, FG_AT, QXT_AT = 0, 4096, 8192
XR_AT = QRT_AT
PX_AT, PXT_AT = QAT_AT, KT_AT
C_FREE = 76
QPT_AT = C_FREE * T
SK_AT = QPT_AT + HP * T
S_AT = SK_AT + HP * P
TK_AT = S_AT + TB * HP * P

C1 = 6.28125
C2 = 0.00193500518798828125
C3 = 3.0199159819567e-07
PI = 3.14159250


def hymba_layer(nc, x, mem, pos, gains, out_gains, w_front, w_u, w_v, sub_keys, sinks,
                ident_d, iota_d, mask_d, decay_d, zx_d, inv_d, x2_dram, out):
    ctx = ExitStack()
    with ctx:
        def sb(name, shape, dt=F32):
            return ctx.enter_context(nc.sbuf_tensor(name, shape, dt))

        def sem(name):
            return ctx.enter_context(nc.semaphore(name))

        big = sb("big", [P, BIG])
        raw = sb("raw", [P, RAW, PW])
        whi = sb("whi", [P, SPL, PW], F32R)
        wlo = sb("wlo", [P, SPL, PW], F32R)
        iota = sb("iota", [P, P], BF16)
        i1_table = sb("i1_table", [P, T])
        table = sb("table", [P, 4, T], BF16)
        hot2_row = sb("hot2_row", [P, 2, P], BF16)
        hot1_rows = sb("hot1_rows", [P, 2, 2, 3, P], BF16)
        stats = sb("stats", [P, 240])
        first = ExitStack()
        xh = first.enter_context(nc.sbuf_tensor("xh", [P, DC, T], F32R))
        xl = first.enter_context(nc.sbuf_tensor("xl", [P, DC, T], F32R))
        first.close()
        x2_back = sb("x2_back", [P, TB, D])
        last_gain = sb("last_gain", [P, D])
        gate_hi = sb("gate_hi", [P, 2, T], F32R)
        gate_lo = sb("gate_lo", [P, 2, T], F32R)
        ps = ctx.enter_context(nc.psum_tensor("ps", [P, 8, 512], F32))

        def at(off, *dims):
            n = 1
            for d in dims:
                n *= d
            v = big[:, off:off + n]
            if len(dims) == 2:
                v = v.rearrange("p (a b) -> p a b", a=dims[0])
            if len(dims) == 3:
                v = v.rearrange("p (a b c) -> p a b c", a=dims[0], b=dims[1])
            if len(dims) == 4:
                v = v.rearrange("p (a b c d) -> p a b c d", a=dims[0], b=dims[1], c=dims[2])
            return v

        ident = at(IDENT_AT, P)
        TK_IOTA = at(IOTA_AT, P)
        H = at(H_AT, TB, IN_COLS)
        Y = at(Y_AT, TB, D)
        QAT = at(QAT_AT, 8, T)
        KT = at(KT_AT, KVH, T)
        PR = at(P_AT, 1024)
        PT = at(PT_AT, 8, P)
        KX = at(KX_AT, XH, T)
        VX = at(VX_AT, TB, XH * XD)
        CS = at(CS_AT, 2, TB, 160)
        DEC = at(DEC_AT, RH, P)
        MASK = at(MASK_AT, 2, P)
        ZX = at(ZX_AT, 2, RH)
        INV = at(INV_AT, 160)
        QRT = at(QRT_AT, RH, 2, T)
        KRT = at(KRT_AT, 2, 2, T)
        IT = at(IT_AT, RH, TB, P)
        ST = at(ST_AT, 2, 2, RD)
        KZ = at(KZ_AT, 2, RD)
        SINK = at(SMALL_AT, QH)
        POSI = at(SMALL_AT + 16, TB).bitcast(I32)
        POSF = at(SMALL_AT + 18, TB)
        ANG = at(MEM_AT + 8192, 3, TB * 160)
        TURN = at(MEM_AT + 8192 + 1280, 2, TB * 160).bitcast(I32)
        SQ = at(QAT_AT, D)
        X1 = at(X1_AT, TB, D)
        XR = at(XR_AT, TB, D)
        QXT = at(QXT_AT, XH, T)
        PX = at(PX_AT, XH * TB, T)
        PXT = at(PXT_AT, XH, TB, T)
        QPT = at(QPT_AT, HP, T)
        SK = at(SK_AT, HP, NK)
        S = at(S_AT, TB * PH, 2 * NK)
        W = at(0, NK, T)

        raw_in = [sem(f"raw_in{i}") for i in range(RAW)]
        hi_done = sem("hi_done")
        lo_done = sem("lo_done")
        lo_v_done = sem("lo_v_done")
        used = sem("used")
        mem_in, x_in, ident_in, gain_in = sem("mem_in"), sem("x_in"), sem("ident_in"), [sem(f"gain_in{i}") for i in range(6)]
        const_in, xr_in, keys_in, x2_out, x2_in, out_done = (sem("const_in"), sem("xr_in"), sem("keys_in"),
                                                            sem("x2_out"), sem("x2_in"), sem("out_done"))
        squares, var_ready, root_ready, normed = sem("squares"), sem("var_ready"), sem("root_ready"), sem("normed")
        xT_ready, xh_ready, xl_ready = sem("xT_ready"), sem("xh_ready"), sem("xl_ready")
        angles, sincos = sem("angles"), sem("sincos")
        tile_out = sem("tile_out")
        roped_a, qk_T, qk_copied = sem("roped_a"), sem("qk_T"), sem("qk_copied")
        scores, scores_read, exp_in, exp_out = sem("scores"), sem("scores_read"), sem("exp_in"), sem("exp_out")
        p_T, p_copied, o_ready, o_out = sem("p_T"), sem("p_copied"), sem("o_ready"), sem("o_out")
        roped, r_T, r_copied, inner, inner_out = sem("roped"), sem("r_T"), sem("r_copied"), sem("inner"), sem("inner_out")
        kz_ready, state, state_out = sem("kz_ready"), sem("state"), sem("state_out")
        ret_o, ret_o_out, ret_cross = sem("ret_o"), sem("ret_o_out"), sem("ret_cross")
        gate_ready, y_ready = sem("gate_ready"), sem("y_ready")
        x_scores, x_max, x_exp, x_prob, x_pT, x_pT_out, x_oT = (sem("x_scores"), sem("x_max"), sem("x_exp"), sem("x_prob"),
                                                               sem("x_pT"), sem("x_pT_out"), sem("x_oT"))
        x3_ready = sem("x3_ready")
        key_scores, key_scores_out = sem("key_scores"), sem("key_scores_out")
        topk, top_ready, top_exp, gates_ready, table_T, table_out = (sem("topk"), sem("top_ready"), sem("top_exp"),
                                                                    sem("gates_ready"), sem("table_T"), sem("table_out"))
        gelu_done, act_taken = sem("gelu_done"), sem("act_taken")
        hot1, hot2, gate_mat, gated = sem("hot1"), sem("hot2"), sem("gate_mat"), sem("gated")
        ghi_done, glo_done = sem("ghi_done"), sem("glo_done")
        dve_step, act_step = sem("dve_step"), sem("act_step")
        y_out = sem("y_out")

        block = ctx.enter_context(nc.Block())

        u_flat = w_u.rearrange("n p c -> (n p) c")
        f_flat = w_front.rearrange("n p c -> (n p) c")
        v_half = w_v.rearrange("(a b) (h c) -> b h a c", b=NK, h=2)

        @block.sync
        def _(sp):
            def load(n0, j, source, split=lo_done):
                sp.wait_ge(split, n0 + (j - RAW + 1))
                sp.dma_start(raw[:, j % RAW, :], source).then_inc(raw_in[j % RAW], 16)

            for j in range(RAW):
                sp.dma_start(raw[:, j, :], w_front[j]).then_inc(raw_in[j], 16)
            for j in range(RAW, BODY):
                load(0, j, w_front[j])
            with sp.Fori(1, FRONT // BODY) as i:
                for j in range(BODY):
                    load(i * BODY, j, w_front[i * BODY + j])
            with sp.Fori(0, 2 * NK // BODY) as i:
                for j in range(BODY):
                    load(i * BODY + U0, j, w_u[i * BODY + j])
            rest = 2 * NK // BODY * BODY
            for j in range(rest, 2 * NK):
                load(U0, j, w_u[j])
            for j in range(BODY):
                load(V0, j, v_half[j // 2, j % 2])
            with sp.Fori(1, 2 * NK // BODY) as i:
                for j in range(BODY):
                    load(i * BODY + (V0 - POOL_END), j, v_half[i * CHUNKS_PER_BODY + j // 2, j % 2], lo_v_done)
            for j in range(rest, 2 * NK):
                load(V0 - POOL_END, j, v_half[j // 2, j % 2], lo_v_done)
            for tb in range(TB):
                sp.wait_ge(y_out, tb + 1)
                sp.dma_start(out[0, tb * P:(tb + 1) * P, :], x2_back[:, tb, :]).then_inc(out_done, 16)
            sp.wait_ge(out_done, 32)

        @block.gpsimd
        def _(pool):
            for dst, src in ((TK_IOTA, iota_d), (MASK, mask_d.rearrange("p (a b) -> p a b", a=2)),
                             (DEC, decay_d.rearrange("p (a b) -> p a b", a=RH)),
                             (ZX, zx_d.rearrange("p (a b) -> p a b", a=2)),
                             (INV, inv_d.partition_broadcast(P)), (POSI, pos),
                             (SINK, sinks.partition_broadcast(P))):
                pool.dma_start(dst, src).then_inc(const_in, 16)

            def rest_of(n0, j):
                pool.wait_ge(hi_done, n0 + (j + 1))
                nc.gpsimd.tensor_tensor(wlo[:, j % SPL, :], raw[:, j % RAW, :], whi[:, j % SPL, :],
                                        ALU.subtract).then_inc(lo_done, 1)

            with pool.Fori(0, POOL_END // BODY) as i:
                for j in range(BODY):
                    rest_of(i * BODY, j)

        @block.scalar
        def _(act):
            steps = [0]

            act.dma_start(at(MEM_AT, TB, D), mem[0].rearrange("(b p) d -> p b d", p=P)).then_inc(mem_in, 16)
            act.dma_start(ident, ident_d).then_inc(ident_in, 16)
            act.dma_start(at(X_AT, TB, D), x[0].rearrange("(b p) d -> p b d", p=P)).then_inc(x_in, 16)
            act.dma_start(at(GN_AT, D), gains[0:1, :].partition_broadcast(P)).then_inc(gain_in[0], 16)
            act.dma_start(at(QRT_AT, D), gains[1:2, :].partition_broadcast(P)).then_inc(gain_in[1], 16)

            def square_sum(src, col):
                nc.scalar.activation(SQ, src, ACT.Square, accum_out=stats[:, col:col + 1]).then_inc(squares, 1)
                steps[0] += 1
                act.wait_ge(squares, steps[0])

            def root(n, cols):
                act.wait_ge(var_ready, n)
                nc.scalar.activation(stats[:, 80:80 + cols], stats[:, 40:40 + cols], ACT.Sqrt).then_inc(root_ready, 1)

            def high(j, n0=0):
                act.wait_ge(raw_in[j % RAW], (n0 + (j // RAW * RAW + RAW)) * (16 // RAW))
                if not (isinstance(n0, int) and n0 + j < SPL):
                    act.wait_ge(used, n0 + (j - SPL + 1))
                nc.scalar.activation(whi[:, j % SPL, :], raw[:, j % RAW, :], ACT.Copy).then_inc(hi_done, 1)

            def transposed_high(k):
                for b in range(8):
                    act.wait_ge(xT_ready, 8 * k + b + 1)
                    nc.scalar.activation(xh[:, 2 * b:2 * b + 2, :],
                                         ps[:, b, :].rearrange("p (a b) -> p a b", a=2), ACT.Copy).then_inc(xh_ready, 1)

            act.wait_ge(mem_in, 16)
            for tb in range(TB):
                square_sum(at(MEM_AT, TB, D)[:, tb, :], tb)
            act.wait_ge(x_in, 16)
            for tb in range(TB):
                square_sum(at(X_AT, TB, D)[:, tb, :], 2 + tb)
            root(1, 4)
            act.wait_ge(angles, 1)
            nc.scalar.activation(CS, ANG[:, 0:2, :].rearrange("p a (b c) -> p a b c", b=TB), ACT.Sin).then_inc(sincos, 1)
            transposed_high(0)
            for j in range(W_XK, W_IN):
                high(j)
            act.wait_ge(used, W_IN)
            transposed_high(1)

            def exps(b):
                act.wait_ge(exp_in, b + 1)
                n, k = BATCH[b][3] - BATCH[b][2], BATCH[b][4]
                nc.scalar.activation(PR[:, 0:n * k], PR[:, 0:n * k], ACT.Exp)
                nc.scalar.activation(stats[:, 128:128 + n], stats[:, 144:144 + n], ACT.Exp).then_inc(exp_out, 1)

            for j in range(W_IN, W_OUT):
                high(j)
                for b in ACT_POINTS.get(j, ()):
                    exps(b)
            act.wait_ge(roped, 6)
            act.dma_start(at(GN_AT, D), out_gains.partition_broadcast(P)).then_inc(gain_in[5], 16)
            act.wait_ge(tile_out, 2 + len(IN_TILES))
            for tb in range(TB):
                nc.scalar.activation(H[:, tb, GR:GR + 1024], H[:, tb, GR:GR + 1024], ACT.Silu).then_inc(gate_ready, 1)
            root(2, 40)
            act.wait_ge(ret_cross, RH)
            act.dma_start(XR, x[0].rearrange("(b p) d -> p b d", p=P)).then_inc(xr_in, 16)
            act.wait_ge(y_ready, 1)
            act.dma_start(at(GN_AT, D), gains[2:3, :].partition_broadcast(P)).then_inc(gain_in[2], 16)
            act.dma_start(at(FG_AT, D), gains[3:4, :].partition_broadcast(P)).then_inc(gain_in[3], 16)
            transposed_high(2)
            for j in range(W_OUT, W_XQ):
                high(j)
            act.wait_ge(tile_out, 17)
            for tb in range(TB):
                square_sum(X1[:, tb, :], tb)
            act.dma_start(SK, sub_keys.rearrange("p (a b) -> p a b", a=HP)).then_inc(keys_in, 16)
            root(3, 2)
            transposed_high(3)
            for j in range(W_XQ, W_XO):
                high(j)
            act.wait_ge(x_max, 1)
            for h in range(XH):
                for tb in range(TB):
                    k = h * TB + tb
                    nc.scalar.activation(PX[:, k, :], ps[:, 4 + h, tb * T:(tb + 1) * T], ACT.Exp,
                                         bias=stats[:, 208 + k:209 + k], scale=XD ** -0.5,
                                         accum_out=stats[:, 216 + k:217 + k]).then_inc(x_exp, 1)
            act.wait_ge(x_oT, 1)
            nc.scalar.activation(xh[:, 0:XH, :], ps[:, 4:8, 0:T], ACT.Copy).then_inc(xh_ready, 1)
            for j in range(W_XO, W_PQ):
                high(j)
            act.wait_ge(tile_out, 22)
            for tb in range(TB):
                square_sum(X1[:, tb, :], tb)
            act.dma_start(x2_dram.rearrange("(b p) d -> p b d", p=P), X1).then_inc(x2_out, 16)
            root(4, 2)
            for b in range(8):
                act.wait_ge(xT_ready, 8 * 4 + b + 1)
                nc.scalar.activation(xh[:, 2 * b:2 * b + 2, :],
                                     ps[:, b, :].rearrange("p (a b) -> p a b", a=2), ACT.Copy).then_inc(xh_ready, 1)
            for j in range(W_PQ, U0):
                high(j)

            act.wait_ge(x2_out, 16)
            act.wait_ge(xl_ready, 34)

            def gelu(k0, c):
                nc.scalar.activation(W[:, k0 + c, :], ps[:, c % ACT_BANKS, 0:T], ACT.Gelu).then_inc(act_taken, 1)

            def gelu_in_place(c):
                a = ps[:, c % ACT_BANKS, 0:T]
                nc.scalar.activation(a, a, ACT.Gelu).then_inc(gelu_done, 1)

            for j in range(BODY):
                high(j, U0)
                if j % 2 == 0 and j >= 4:
                    gelu(0, j // 2 - 2)

            def body(i):
                for j in range(BODY):
                    high(j, i * BODY + U0)
                    if j % 2 == 0:
                        gelu(i * CHUNKS_PER_BODY - ACT_BANKS, j // 2 - 2 + ACT_BANKS)

            with act.Fori(1, C_TABLES // CHUNKS_PER_BODY) as i:
                body(i)
            act.wait_ge(top_ready, 1)
            GE = at(TK_AT, TB * PH, TOPK)
            nc.scalar.activation(GE, GE, ACT.Exp).then_inc(top_exp, 1)
            with act.Fori(C_TABLES // CHUNKS_PER_BODY, C_GATE // CHUNKS_PER_BODY) as i:
                body(i)
            with act.Fori(C_GATE // CHUNKS_PER_BODY, NK // CHUNKS_PER_BODY) as i:
                for j in range(BODY):
                    high(j, i * BODY + U0)
                    if j % 2 == 0:
                        gelu_in_place(j // 2 - 2 + ACT_BANKS)
            for j in range(NK // CHUNKS_PER_BODY * BODY, 2 * NK):
                high(j, U0)
                if j % 2 == 0:
                    gelu_in_place(j // 2 - 2)

            def high_v(n0, j):
                act.wait_ge(raw_in[j % RAW], (n0 + (j // RAW * RAW + RAW + V0 // RAW * RAW)) * (16 // RAW))
                act.wait_ge(used, n0 + (V0 + j - SPL + 1))
                nc.scalar.activation(whi[:, (V0 + j) % SPL, :], raw[:, j % RAW, :], ACT.Copy).then_inc(hi_done, 1)

            def gated_high(k0, k):
                nc.scalar.activation(gate_hi[:, k % 2, :], W[:, k0 + k, :], ACT.Copy).then_inc(ghi_done, 1)

            assert V0 % RAW == 0
            high_v(0, 0)
            gelu_in_place(NK - 2)
            high_v(0, 1)
            high_v(0, 2)
            gelu_in_place(NK - 1)
            act.wait_ge(used, V0)
            act.wait_ge(gated, TOK_PAIRS)
            act.wait_ge(act_taken, NK)
            gated_high(0, 0)
            gated_high(0, 1)
            act.dma_start(x2_back[:, :, :], x2_dram.rearrange("(b p) d -> p b d", p=P)).then_inc(x2_in, 16)
            act.dma_start(last_gain[:, :], gains[4:5, :].partition_broadcast(P)).then_inc(gain_in[4], 16)
            for j in range(3, BODY):
                high_v(0, j)
                if j % 2 == 0:
                    gated_high(0, j // 2)
            with act.Fori(1, 2 * NK // BODY) as i:
                for j in range(BODY):
                    high_v(i * BODY, j)
                    if j % 2 == 0:
                        gated_high(i * CHUNKS_PER_BODY, j // 2)
            for j in range(2 * NK // BODY * BODY, 2 * NK):
                high_v(0, j)
                if j % 2 == 0:
                    gated_high(0, j // 2)
            act.wait_ge(glo_done, NK)
            for tb in range(TB):
                act.wait_ge(x3_ready, tb + 1)
                nc.scalar.activation(at(0, TB, D)[:, tb, :], x2_back[:, tb, :], ACT.Square,
                                     accum_out=stats[:, tb:tb + 1]).then_inc(squares, 1)
            root(5, 2)

        @block.vector
        def _(dve):
            n = [0]

            def step(ins):
                n[0] += 1
                ins.then_inc(dve_step, 1)
                dve.wait_ge(dve_step, n[0])

            def inverse_root(k, cols, eps):
                v, r, t = stats[:, 40:40 + cols], stats[:, 160:160 + cols], stats[:, 80:80 + cols]
                dve.wait_ge(root_ready, k)
                step(nc.vector.reciprocal(r, t))
                step(nc.vector.tensor_tensor(t, r, r, ALU.mult))
                step(nc.vector.tensor_tensor(t, t, v, ALU.mult))
                step(nc.vector.tensor_scalar(t, t, -0.5, 1.5, ALU.mult, ALU.add))
                step(nc.vector.tensor_tensor(r, r, t, ALU.mult))

            def variances(cols, squares_done):
                dve.wait_ge(squares, squares_done)
                nc.vector.tensor_scalar(stats[:, 40:40 + cols], stats[:, 0:cols], 1.0 / D, EPS,
                                        ALU.mult, ALU.add).then_inc(var_ready, 1)

            def norm_rows(src, gain, col):
                for tb in range(TB):
                    nc.vector.scalar_tensor_tensor(Y[:, tb, :], src[:, tb, :], stats[:, 160 + col + tb:161 + col + tb],
                                                   gain, ALU.mult, ALU.mult).then_inc(normed, 1)

            def transposed_low(first_count):
                for b in range(8):
                    dve.wait_ge(xh_ready, first_count + b + 1)
                    nc.vector.tensor_tensor(xl[:, 2 * b:2 * b + 2, :],
                                            ps[:, b, :].rearrange("p (a b) -> p a b", a=2),
                                            xh[:, 2 * b:2 * b + 2, :], ALU.subtract).then_inc(xl_ready, 1)

            variances(4, 4)
            dve.wait_ge(const_in, 7 * 16)
            step(nc.vector.tensor_copy(iota[:, :], TK_IOTA))
            TF = at(MEM_AT + 8192 + 1920, 2, TB * 160)
            step(nc.vector.tensor_copy(POSF, POSI))
            for tb in range(TB):
                step(nc.vector.tensor_scalar(ANG[:, 2, tb * 160:(tb + 1) * 160], INV, POSF[:, tb:tb + 1], None, ALU.mult))
            for k, shift in ((0, 0.0), (1, 0.25)):
                step(nc.vector.tensor_scalar(TF[:, k, :], ANG[:, 2, :], 0.15915494309189535, shift, ALU.mult, ALU.add))
                step(nc.vector.tensor_copy(TURN[:, k, :], TF[:, k, :]))
                step(nc.vector.tensor_copy(TF[:, k, :], TURN[:, k, :]))
                step(nc.vector.scalar_tensor_tensor(ANG[:, k, :], TF[:, k, :], -C1, ANG[:, 2, :], ALU.mult, ALU.add))
                step(nc.vector.scalar_tensor_tensor(ANG[:, k, :], TF[:, k, :], -C2, ANG[:, k, :], ALU.mult, ALU.add))
                step(nc.vector.scalar_tensor_tensor(ANG[:, k, :], TF[:, k, :], -C3, ANG[:, k, :], ALU.mult, ALU.add))
                if k:
                    step(nc.vector.tensor_scalar(ANG[:, k, :], ANG[:, k, :], PI / 2, None, ALU.add))
            nc.vector.tensor_scalar(ANG[:, 0:2, :], ANG[:, 0:2, :], PI, -PI, ALU.min, ALU.max).then_inc(angles, 1)
            inverse_root(1, 4, EPS)
            dve.wait_ge(gain_in[0], 16)
            norm_rows(at(MEM_AT, TB, D), at(GN_AT, D), 0)
            transposed_low(0)
            dve.wait_ge(gain_in[1], 16)
            dve.wait_ge(xT_ready, 8)
            norm_rows(at(X_AT, TB, D), at(QRT_AT, D), 2)
            dve.wait_ge(used, 8)
            nc.vector.tensor_copy(KX, ps[:, 0:4, 0:T]).then_inc(tile_out, 1)
            dve.wait_ge(used, 16)
            nc.vector.tensor_copy(VX, ps[:, 4:6, :]).then_inc(tile_out, 1)
            transposed_low(8)

            def in_tile(t):
                c0, w = IN_TILES[t]
                dve.wait_ge(used, TILE_END[t])
                b = 2 * (t % 2)
                nc.vector.tensor_copy(H[:, :, c0:c0 + w], ps[:, b:b + 2, 0:w]).then_inc(tile_out, 1)
                dve.wait_ge(tile_out, 3 + t)

            ropes = [0]

            def rope(tb, c0, heads, half, tab):
                v = H[:, tb, c0:c0 + heads * 2 * half].rearrange("p (n two f) -> p n two f", two=2, f=half)
                x1, x2 = v[:, :, 0, :], v[:, :, 1, :]
                m = heads * half
                t = [at(GN_AT + 576 * k, heads, half) if m > 512 else at(GN_AT + 512 * k, heads, half) for k in range(3)]
                sin, cos = (CS[:, k, tb, tab:tab + half].unsqueeze(1).broadcast_to([P, heads, half]) for k in range(2))
                nc.vector.tensor_tensor(t[0], x1, cos, ALU.mult)
                nc.vector.tensor_tensor(t[1], x2, sin, ALU.mult)
                step(nc.vector.tensor_tensor(t[2], x1, sin, ALU.mult))
                step(nc.vector.tensor_tensor(x1, t[0], t[1], ALU.subtract))
                step(nc.vector.tensor_tensor(t[0], x2, cos, ALU.mult))
                nc.vector.tensor_tensor(x2, t[0], t[2], ALU.add).then_inc(roped, 1)
                ropes[0] += 1
                dve.wait_ge(roped, ropes[0])

            def rope_a(_):
                dve.wait_ge(sincos, 1)
                for tb in range(TB):
                    rope(tb, QA, QH + KVH, HD // 2, 0)
                for tb in range(TB):
                    for g in range(KVH):
                        src = H[:, tb, KA + g * HD:KA + (g + 1) * HD].unsqueeze(1).broadcast_to([P, 2, HD])
                        nc.vector.tensor_copy(at(P_AT + (tb * KVH + g) * P, 2, HD), src).then_inc(roped_a, 1)

            def qk_copies(g):
                dve.wait_ge(qk_T, g + 1)
                b = 4 if g == 0 else 6
                if g == 0:
                    nc.vector.tensor_copy(KT, ps[:, 6, :].rearrange("p (a b) -> p a b", a=2))
                nc.vector.tensor_copy(QAT[:, 4 * g:4 * g + 4, :],
                                      ps[:, b:b + 2, :].rearrange("p a (b c) -> p (a b) c", b=2)).then_inc(qk_copied, 1)

            def softmax_in(b):
                g, tb, h0, h1, w = BATCH[b]
                m = h1 - h0
                pr = PR[:, 0:m * w].rearrange("p (a b) -> p a b", a=m)
                src = ps[:, 4:6, :].rearrange("p a b -> p (a b)")[:, 0:m * w].rearrange("p (a b) -> p a b", a=m)
                mask = MASK.rearrange("p a b -> p (a b)")[:, 2 * P - w:2 * P].unsqueeze(1).broadcast_to([P, m, w])
                dve.wait_ge(scores, b + 1)
                if b:
                    dve.wait_ge(p_T, b)
                nc.vector.scalar_tensor_tensor(pr, src, HD ** -0.5, mask, ALU.mult, ALU.add).then_inc(scores_read, 1)
                dve.wait_ge(scores_read, b + 1)
                mx = stats[:, 120:120 + m]
                step(nc.vector.reduce_max(mx, pr, AX))
                mx2 = mx.rearrange("p (b a) -> p b a", b=2)
                sink = SINK[:, h0:h1].rearrange("p (a b) -> p b a", b=2)
                step(nc.vector.tensor_tensor(mx2, mx2, sink, ALU.max))
                nc.vector.tensor_tensor(stats[:, 144:144 + m].rearrange("p (b a) -> p b a", b=2), sink, mx2, ALU.subtract)
                nc.vector.tensor_tensor(pr, pr, mx.unsqueeze(2).broadcast_to([P, m, w]), ALU.subtract).then_inc(exp_in, 1)

            def softmax_sum(b):
                g, tb, h0, h1, w = BATCH[b]
                m = h1 - h0
                dve.wait_ge(exp_out, b + 1)
                pr = PR[:, 0:m * w].rearrange("p (a b) -> p a b", a=m)
                r = stats[:, 200 + 8 * (b % 2):200 + 8 * (b % 2) + m]
                step(nc.vector.reduce_sum(r, pr, AX))
                step(nc.vector.tensor_tensor(r, r, stats[:, 128:128 + m], ALU.add))
                step(nc.vector.reciprocal(r, r))

            def o_rows(b):
                g, tb, h0, h1, w = BATCH[b]
                m = h1 - h0
                dve.wait_ge(o_ready, b + 1)
                r = stats[:, 200 + 8 * (b % 2):200 + 8 * (b % 2) + m]
                nc.vector.tensor_tensor(Y[:, tb, h0 * HD:h1 * HD].rearrange("p (a b d) -> p a b d", b=2, d=HD),
                                        ps[:, 6, 0:m * HD].rearrange("p (a b d) -> p a b d", b=2, d=HD),
                                        r.rearrange("p (b a) -> p a b", b=2).unsqueeze(3).broadcast_to([P, m // 2, 2, HD]),
                                        ALU.mult).then_inc(o_out, 1)

            def p_copies(b):
                dve.wait_ge(p_T, b + 1)
                nc.vector.tensor_copy(PT, ps[:, 6:8, :].rearrange("p a (b c) -> p (a b) c", b=4)).then_inc(p_copied, 1)

            def rope_r(c0):
                for tb in range(TB):
                    rope(tb, c0, RH, RD // 2, 32)

            def r_copies(r):
                dve.wait_ge(r_T, r + 1)
                nc.vector.tensor_copy(QRT[:, r], ps[:, 4, :].rearrange("p (a b) -> p a b", a=2))
                nc.vector.tensor_copy(KRT[:, r % 2], ps[:, 5, :].rearrange("p (a b) -> p a b", a=2)).then_inc(r_copied, 1)

            def inner_decay(r):
                dve.wait_ge(inner, r + 1)
                nc.vector.tensor_tensor(IT[:, r], ps[:, 6, 0:T].rearrange("p (a b) -> p a b", a=TB),
                                        DEC[:, r, :].unsqueeze(1).broadcast_to([P, TB, P]), ALU.mult).then_inc(inner_out, 1)

            def kz_rows(r):
                if r >= 2:
                    dve.wait_ge(state, r - 1)
                nc.vector.tensor_scalar(KZ[:, r % 2, :], H[:, 0, KR + r * RD:KR + (r + 1) * RD], ZX[:, 0, r:r + 1],
                                        None, ALU.mult).then_inc(kz_ready, 1)

            def state_copy(r):
                dve.wait_ge(state, r + 1)
                nc.vector.tensor_copy(ST[:, r % 2], ps[:, 7, :].rearrange("p (a b) -> p a b", a=2)).then_inc(state_out, 1)

            def cross_rows(r):
                dve.wait_ge(ret_o, r + 1)
                nc.vector.tensor_copy(Y[:, :, 1024 + r * RD:1024 + (r + 1) * RD],
                                      ps[:, 6, :].rearrange("p (a b) -> p a b", a=TB)).then_inc(ret_o_out, 1)
                dve.wait_ge(ret_o_out, r + 1)
                y = Y[:, 1, 1024 + r * RD:1024 + (r + 1) * RD]
                nc.vector.scalar_tensor_tensor(y, ps[:, 7, 0:RD], ZX[:, 1, r:r + 1], y, ALU.mult, ALU.add).then_inc(ret_cross, 1)

            do = {"tile": in_tile, "rope_a": rope_a, "qk": qk_copies, "sin": softmax_in, "ssum": softmax_sum,
                  "o": o_rows, "pt": p_copies, "rope_r": rope_r, "rc": r_copies, "dec": inner_decay, "kz": kz_rows,
                  "st": state_copy, "cross": cross_rows}
            for what, k in DVE_ORDER:
                do[what](k)

            dve.wait_ge(ret_cross, RH)
            dve.wait_ge(o_out, len(BATCH))
            SQA = at(P_AT, 2, 1024)
            ms = stats[:, 0:32].rearrange("p (a b) -> p a b", a=TB)
            step(nc.vector.tensor_tensor(SQA, Y[:, :, 0:1024], Y[:, :, 0:1024], ALU.mult))
            for tb in range(TB):
                step(nc.vector.reduce_sum(ms[:, tb, :], SQA[:, tb, :].rearrange("p (a b) -> p a b", a=QH), AX))
            step(nc.vector.tensor_scalar(stats[:, 40:72], stats[:, 0:32], 1.0 / HD, EPS, ALU.mult, ALU.add))
            BN = at(QAT_AT, TB * RH, 6)
            MV = at(QAT_AT + 64, TB * RH, 2)
            for tb in range(TB):
                for r in range(RH):
                    step(nc.vector.bn_stats(BN[:, tb * RH + r, :], Y[:, tb, 1024 + r * RD:1024 + (r + 1) * RD]))
                    step(nc.vector.bn_aggr(MV[:, tb * RH + r, :], BN[:, tb * RH + r, :]))
            nc.vector.tensor_scalar(stats[:, 72:80], MV[:, :, 1], GN_EPS, None, ALU.add).then_inc(var_ready, 1)
            inverse_root(2, 40, EPS)
            for tb in range(TB):
                ya = Y[:, tb, 0:1024].rearrange("p (a b) -> p a b", a=QH)
                nc.vector.tensor_tensor(ya, ya, stats[:, 160 + 16 * tb:176 + 16 * tb].unsqueeze(2).broadcast_to([P, QH, HD]), ALU.mult)
                for r in range(RH):
                    yr = Y[:, tb, 1024 + r * RD:1024 + (r + 1) * RD]
                    k = tb * RH + r
                    ins = nc.vector.tensor_scalar(yr, yr, MV[:, k, 0:1], stats[:, 192 + k:193 + k], ALU.subtract, ALU.mult)
                step(ins)
            dve.wait_ge(gain_in[5], 16)
            step(nc.vector.tensor_tensor(Y, Y, at(GN_AT, D).unsqueeze(1).broadcast_to([P, TB, D]), ALU.mult))
            dve.wait_ge(gate_ready, 2)
            nc.vector.tensor_tensor(Y[:, :, 1024:D], Y[:, :, 1024:D], H[:, :, GR:GR + 1024], ALU.mult).then_inc(y_ready, 1)
            transposed_low(16)

            dve.wait_ge(xr_in, 16)
            for t in range(4):
                dve.wait_ge(used, W_OUT + 8 * t + 8)
                b = 2 * (t % 2)
                ins = nc.vector.tensor_tensor(X1[:, :, 512 * t:512 * t + 512], ps[:, b:b + 2, :],
                                              XR[:, :, 512 * t:512 * t + 512], ALU.add).then_inc(tile_out, 1)
            variances(2, 6)
            inverse_root(3, 2, EPS)
            dve.wait_ge(gain_in[2], 16)
            dve.wait_ge(xT_ready, 24)
            norm_rows(X1, at(GN_AT, D), 0)
            transposed_low(24)

            dve.wait_ge(used, W_XO)
            nc.vector.tensor_copy(QXT, ps[:, 0:4, 0:T]).then_inc(tile_out, 1)
            dve.wait_ge(x_scores, 1)
            sc = ps[:, 4:8, :].rearrange("p a (b c) -> p (a b) c", b=TB)
            step(nc.vector.reduce_max(stats[:, 224:232], sc, AX))
            nc.vector.tensor_scalar(stats[:, 208:216], stats[:, 224:232], -XD ** -0.5, None, ALU.mult).then_inc(x_max, 1)
            dve.wait_ge(x_exp, 8)
            step(nc.vector.reciprocal(stats[:, 232:240], stats[:, 216:224]))
            nc.vector.tensor_tensor(PX, PX, stats[:, 232:240].unsqueeze(2).broadcast_to([P, 8, T]), ALU.mult).then_inc(x_prob, 1)
            dve.wait_ge(x_pT, 1)
            nc.vector.tensor_copy(PXT, ps[:, 0:4, :].rearrange("p a (b c) -> p a b c", b=TB)).then_inc(x_pT_out, 1)
            dve.wait_ge(xh_ready, 33)
            nc.vector.tensor_tensor(xl[:, 0:XH, :], ps[:, 4:8, 0:T], xh[:, 0:XH, :], ALU.subtract).then_inc(xl_ready, 1)
            for t in range(4):
                dve.wait_ge(used, W_XO + 2 * t + 2)
                b = 2 * (t % 2)
                dst = X1[:, :, 512 * t:512 * t + 512]
                nc.vector.tensor_tensor(dst, ps[:, b:b + 2, :], dst, ALU.add).then_inc(tile_out, 1)

            variances(2, 8)
            inverse_root(4, 2, EPS)
            dve.wait_ge(gain_in[3], 16)
            norm_rows(X1, at(FG_AT, D), 0)
            transposed_low(33)
            for t in range(4):
                dve.wait_ge(used, W_PQ + 8 * t + 8)
                b = 4 * (t % 2)
                nc.vector.tensor_copy(QPT[:, 4 * t:4 * t + 4, :], ps[:, b:b + 4, 0:T]).then_inc(tile_out, 1)
            for tb in range(TB):
                dve.wait_ge(key_scores, tb + 1)
                nc.vector.tensor_copy(S[:, tb * PH:(tb + 1) * PH, :],
                                      ps[:, 4 * tb:4 * tb + 4, :].rearrange("p a (b c) -> p (a b) c", b=2)).then_inc(key_scores_out, 1)
            dve.wait_ge(key_scores_out, 2)
            nc.vector.memset(W[:, C_ONES:C_FREE, :], 1.0)

            o = TK_AT
            def small(*dims):
                nonlocal o
                v = at(o, *dims)
                m = 1
                for d in dims:
                    m *= d
                o += m
                return v
            GE = small(TB * PH, TOPK)
            CH = small(2, TB * PH * TOPK)
            cur, cur2, v, ixf = small(2, NK), small(2, NK), small(2, TOPK), small(2, TOPK)
            ix = small(2, TOPK).bitcast(U32)
            cand, cand2, top = small(TOPK * TOPK), small(TOPK * TOPK), small(TOPK)
            where = small(TOPK).bitcast(U32)
            ab, abf = small(2, TOPK).bitcast(U32), small(2, TOPK)
            oh = small(2, TOPK, TOPK)
            assert o <= IOTA_AT
            LOW = -3.0e38
            with dve.Fori(0, TB * PH) as r:
                k = [0]

                def tick(ins):
                    k[0] += 1
                    ins.then_inc(topk, 1)
                    dve.wait_ge(topk, k[0])

                tick(nc.vector.tensor_copy(cur, S[:, bass.ds(r, 1), :].rearrange("p a (b c) -> p (a b) c", b=2)))
                for c, half in ((cur, 0), (cur2, 8)):
                    for p in range(2):
                        ins = nc.vector.max(v[:, p, half:half + 8], c[:, p, :])
                    tick(ins)
                    for p in range(2):
                        ins = nc.vector.max_index(ix[:, p, half:half + 8], v[:, p, half:half + 8], c[:, p, :])
                    if half == 0:
                        for p in range(2):
                            ins = nc.vector.match_replace(cur2[:, p, :], v[:, p, 0:8], cur[:, p, :], LOW)
                    tick(ins)
                tick(nc.vector.tensor_copy(ixf, ix))
                tick(nc.vector.tensor_tensor(cand.rearrange("p (a b) -> p a b", a=TOPK),
                                             v[:, 0, :].unsqueeze(2).broadcast_to([P, TOPK, TOPK]),
                                             v[:, 1, :].unsqueeze(1).broadcast_to([P, TOPK, TOPK]), ALU.add))
                tick(nc.vector.max(top[:, 0:8], cand))
                tick(nc.vector.max_index(where[:, 0:8], top[:, 0:8], cand))
                tick(nc.vector.match_replace(cand2, top[:, 0:8], cand, LOW))
                tick(nc.vector.max(top[:, 8:16], cand2))
                tick(nc.vector.max_index(where[:, 8:16], top[:, 8:16], cand2))
                tick(nc.vector.tensor_copy(GE[:, bass.ds(r, 1), :], top.unsqueeze(1)))
                tick(nc.vector.tensor_scalar(ab[:, 0, :], where, 4, None, ALU.logical_shift_right))
                tick(nc.vector.tensor_scalar(ab[:, 1, :], where, 15, None, ALU.bitwise_and))
                tick(nc.vector.tensor_copy(abf, ab))
                tick(nc.vector.tensor_tensor(oh, iota[:, 0:TOPK].unsqueeze(1).unsqueeze(1).broadcast_to([P, 2, TOPK, TOPK]),
                                             abf.unsqueeze(3).broadcast_to([P, 2, TOPK, TOPK]), ALU.is_equal))
                tick(nc.vector.tensor_tensor(oh, oh, ixf.unsqueeze(2).broadcast_to([P, 2, TOPK, TOPK]), ALU.mult))
                tick(nc.vector.reduce_sum(CH[:, :, bass.ds(r * TOPK, TOPK)], oh, AX))
                dve.sem_clear(topk)
            top1 = stats[:, 0:16]
            step(nc.vector.tensor_copy(top1.unsqueeze(2), GE[:, :, 0:1]))
            nc.vector.tensor_tensor(GE, GE, top1.unsqueeze(2).broadcast_to([P, 16, TOPK]), ALU.subtract).then_inc(top_ready, 1)
            dve.wait_ge(top_exp, 1)
            step(nc.vector.reduce_sum(top1, GE, AX))
            step(nc.vector.reciprocal(top1, top1))
            nc.vector.tensor_tensor(GE, GE, top1.unsqueeze(2).broadcast_to([P, 16, TOPK]), ALU.mult).then_inc(gates_ready, 1)
            dve.wait_ge(table_T, 1)
            nc.vector.tensor_copy(i1_table[:, :], ps[:, 4, 0:T])
            nc.vector.tensor_copy(table[:, 0, :], ps[:, 4, T:2 * T])
            rest = at(TK_AT, 2, T)
            step(nc.vector.tensor_copy(table[:, 1, :], ps[:, 5, 0:T]))
            step(nc.vector.tensor_tensor(rest[:, 0, :], ps[:, 5, 0:T], table[:, 1, :], ALU.subtract))
            step(nc.vector.tensor_copy(table[:, 2, :], rest[:, 0, :]))
            step(nc.vector.tensor_tensor(rest[:, 1, :], rest[:, 0, :], table[:, 2, :], ALU.subtract))
            step(nc.vector.tensor_copy(table[:, 3, :], rest[:, 1, :]))
            step(nc.vector.memset(W[:, C_FREE:NK, :], 1.0))

            def hot_i1(g, q):
                for m in range(2):
                    t = bass.ds(g * 2 + m, 1)
                    parts = table[:, 1:4, t].broadcast_to([P, 3, P])
                    ins = nc.vector.scalar_tensor_tensor(hot1_rows[:, q, m], iota[:, :].unsqueeze(1).broadcast_to([P, 3, P]),
                                                         i1_table[:, t], parts, ALU.is_equal, ALU.mult)
                ins.then_inc(hot1, 1)

            def hot_i2(g):
                nc.vector.tensor_tensor(hot2_row[:, :, :], iota[:, :].unsqueeze(1).broadcast_to([P, 2, P]),
                                        table[:, 0, bass.ds(g * 2, 2)].unsqueeze(2).broadcast_to([P, 2, P]),
                                        ALU.is_equal).then_inc(hot2, 1)

            def take_chunk(k0, c, pairs):
                dve.wait_ge(gelu_done, k0 + (c + 1 - C_ONES))
                if not (isinstance(pairs, int) and pairs == 0):
                    dve.wait_ge(gated, pairs)
                nc.vector.tensor_tensor(W[:, k0 + c, :], ps[:, c % ACT_BANKS, 0:T], W[:, k0 + c, :], ALU.mult).then_inc(act_taken, 1)

            def gate_step(i, j, last=TOK_PAIRS):
                g = i * BODY + j
                dve.wait_ge(gate_mat, g + 1)
                if last > j + 1:
                    hot_i2(g + 1)
                if j % 2 == 0:
                    take_chunk(i * CHUNKS_PER_BODY + (C_GATE - CHUNKS_PER_BODY), j // 2 - 2 + CHUNKS_PER_BODY, g)
                dve.wait_ge(act_taken, i * CHUNKS_PER_BODY + (C_ONES + 1 + j // 2))
                w = W[:, :, bass.ds(g * 2, 2)]
                nc.vector.tensor_tensor(w, ps[:, 4 + j % 2, 0:T].rearrange("p (m k) -> p k m", m=2), w, ALU.mult).then_inc(gated, 1)
                if last > j + 2:
                    hot_i1(g + 2, j % 2)

            hot_i2(0)
            hot_i1(0, 0)
            hot_i1(1, 1)
            full = TOK_PAIRS // BODY
            for j in range(BODY):
                gate_step(0, j)
            with dve.Fori(1, full) as i:
                for j in range(BODY):
                    gate_step(i, j)
            for j in range(TOK_PAIRS - full * BODY):
                gate_step(full, j, TOK_PAIRS - full * BODY)
            for k in range(C_ONES + TOK_PAIRS // 2, NK):
                take_chunk(0, k, TOK_PAIRS)

            def v_step(n0, k0, j, split=True):
                if split:
                    dve.wait_ge(hi_done, n0 + (V0 + j + 1))
                    s = (V0 + j) % SPL
                    nc.vector.tensor_tensor(wlo[:, s, :], raw[:, j % RAW, :], whi[:, s, :], ALU.subtract).then_inc(lo_v_done, 1)
                if j % 2 == 0:
                    dve.wait_ge(ghi_done, k0 + (j // 2 + 1))
                    nc.vector.tensor_tensor(gate_lo[:, j // 2 % 2, :], W[:, k0 + j // 2, :],
                                            gate_hi[:, j // 2 % 2, :], ALU.subtract).then_inc(glo_done, 1)

            dve.wait_ge(used, V0)
            for j in range(BODY):
                v_step(0, 0, j, split=V0 + j >= POOL_END)
            with dve.Fori(1, 2 * NK // BODY) as i:
                for j in range(BODY):
                    v_step(i * BODY, i * CHUNKS_PER_BODY, j)
            for j in range(2 * NK // BODY * BODY, 2 * NK):
                v_step(0, 0, j)

            dve.wait_ge(x2_in, 16)
            dve.wait_ge(used, END)
            for tb in range(TB):
                nc.vector.tensor_tensor(x2_back[:, tb, :], ps[:, 4 * tb:4 * tb + 4, :].rearrange("p a b -> p (a b)"),
                                        x2_back[:, tb, :], ALU.add).then_inc(x3_ready, 1)
            variances(2, 10)
            inverse_root(5, 2, EPS)
            dve.wait_ge(gain_in[4], 16)
            for tb in range(TB):
                nc.vector.scalar_tensor_tensor(x2_back[:, tb, :], x2_back[:, tb, :], stats[:, 160 + tb:161 + tb],
                                               last_gain[:, :], ALU.mult, ALU.mult).then_inc(y_out, 1)

        @block.tensor
        def _(pe):
            def transposes(k):
                pe.wait_ge(normed if k != 2 else y_ready, {0: 2, 1: 4, 2: 1, 3: 6, 4: 8}[k])
                for b in range(8):
                    for c in range(2):
                        for tb in range(TB):
                            m = 2 * b + c
                            ins = nc.tensor.transpose(ps[:, b, (c * TB + tb) * P:(c * TB + tb + 1) * P],
                                                      Y[:, tb, m * P:(m + 1) * P], ident)
                    ins.then_inc(xT_ready, 1)

            def three(out_ap, sh, sl, mh, ml, start, stop):
                nc.tensor.matmul(out_ap, sh, mh, start=start, stop=False)
                nc.tensor.matmul(out_ap, sh, ml, start=False, stop=False)
                return nc.tensor.matmul(out_ap, sl, mh, start=False, stop=stop)

            def rows_piece(n, c0, width, last_chunk, banks):
                pe.wait_ge(lo_done, n + 1)
                s = n % SPL
                for tb in range(TB):
                    for c in range(PW // width):
                        m = c0 + c
                        t = slice(tb * P, (tb + 1) * P)
                        cols = slice(c * width, (c + 1) * width)
                        ins = three(ps[:, banks + tb, 0:width], xh[:, m, t], xl[:, m, t], whi[:, s, cols], wlo[:, s, cols],
                                    m == 0, m == last_chunk)
                ins.then_inc(used, 1)

            def cols_piece(n, c0, last_chunk, banks):
                pe.wait_ge(lo_done, n + 1)
                s = n % SPL
                for c in range(2):
                    for b in range(4):
                        m = c0 + c
                        cols = slice(c * 512 + b * P, c * 512 + (b + 1) * P)
                        ins = three(ps[:, banks + b, 0:T], whi[:, s, cols], wlo[:, s, cols], xh[:, m, :], xl[:, m, :],
                                    m == 0, m == last_chunk)
                ins.then_inc(used, 1)

            pe.wait_ge(ident_in, 16)
            transposes(0)
            pe.wait_ge(xl_ready, 8)
            for n in range(W_XK, W_XV):
                cols_piece(n, 2 * (n - W_XK), DC - 1, 0)
            for n in range(W_XV, W_IN):
                rows_piece(n, 2 * (n - W_XV), 512, DC - 1, 4)
            pe.wait_ge(tile_out, 2)
            transposes(1)
            pe.wait_ge(xl_ready, 16)

            def qk_transposes(g):
                if g == 0:
                    pe.wait_ge(roped_a, 4)
                    for k in range(KVH):
                        for tb in range(TB):
                            nc.tensor.transpose(ps[:, 6, (k * TB + tb) * P:(k * TB + tb + 1) * P],
                                                at(P_AT + (tb * KVH + k) * P, P), ident)
                else:
                    pe.wait_ge(qk_copied, 1)
                for c in range(4):
                    for tb in range(TB):
                        m = c * TB + tb
                        ins = nc.tensor.transpose(ps[:, (4 if g == 0 else 6) + m // 4, (m % 4) * P:(m % 4 + 1) * P],
                                                  H[:, tb, (4 * g + c) * P:(4 * g + c + 1) * P], ident)
                ins.then_inc(qk_T, 1)

            def head_scores(b):
                g, tb, h0, h1, w = BATCH[b]
                pe.wait_ge(qk_copied, 1 + g)
                if b:
                    pe.wait_ge(scores_read, b)
                for h in range(h0, h1):
                    lo = h % 2 * HD
                    col = (h - h0) // 2 * w
                    ins = nc.tensor.matmul(ps[:, 4 + h % 2, col:col + w],
                                           QAT[lo:lo + HD, h // 2, tb * P:(tb + 1) * P],
                                           KT[lo:lo + HD, g, 0:w], start=True, stop=True)
                ins.then_inc(scores, 1)

            def p_transposes(b):
                g, tb, h0, h1, w = BATCH[b]
                pe.wait_ge(exp_out, b + 1)
                pe.wait_ge(qk_copied, 2)
                if b:
                    pe.wait_ge(o_out, b)
                for m in range(8):
                    ins = nc.tensor.transpose(ps[:, 6 + m // 4, (m % 4) * P:(m % 4 + 1) * P], PR[:, m * P:(m + 1) * P],
                                              ident)
                ins.then_inc(p_T, 1)

            def head_outputs(b):
                g, tb, h0, h1, w = BATCH[b]
                pe.wait_ge(p_copied, b + 1)
                nk = w // P
                for k in range(h1 - h0):
                    for kc in range(nk):
                        q = k % 2 * ((h1 - h0) // 2) + k // 2
                        ins = nc.tensor.matmul(ps[:, 6, k * HD:(k + 1) * HD], PT[:, q * nk + kc, :],
                                               H[:, kc, VA + g * HD:VA + (g + 1) * HD], start=kc == 0, stop=kc == nk - 1)
                ins.then_inc(o_ready, 1)

            def r_transposes(r):
                pe.wait_ge(roped, 6)
                if r == 0:
                    pe.wait_ge(scores_read, len(BATCH))
                else:
                    pe.wait_ge(r_copied, r)
                for k, c0 in ((0, QR), (1, KR)):
                    for dc in range(2):
                        for tb in range(TB):
                            ins = nc.tensor.transpose(ps[:, 4 + k, (dc * TB + tb) * P:(dc * TB + tb + 1) * P],
                                                      H[:, tb, c0 + r * RD + dc * P:c0 + r * RD + (dc + 1) * P], ident)
                ins.then_inc(r_T, 1)

            def r_inner(r):
                pe.wait_ge(r_copied, r + 1)
                if r == 0:
                    pe.wait_ge(o_out, len(BATCH))
                else:
                    pe.wait_ge(ret_o_out, r)
                for tb in range(TB):
                    for dc in range(2):
                        ins = nc.tensor.matmul(ps[:, 6, tb * P:(tb + 1) * P], KRT[:, r % 2, dc, tb * P:(tb + 1) * P],
                                               QRT[:, r, dc, tb * P:(tb + 1) * P], start=dc == 0, stop=dc == 1)
                ins.then_inc(inner, 1)

            def r_state(r):
                pe.wait_ge(kz_ready, r + 1)
                pe.wait_ge(tile_out, 2 + 9)
                if r:
                    pe.wait_ge(ret_cross, r)
                for dc in range(2):
                    ins = nc.tensor.matmul(ps[:, 7, dc * RD:(dc + 1) * RD], KZ[:, r % 2, dc * P:(dc + 1) * P],
                                           H[:, 0, VR + r * RD:VR + (r + 1) * RD], start=True, stop=True)
                ins.then_inc(state, 1)

            def r_out(r):
                pe.wait_ge(inner_out, r + 1)
                pe.wait_ge(state_out, r + 1)
                for tb in range(TB):
                    nc.tensor.matmul(ps[:, 6, tb * RD:(tb + 1) * RD], IT[:, r, tb, :], H[:, tb, VR + r * RD:VR + (r + 1) * RD],
                                     start=True, stop=True)
                for dc in range(2):
                    ins = nc.tensor.matmul(ps[:, 7, 0:RD], QRT[:, r, dc, P:T], ST[:, r % 2, dc, :], start=dc == 0, stop=dc == 1)
                ins.then_inc(ret_o, 1)

            do = {"qk": qk_transposes, "s": head_scores, "pt": p_transposes, "o": head_outputs, "rt": r_transposes,
                  "ri": r_inner, "rs": r_state, "ro": r_out}
            n = W_IN
            for t, (c0, w) in enumerate(IN_TILES):
                if t >= 2:
                    pe.wait_ge(tile_out, 2 + t - 1)
                per = PW // w
                for j in range(DC // per):
                    rows_piece(n, j * per, w, DC - 1, 2 * (t % 2))
                    for what, k in PE_POINTS.get(n, ()):
                        do[what](k)
                    n += 1
            assert n == W_OUT
            for what, k in PE_LAST:
                do[what](k)
            pe.wait_ge(ret_cross, RH)
            transposes(2)
            pe.wait_ge(xl_ready, 24)
            for t in range(4):
                if t >= 2:
                    pe.wait_ge(tile_out, 13 + t - 1)
                for j in range(8):
                    rows_piece(W_OUT + 8 * t + j, 2 * j, 512, DC - 1, 2 * (t % 2))
            pe.wait_ge(tile_out, 17)
            transposes(3)
            pe.wait_ge(xl_ready, 32)
            for j in range(8):
                cols_piece(W_XQ + j, 2 * j, DC - 1, 0)
            pe.wait_ge(tile_out, 18)
            for h in range(XH):
                for tb in range(TB):
                    ins = nc.tensor.matmul(ps[:, 4 + h, tb * T:(tb + 1) * T], QXT[:, h, tb * P:(tb + 1) * P], KX[:, h, :],
                                           start=True, stop=True)
            ins.then_inc(x_scores, 1)
            pe.wait_ge(x_prob, 1)
            for h in range(XH):
                for mb in range(TB):
                    for tb in range(TB):
                        ins = nc.tensor.transpose(ps[:, h, mb * T + tb * P:mb * T + (tb + 1) * P],
                                                  PX[:, h * TB + tb, mb * P:(mb + 1) * P], ident)
            ins.then_inc(x_pT, 1)
            pe.wait_ge(x_pT_out, 1)
            for h in range(XH):
                for mb in range(TB):
                    ins = nc.tensor.matmul(ps[:, 4 + h, 0:T], VX[:, mb, h * XD:(h + 1) * XD], PXT[:, h, mb, :],
                                           start=mb == 0, stop=mb == 1)
            ins.then_inc(x_oT, 1)
            pe.wait_ge(xl_ready, 33)
            for t in range(4):
                if t >= 2:
                    pe.wait_ge(tile_out, 18 + t - 1)
                for j in range(2):
                    rows_piece(W_XO + 2 * t + j, 2 * j, 512, XH - 1, 2 * (t % 2))
            pe.wait_ge(tile_out, 22)
            transposes(4)
            pe.wait_ge(xl_ready, 41)
            for t in range(4):
                if t >= 2:
                    pe.wait_ge(tile_out, 22 + t - 1)
                for j in range(8):
                    cols_piece(W_PQ + 8 * t + j, 2 * j, DC - 1, 4 * (t % 2))
            pe.wait_ge(tile_out, 26)
            pe.wait_ge(keys_in, 16)
            for tb in range(TB):
                for hp in range(HP):
                    ins = nc.tensor.matmul(ps[:, 4 * tb + hp // 4, hp % 4 * NK:(hp % 4 + 1) * NK],
                                           QPT[:, hp, tb * P:(tb + 1) * P], SK[:, hp, :], start=True, stop=True)
                ins.then_inc(key_scores, 1)

            def u_piece(i, j):
                if j % 2 == 0 and not (isinstance(i, int) and i == 0 and j < 2 * ACT_BANKS):
                    pe.wait_ge(act_taken, i * CHUNKS_PER_BODY + (j // 2 - ACT_BANKS + 1))
                pe.wait_ge(lo_done, i * BODY + (U0 + j + 1))
                s = j % SPL
                for c in range(8):
                    m = j % 2 * 8 + c
                    cols = slice(c * P, (c + 1) * P)
                    ins = three(ps[:, j // 2 % ACT_BANKS, 0:T], whi[:, s, cols], wlo[:, s, cols], xh[:, m, :], xl[:, m, :],
                                m == 0, m == DC - 1)
                ins.then_inc(used, 1)

            def gate_products(i, j):
                pe.wait_ge(hot1, i * BODY + (j + 1))
                pe.wait_ge(hot2, i * BODY + (j + 1))
                if not (isinstance(i, int) and i == 0 and j < 2):
                    pe.wait_ge(gated, i * BODY + (j - 1))
                for m in range(2):
                    for part in range(3):
                        ins = nc.tensor.matmul(ps[:, 4 + j % 2, m * P:(m + 1) * P], hot1_rows[:, j % 2, m, part, :],
                                               hot2_row[:, m, :], start=part == 0, stop=part == 2)
                ins.then_inc(gate_mat, 1)

            pe.wait_ge(key_scores_out, 2)
            for j in range(BODY):
                u_piece(0, j)
            with pe.Fori(1, C_TABLES // CHUNKS_PER_BODY) as i:
                for j in range(BODY):
                    u_piece(i, j)
            pe.wait_ge(gates_ready, 1)
            CH = at(TK_AT + 256, 2, T)
            GE = at(TK_AT, T)
            for k in range(3):
                for tb in range(TB):
                    src = (CH[:, k, :] if k < 2 else GE)[:, tb * P:(tb + 1) * P]
                    ins = nc.tensor.transpose(ps[:, 4 + k // 2, (k % 2 * TB + tb) * P:(k % 2 * TB + tb + 1) * P], src, ident)
            ins.then_inc(table_T, 1)
            with pe.Fori(C_TABLES // CHUNKS_PER_BODY, C_GATE // CHUNKS_PER_BODY) as i:
                for j in range(BODY):
                    u_piece(i, j)
            first = C_GATE // CHUNKS_PER_BODY
            full = TOK_PAIRS // BODY
            for j in range(BODY):
                u_piece(first, j)
                gate_products(0, j)
            with pe.Fori(1, full) as i:
                for j in range(BODY):
                    u_piece(i + first, j)
                    gate_products(i, j)
            for j in range(2 * NK - (first + full) * BODY):
                u_piece(first + full, j)
                if full * BODY + j < TOK_PAIRS:
                    gate_products(full, j)

            def v_piece(n0, k0, j, first=False, last=False):
                if j % 2 == 0:
                    pe.wait_ge(glo_done, k0 + (j // 2 + 1))
                if isinstance(n0, int) and n0 + V0 + j < POOL_END:
                    pe.wait_ge(lo_done, V0 + j + 1)
                else:
                    pe.wait_ge(lo_v_done, n0 + (V0 - POOL_END + j + 1))
                s, g = (V0 + j) % SPL, j // 2 % 2
                for tb in range(TB):
                    for c in range(2):
                        t = slice(tb * P, (tb + 1) * P)
                        cols = slice(c * 512, (c + 1) * 512)
                        ins = three(ps[:, 4 * tb + 2 * (j % 2) + c, :], gate_hi[:, g, t], gate_lo[:, g, t], whi[:, s, cols],
                                    wlo[:, s, cols], first, last)
                ins.then_inc(used, 1)

            pe.wait_ge(gated, TOK_PAIRS)
            pe.wait_ge(act_taken, NK)
            for j in range(BODY):
                v_piece(0, 0, j, first=j < 2)
            with pe.Fori(1, 2 * NK // BODY) as i:
                for j in range(BODY):
                    v_piece(i * BODY, i * CHUNKS_PER_BODY, j)
            for j in range(2 * NK // BODY * BODY, 2 * NK):
                v_piece(0, 0, j, last=j >= 2 * NK - 2)


BATCH = [(g, tb, h0, h1, w) for g in range(KVH) for tb, h0, h1, w in
         ((0, 8 * g, 8 * g + 8, P), (1, 8 * g, 8 * g + 4, 2 * P), (1, 8 * g + 4, 8 * g + 8, 2 * P))]
TILE_END = []
for _c, _w in IN_TILES:
    TILE_END.append((TILE_END[-1] if TILE_END else W_IN) + DC * _w // PW)


def _half(t, h):
    return TILE_END[t] - 8 + 4 * h + 3


PE_POINTS = {_half(3, 0): [("qk", 0)], _half(3, 1): [("qk", 1), ("s", 0)]}
for _b in range(7):
    _steps = ([("o", _b - 1)] if _b else []) + ([("s", _b + 1)] if _b < 5 else []) + ([("pt", _b)] if _b < 6 else [])
    PE_POINTS[_half(4 + _b // 2, _b % 2)] = _steps
PE_POINTS[_half(7, 1)] = [("rt", 0)]
for _r, _at in enumerate((_half(8, 1), _half(9, 0), _half(9, 1), _half(10, 0))):
    PE_POINTS[_at] = ([("ro", _r - 1)] if _r else []) + [("ri", _r), ("rs", _r)] + ([("rt", _r + 1)] if _r < 3 else [])
PE_LAST = [("ro", 3)]

ACT_POINTS = {_half(4 + _b // 2, _b % 2): [_b] for _b in range(6)}

DVE_ORDER = [("tile", 0), ("tile", 1), ("tile", 2), ("rope_a", 0), ("qk", 0), ("tile", 3), ("qk", 1), ("sin", 0)]
for _b in range(7):
    if _b < 6:
        DVE_ORDER.append(("ssum", _b))
    if _b:
        DVE_ORDER.append(("o", _b - 1))
    if _b < 6:
        DVE_ORDER.append(("pt", _b))
    if _b < 5:
        DVE_ORDER.append(("sin", _b + 1))
    if _b in (1, 3):
        DVE_ORDER.append(("tile", 4 + _b // 2))
    if _b == 2:
        DVE_ORDER.append(("rope_r", QR))
    if _b == 5:
        DVE_ORDER.append(("tile", 6))
DVE_ORDER += [("rope_r", KR), ("kz", 0), ("tile", 7), ("rc", 0), ("tile", 8)]
for _r in range(4):
    DVE_ORDER += ([("cross", _r - 1)] if _r else []) + [("dec", _r), ("st", _r)] + \
                 ([("rc", _r + 1), ("kz", _r + 1)] if _r < 3 else [])
    if _r == 2:
        DVE_ORDER.append(("tile", 9))
DVE_ORDER += [("cross", 3), ("tile", 10)]


def _pieces(w, width):
    per = PW // width
    k = w.shape[0] // P // per
    return w.reshape(k, per, P, width).transpose(0, 2, 1, 3).reshape(k, P, PW)


def kernel(**inputs):
    import numpy as np
    import concourse.bacc as bacc
    from concourse.bass_utils import run_bass_kernel_spmd

    a = {k: np.asarray(v) for k, v in inputs.items()}

    def tiles(w):
        return [_pieces(w[:, c:c + 512], 512) for c in range(0, w.shape[1], 512)]

    w_in = a["w_in"][0]
    front = [_pieces(a["w_xk"][0], 512), _pieces(a["w_xv"][0], 512)]
    front += [_pieces(w_in[:, c:c + w], w) for c, w in IN_TILES]
    front += tiles(a["w_out"][0]) + tiles(a["w_xq"][0]) + tiles(a["w_xo"][0]) + tiles(a["w_peer_q"][0])
    u = a["peer_u"][0].reshape(NK, NK, 2, 8, P).transpose(1, 2, 4, 3, 0).reshape(2 * NK, P, PW)
    lg = np.log1p(-np.exp2(-5.0 - np.arange(RH)))
    i = np.arange(P)
    diff = i[None, :] - i[:, None]
    decay = np.where(diff[None] >= 0, np.exp(np.maximum(diff, 0)[None] * lg[:, None, None]), 0.0) * RD ** -0.5
    zeta = np.exp((P - 1 - i)[:, None] * lg[None, :]) * RD ** -0.5
    xi = np.exp((i + 1)[:, None] * lg[None, :])
    mask = np.stack([i[None, :] > i[:, None], i[None, :] <= i[:, None]], 1)
    theta = np.float32(10000.0)
    inv = np.concatenate([theta ** (-np.arange(0, d, 2, dtype=np.float32) / np.float32(d)) for d in (HD, RD)])
    arrays = {
        "x": a["x"], "mem": a["mem"], "pos": a["positions"].astype(np.int32).reshape(TB, P).T,
        "gains": np.stack([a["mem_norm_gain"][0], a["mix_norm_gain"][0], a["cross_norm_gain"][0],
                           a["ffn_norm_gain"][0], a["final_norm_gain"]]),
        "out_gains": np.concatenate([a["att_out_gain"][0], a["ret_out_gain"][0]])[None],
        "w_front": np.concatenate(front), "w_u": u, "w_v": a["peer_v"][0],
        "sub_keys": a["peer_sub_keys"][0].reshape(HP, NK, P).transpose(2, 0, 1).reshape(P, HP * NK),
        "sinks": a["att_sinks"].reshape(1, QH),
        "c_ident": np.eye(P, dtype=np.float32), "c_iota": np.tile(i.astype(np.float32), (P, 1)),
        "c_mask": np.where(mask, 0.0, -1e30).astype(np.float32).reshape(P, 2 * P),
        "c_decay": decay.astype(np.float32).transpose(1, 0, 2).reshape(P, RH * P),
        "c_zx": np.concatenate([zeta, xi], 1).astype(np.float32), "c_inv": inv.astype(np.float32)[None],
    }
    arrays = {k: np.ascontiguousarray(v) for k, v in arrays.items()}
    nc = bacc.Bacc("TRN2", target_bir_lowering=False, num_devices=1)
    args = [nc.dram_tensor(f"in_{k}", v.shape, mybir.dt.from_np(v.dtype), kind="ExternalInput").ap()
            for k, v in arrays.items()]
    x2_dram = nc.dram_tensor("x2_scratch", (T, D), F32, kind="Internal").ap()
    out = nc.dram_tensor("out_0", (1, T, D), F32, kind="ExternalOutput").ap()
    hymba_layer(nc, *args, x2_dram, out)
    r = run_bass_kernel_spmd(nc, [{f"in_{k}": v for k, v in arrays.items()}], core_ids=[0])
    return r.results[0]["out_0"]
```

```python
from contextlib import ExitStack

import concourse.bass as bass
from concourse import mybir

F32 = mybir.dt.float32
F32R = mybir.dt.float32r
BF16 = mybir.dt.bfloat16
I32 = mybir.dt.int32
U32 = mybir.dt.uint32
ALU = mybir.AluOpType
ACT = mybir.ActivationFunctionType
AX = mybir.AxisListType.X

P = 128
T = 256
TB = T // P
D = 2048
DC = D // P
EPS = 1e-6
GN_EPS = 1e-5
HD, QH, KVH = 64, 16, 2
RH, RD = 4, 256
XH, XD = 4, 128
PH, NK, TOPK = 8, 128, 16
HP = 2 * PH
QA, KA, VA = 0, 1024, 1152
QR, KR, VR, GR = 1280, 2304, 3328, 4352
IN_COLS = 5376

PW = 1024
RAW = 4
SPL = 3
BODY = 12
IN_TILES = [(0, 512), (512, 512), (1024, 256)] + [(QR + 512 * n, 512) for n in range(8)]
W_IN = 0
W_XK = W_IN + DC * IN_COLS // PW
W_OUT = W_XK + 8
W_XQ = W_OUT + 32
W_XV = W_XQ + 8
W_XO = W_XV + 8
W_PQ = W_XO + 8
FRONT = W_PQ + 32
U0 = FRONT
V0 = U0 + 2 * NK
END = V0 + 2 * NK
assert FRONT % BODY == 0
N_IN = len(IN_TILES)
N_XK = N_IN + 1
N_OUT = N_XK + 4
N_XQ = N_OUT + 1
N_XV = N_XQ + 1
N_XO = N_XV + 4
N_PQ = N_XO + 4
A_X, A_MEM, A_Y, A_X1, A_MEM2, A_O, A_X2, A_NORMED = 0, 8, 16, 24, 32, 40, 44, 52
T_Y, T_X1, T_X2 = 0, 8, 16
CHUNKS_PER_BODY = BODY // 2
C_TABLES, C_GATE = 54, 60
C_ONES = C_GATE - 2
TOK_PAIRS = T // 2
ACT_BANKS = 3
POOL_END = V0 + 8
assert POOL_END == V0 + BODY - RAW and POOL_END % BODY == 0 and CHUNKS_PER_BODY % ACT_BANKS == 0

BIG = NK * T
H_AT = 0
XT_AT = 4096
ANG_AT = 8192
Y_AT = TB * IN_COLS
GN_AT = Y_AT + TB * D
QAT_AT = GN_AT + D
KT_AT = QAT_AT + 8 * T
P_AT = KT_AT + 2 * T
PT_AT = P_AT + 1024
KX_AT = PT_AT + 1024
VX_AT = KX_AT + 1024
CS_AT = VX_AT + 1024
DEC_AT = CS_AT + 2 * TB * 160
MASK_AT = DEC_AT + 512
ZX_AT = MASK_AT + 256
INV_AT = ZX_AT + 8
QRT_AT = INV_AT + 160
KRT_AT = QRT_AT + RH * 512
IT_AT = KRT_AT + 2 * 512
ST_AT = IT_AT + RH * 256
KZ_AT = ST_AT + 2 * 512
SMALL_AT = KZ_AT + 2 * 256
IDENT_AT = BIG - P
IOTA_AT = IDENT_AT - P
GAIN_AT = IOTA_AT - 5 * DC
ONES_AT = SMALL_AT + 64
DIAG_AT = ONES_AT + P
RB_AT = DIAG_AT + T
BN_AT = RB_AT + T
assert BN_AT + 64 <= GAIN_AT
MEMT_AT = QAT_AT
MEM_AT = QRT_AT
assert MEMT_AT + DC * T <= KX_AT
X1_AT, QXT_AT, TMP_AT = 0, 8192, 8192
XR_AT = QRT_AT
PX_AT, PXT_AT = 4096, 6144
C_FREE = 76
QPT_AT = C_FREE * T
SK_AT = QPT_AT + HP * T
S_AT = SK_AT + HP * P
TK_AT = S_AT + TB * HP * P

SS, VAR, ROOT, R = 0, 10, 20, 30
N_X, N_MEM, N_X1, N_X2, N_LAST = 0, 2, 4, 6, 8
A_SS, A_VAR, A_ROOT, A_R = 40, 72, 104, 136
R_VAR, R_ROOT, R_R = 168, 176, 184
MX, ES, SD, RV = 192, 200, 208, 216
CM, NM, SM, CR, SC = 40, 48, 56, 64, 72
LAST_SS = 76
TOP = 80

C1 = 6.28125
C2 = 0.00193500518798828125
C3 = 3.0199159819567e-07
PI = 3.14159250


def hymba_layer(nc, x, mem, x_t, mem_t, pos, gain_cols, last_gain_d, w_front, w_u, w_v, sub_keys, sinks,
                ident_d, iota_d, mask_d, decay_d, zx_d, inv_d, x2_dram, out):
    ctx = ExitStack()
    with ctx:
        def sb(name, shape, dt=F32):
            return ctx.enter_context(nc.sbuf_tensor(name, shape, dt))

        def sem(name):
            return ctx.enter_context(nc.semaphore(name))

        big = sb("big", [P, BIG])
        raw = sb("raw", [P, RAW, PW])
        whi = sb("whi", [P, SPL, PW], F32R)
        wlo = sb("wlo", [P, SPL, PW], F32R)
        iota = sb("iota", [P, P], BF16)
        stats = sb("stats", [P, 240])
        of_u = ExitStack()
        i1_table = of_u.enter_context(nc.sbuf_tensor("i1_table", [P, T], F32))
        hot2_row = of_u.enter_context(nc.sbuf_tensor("hot2_row", [P, 2, P], BF16))
        hot1_rows = of_u.enter_context(nc.sbuf_tensor("hot1_rows", [P, 2, 2, 3, P], BF16))
        of_u.close()
        gate_hi = sb("gate_hi", [P, 2, T], F32R)
        gate_lo = sb("gate_lo", [P, 2, T], F32R)
        sb("rest_of_gates", [P, 128])
        first = ExitStack()
        xh = first.enter_context(nc.sbuf_tensor("xh", [P, DC, T], F32R))
        xl = first.enter_context(nc.sbuf_tensor("xl", [P, DC, T], F32R))
        first.close()
        x2_back = sb("x2_back", [P, TB, D])
        last_gain = sb("last_gain", [P, D])
        ps = ctx.enter_context(nc.psum_tensor("ps", [P, 8, 512], F32))
        i2_table = ps[:, 3, T:2 * T]
        parts_table = ps[:, 6:8, :].rearrange("p a b -> p (a b)")[:, 0:3 * T].rearrange("p (a b) -> p a b", a=3)

        def at(off, *dims):
            n = 1
            for d in dims:
                n *= d
            v = big[:, off:off + n]
            if len(dims) == 2:
                v = v.rearrange("p (a b) -> p a b", a=dims[0])
            if len(dims) == 3:
                v = v.rearrange("p (a b c) -> p a b c", a=dims[0], b=dims[1])
            if len(dims) == 4:
                v = v.rearrange("p (a b c d) -> p a b c d", a=dims[0], b=dims[1], c=dims[2])
            return v

        ident = at(IDENT_AT, P)
        IOTA_F32 = at(IOTA_AT, P)
        H = at(H_AT, TB, IN_COLS)
        Y = at(Y_AT, TB, D)
        QAT = at(QAT_AT, 8, T)
        KT = at(KT_AT, KVH, T)
        PR = at(P_AT, 1024)
        PT = at(PT_AT, 8, P)
        KX = at(KX_AT, XH, T)
        VX = at(VX_AT, TB, XH * XD)
        CS = at(CS_AT, 2, TB, 160)
        DEC = at(DEC_AT, RH, P)
        MASK = at(MASK_AT, 2, P)
        ZX = at(ZX_AT, 2, RH)
        INV = at(INV_AT, 160)
        QRT = at(QRT_AT, RH, 2, T)
        KRT = at(KRT_AT, 2, 2, T)
        IT = at(IT_AT, RH, TB, P)
        ST = at(ST_AT, 2, 2, RD)
        KZ = at(KZ_AT, 2, RD)
        SINK = at(SMALL_AT, QH)
        POSI = at(SMALL_AT + 16, TB).bitcast(I32)
        POSF = at(SMALL_AT + 18, TB)
        ANG = at(ANG_AT, 3, TB * 160)
        TURN = at(ANG_AT + 1280, 2, TB * 160).bitcast(I32)
        XT = at(XT_AT, DC, T)
        MEMT = at(MEMT_AT, DC, T)
        GAIN = at(GAIN_AT, 5, DC)
        ONES = at(ONES_AT, P)
        DIAG = at(DIAG_AT, TB, P)
        RB = at(RB_AT, T)
        BN = at(BN_AT, TB * RH, 6)
        MV = at(BN_AT + 48, TB * RH, 2)
        TMP = at(TMP_AT, DC, T)
        FINAL = at(0, TB, D)
        X1 = at(X1_AT, TB, D)
        XR = at(XR_AT, TB, D)
        QXT = at(QXT_AT, XH, T)
        PX = at(PX_AT, XH * TB, T)
        PXT = at(PXT_AT, XH, TB, T)
        QPT = at(QPT_AT, HP, T)
        SK = at(SK_AT, HP, NK)
        S = at(S_AT, TB * PH, 2 * NK)
        W = at(0, NK, T)

        raw_in = [sem(f"raw_in{i}") for i in range(RAW)]
        hi_done = sem("hi_done")
        lo_done = sem("lo_done")
        lo_v_done = sem("lo_v_done")
        used = sem("used")
        ident_in, gain_in = sem("ident_in"), sem("gain_in")
        xr_in = [sem(f"xr_in{i}") for i in range(TB)]
        x_in, mem_in = [sem(f"x_in{i}") for i in range(TB)], [sem(f"mem_in{i}") for i in range(TB)]
        xT_in, memT_in = [sem(f"xT_in{i}") for i in range(4)], [sem(f"memT_in{i}") for i in range(2)]
        const_in, keys_in, last_gain_in = sem("const_in"), sem("keys_in"), sem("last_gain_in")
        x2_out, x2_in, out_done = sem("x2_out"), sem("x2_in"), sem("out_done")
        squares, var_ready, root_ready = sem("squares"), sem("var_ready"), sem("root_ready")
        diag_ready, rb_ready, rb_out, rescaled = sem("diag_ready"), sem("rb_ready"), sem("rb_out"), sem("rescaled")
        xT_ready, xh_ready, xl_ready = sem("xT_ready"), sem("xh_ready"), sem("xl_ready")
        angles, sincos = sem("angles"), sem("sincos")
        tile_out = sem("tile_out")
        roped_a, qk_T, qk_copied = sem("roped_a"), sem("qk_T"), sem("qk_copied")
        scores, scores_read, exp_in, exp_out = sem("scores"), sem("scores_read"), sem("exp_in"), sem("exp_out")
        p_T, p_copied, o_ready, o_out = sem("p_T"), sem("p_copied"), sem("o_ready"), sem("o_out")
        roped, r_T, r_copied, inner, inner_out = sem("roped"), sem("r_T"), sem("r_copied"), sem("inner"), sem("inner_out")
        kz_ready, state, state_out = sem("kz_ready"), sem("state"), sem("state_out")
        ret_o, ret_o_out, ret_cross = sem("ret_o"), sem("ret_o_out"), sem("ret_cross")
        gate_ready, y_ready = sem("gate_ready"), sem("y_ready")
        x_scores, x_max, x_exp, x_prob, x_pT, x_pT_out, x_oT = (sem("x_scores"), sem("x_max"), sem("x_exp"), sem("x_prob"),
                                                               sem("x_pT"), sem("x_pT_out"), sem("x_oT"))
        x3_ready = sem("x3_ready")
        key_scores, key_scores_out = sem("key_scores"), sem("key_scores_out")
        topk, top_ready, top_exp, gates_ready, table_T = (sem("topk"), sem("top_ready"), sem("top_exp"),
                                                          sem("gates_ready"), sem("table_T"))
        gelu_done, act_taken = sem("gelu_done"), sem("act_taken")
        hot1, hot2, gate_mat, gated = sem("hot1"), sem("hot2"), sem("gate_mat"), sem("gated")
        ghi_done, glo_done = sem("ghi_done"), sem("glo_done")
        dve_step = sem("dve_step")
        rows_done, gained_right, last_r = sem("rows_done"), sem("gained_right"), sem("last_r")
        y_out = [sem(f"y_out{i}") for i in range(2)]

        def act_source(first_count, m):
            if first_count == A_X:
                return XT[:, m, :]
            if first_count in (A_MEM, A_MEM2):
                return MEMT[:, m, :]
            if first_count == A_NORMED:
                return TMP[:, m, :]
            return ps[:, pair_bank(first_count, m // 2), m % 2 * T:(m % 2 + 1) * T]

        gain_of = {A_X: 0, A_MEM: 1, A_MEM2: 1, A_Y: 2, A_X1: 3, A_X2: 4}
        freed_by = {A_MEM: W_XK - 8, A_Y: W_XK, A_X1: W_XQ - 8, A_MEM2: W_XQ, A_X2: W_PQ - 8, A_NORMED: U0 - 8}

        block = ctx.enter_context(nc.Block())

        @block.sync
        def _(sp):
            def load(n0, j, source, split=lo_done):
                sp.wait_ge(split, n0 + (j - RAW + 1))
                sp.dma_start(raw[:, j % RAW, :], source).then_inc(raw_in[j % RAW], 16)

            for j in range(RAW):
                sp.dma_start(raw[:, j, :], w_front[j]).then_inc(raw_in[j], 16)
            constants = ((IOTA_F32, iota_d), (POSI, pos), (INV, inv_d.partition_broadcast(P)),
                         (MASK, mask_d.rearrange("p (a b) -> p a b", a=2)), (SINK, sinks.partition_broadcast(P)),
                         (DEC, decay_d.rearrange("p (a b) -> p a b", a=RH)), (ZX, zx_d.rearrange("p (a b) -> p a b", a=2)))
            for j in range(RAW, BODY):
                load(0, j, w_front[j])
                if j - RAW < len(constants):
                    dst, src = constants[j - RAW]
                    sp.dma_start(dst, src).then_inc(const_in, 16)
            with sp.Fori(1, FRONT // BODY) as i:
                for j in range(BODY):
                    load(i * BODY, j, w_front[i * BODY + j])
            with sp.Fori(0, 2 * NK // BODY) as i:
                for j in range(BODY):
                    load(i * BODY + U0, j, w_u[i * BODY + j])
            rest = 2 * NK // BODY * BODY
            for j in range(rest, 2 * NK):
                load(U0, j, w_u[j])
            for j in range(BODY):
                load(V0, j, w_v[j])
            with sp.Fori(1, 2 * NK // BODY) as i:
                for j in range(BODY):
                    load(i * BODY + (V0 - POOL_END), j, w_v[i * BODY + j], lo_v_done)
            for j in range(rest, 2 * NK):
                load(V0 - POOL_END, j, w_v[j], lo_v_done)
            for tb in range(TB):
                for half in (0, 1):
                    sp.wait_ge(y_out[half], tb + 1)
                    cols = slice(half * 1024, (half + 1) * 1024)
                    sp.dma_start(out[0, tb * P:(tb + 1) * P, cols], x2_back[:, tb, cols]).then_inc(out_done, 16)
            sp.wait_ge(out_done, 64)

        @block.gpsimd
        def _(pool):
            def rest_of(n0, j):
                pool.wait_ge(hi_done, n0 + (j + 1))
                nc.gpsimd.tensor_tensor(wlo[:, j % SPL, :], raw[:, j % RAW, :], whi[:, j % SPL, :],
                                        ALU.subtract).then_inc(lo_done, 1)

            with pool.Fori(0, POOL_END // BODY) as i:
                for j in range(BODY):
                    rest_of(i * BODY, j)

            pool.wait_ge(last_gain_in, 16)
            pool.wait_ge(glo_done, NK)
            for tb in range(TB):
                pool.wait_ge(x3_ready, 2 * tb + 2)
                nc.gpsimd.tensor_tensor(FINAL[:, tb, 1024:D], x2_back[:, tb, 1024:D], last_gain[:, 1024:D],
                                        ALU.mult).then_inc(gained_right, 1)

        @block.scalar
        def _(act):
            steps = [0]

            act.dma_start(GAIN, gain_cols.rearrange("p (a b) -> p a b", a=5)).then_inc(gain_in, 16)
            for q in range(4):
                act.dma_start(XT[:, 4 * q:4 * q + 4, :], x_t[:, 4 * q:4 * q + 4, :]).then_inc(xT_in[q], 16)

            def load_rows(k):
                tb, cols = k // 2, slice(k % 2 * 1024, (k % 2 + 1) * 1024)
                act.dma_start(Y[:, tb, cols], x[0, tb * P:(tb + 1) * P, cols]).then_inc(x_in[tb], 16)

            def load_memory_rows(k):
                tb, cols = k // 2, slice(k % 2 * 1024, (k % 2 + 1) * 1024)
                act.dma_start(at(MEM_AT, TB, D)[:, tb, cols], mem[0, tb * P:(tb + 1) * P, cols]).then_inc(mem_in[tb], 16)

            def load_ident(_):
                act.dma_start(ident, ident_d).then_inc(ident_in, 16)

            def square_sum(src, col, unread):
                steps[0] += 1
                nc.scalar.activation(unread, src, ACT.Square, accum_out=stats[:, SS + col:SS + col + 1]).then_inc(squares, 1)
                act.wait_ge(squares, steps[0])

            def root(n, var, to, cols):
                act.wait_ge(var_ready, n)
                nc.scalar.activation(stats[:, to:to + cols], stats[:, var:var + cols], ACT.Sqrt).then_inc(root_ready, 1)

            def high(j, n0=0):
                act.wait_ge(raw_in[j % RAW], (n0 + (j // RAW * RAW + RAW)) * (16 // RAW))
                if not (isinstance(n0, int) and n0 + j < SPL):
                    act.wait_ge(used, n0 + (j - SPL + 1))
                nc.scalar.activation(whi[:, j % SPL, :], raw[:, j % RAW, :], ACT.Copy).then_inc(hi_done, 1)

            def split_high(v, b):
                if v == A_X:
                    act.wait_ge(gain_in, 16)
                    act.wait_ge(xT_in[b // 2], 16)
                else:
                    act.wait_ge(used, freed_by[v] + b + 1)
                if v == A_MEM:
                    act.wait_ge(memT_in[b // 4], 16)
                elif v == A_NORMED:
                    act.wait_ge(rescaled, b + 1)
                elif v in (A_Y, A_X1, A_X2):
                    act.wait_ge(xT_ready, {A_Y: T_Y, A_X1: T_X1, A_X2: T_X2}[v] + b + 1)
                for m in (2 * b, 2 * b + 1):
                    g = 1.0 if v == A_NORMED else GAIN[:, gain_of[v], m:m + 1]
                    ins = nc.scalar.activation(xh[:, m, :], act_source(v, m), ACT.Copy, scale=g)
                ins.then_inc(xh_ready, 1)

            def split_heads(h):
                act.wait_ge(x_oT, h + 1)
                nc.scalar.activation(xh[:, DC - XH + h, :], ps[:, h, 0:T], ACT.Copy).then_inc(xh_ready, 1)

            def exps(b):
                act.wait_ge(exp_in, b + 1)
                n, k = BATCH[b][3] - BATCH[b][2], BATCH[b][4]
                nc.scalar.activation(PR[:, 0:n * k], PR[:, 0:n * k], ACT.Exp)
                nc.scalar.activation(stats[:, ES:ES + n], stats[:, SD:SD + n], ACT.Exp).then_inc(exp_out, 1)

            def square_x(tb):
                act.wait_ge(x_in[tb], 32)
                square_sum(Y[:, tb, :], N_X + tb, at(QAT_AT, D))

            def square_mem(tb):
                act.wait_ge(mem_in[tb], 32)
                square_sum(at(MEM_AT, TB, D)[:, tb, :], N_MEM + tb, at(QAT_AT, D))

            def square_x1(tb):
                act.wait_ge(tile_out, N_OUT)
                square_sum(X1[:, tb, :], N_X1 + tb, at(Y_AT, D))

            def square_x2(tb):
                act.wait_ge(tile_out, N_XO)
                square_sum(X1[:, tb, :], N_X2 + tb, at(Y_AT, D))

            def sines(_):
                act.wait_ge(angles, 1)
                nc.scalar.activation(CS, ANG[:, 0:2, :].rearrange("p a (b c) -> p a b c", b=TB), ACT.Sin).then_inc(sincos, 1)

            def load_memory(h):
                act.wait_ge(o_out, len(BATCH))
                act.dma_start(MEMT[:, 8 * h:8 * h + 8, :], mem_t[:, 8 * h:8 * h + 8, :]).then_inc(memT_in[h], 16)

            def gates(tb):
                act.wait_ge(tile_out, N_IN)
                nc.scalar.activation(H[:, tb, GR:GR + 1024], H[:, tb, GR:GR + 1024], ACT.Silu).then_inc(gate_ready, 1)

            def load_x(tb):
                act.wait_ge(ret_cross, RH)
                act.dma_start(XR[:, tb, :], x[0, tb * P:(tb + 1) * P, :]).then_inc(xr_in[tb], 16)

            def load_keys(_):
                act.wait_ge(tile_out, N_OUT)
                act.dma_start(SK, sub_keys.rearrange("p (a b) -> p a b", a=HP)).then_inc(keys_in, 16)

            def cross_exps(_):
                act.wait_ge(x_max, 1)
                for h in range(XH):
                    for tb in range(TB):
                        k = h * TB + tb
                        ins = nc.scalar.activation(PX[:, k, :], ps[:, 4 + h, tb * T:(tb + 1) * T], ACT.Exp,
                                                   bias=stats[:, NM + k:NM + k + 1], scale=stats[:, SC + tb:SC + tb + 1],
                                                   accum_out=stats[:, SM + k:SM + k + 1])
                ins.then_inc(x_exp, 1)

            def store_x2(tb):
                act.wait_ge(tile_out, N_XO)
                act.dma_start(x2_dram[tb * P:(tb + 1) * P, :], X1[:, tb, :]).then_inc(x2_out, 16)

            do = {"x": lambda b: split_high(A_X, b), "mem": lambda b: split_high(A_MEM, b),
                  "y": lambda b: split_high(A_Y, b), "x1": lambda b: split_high(A_X1, b),
                  "mem2": lambda b: split_high(A_MEM2, b), "x2": lambda b: split_high(A_X2, b),
                  "normed": lambda b: split_high(A_NORMED, b), "o": split_heads, "exp": exps,
                  "square_x": square_x, "square_mem": square_mem, "square_x1": square_x1, "square_x2": square_x2,
                  "root_x": lambda _: root(1, VAR + N_X, ROOT + N_X, 2),
                  "root_mem": lambda _: root(2, VAR + N_MEM, ROOT + N_MEM, 2),
                  "root_att": lambda _: root(3, A_VAR, A_ROOT, 32), "root_ret": lambda _: root(4, R_VAR, R_ROOT, 8),
                  "root_x1": lambda _: root(5, VAR + N_X1, ROOT + N_X1, 2),
                  "root_x2": lambda _: root(6, VAR + N_X2, ROOT + N_X2, 2),
                  "sines": sines, "load_rows": load_rows, "load_ident": load_ident, "load_memory_rows": load_memory_rows,
                  "load_memory": load_memory, "gates": gates, "load_x": load_x,
                  "load_keys": load_keys, "cross_exps": cross_exps, "store_x2": store_x2}
            for j in range(U0):
                high(j)
                for what, k in ACT_POINTS.get(j, ()):
                    do[what](k)

            def gelu(k0, c):
                nc.scalar.activation(W[:, k0 + c, :], ps[:, c % ACT_BANKS, 0:T], ACT.Gelu).then_inc(act_taken, 1)

            def gelu_in_place(c):
                a = ps[:, c % ACT_BANKS, 0:T]
                nc.scalar.activation(a, a, ACT.Gelu).then_inc(gelu_done, 1)

            for j in range(BODY):
                high(j, U0)
                for what, k in ACT_POINTS.get(U0 + j, ()):
                    do[what](k)
                if j == 4:
                    act.wait_ge(x2_out, 32)
                if j % 2 == 0 and j >= 4:
                    gelu(0, j // 2 - 2)

            def body(i):
                for j in range(BODY):
                    high(j, i * BODY + U0)
                    if j % 2 == 0:
                        gelu(i * CHUNKS_PER_BODY - ACT_BANKS, j // 2 - 2 + ACT_BANKS)

            with act.Fori(1, C_TABLES // CHUNKS_PER_BODY) as i:
                body(i)
            act.wait_ge(top_ready, 1)
            GE = at(TK_AT, TB * PH, TOPK)
            nc.scalar.activation(GE, GE, ACT.Exp).then_inc(top_exp, 1)
            with act.Fori(C_TABLES // CHUNKS_PER_BODY, C_GATE // CHUNKS_PER_BODY) as i:
                body(i)
            with act.Fori(C_GATE // CHUNKS_PER_BODY, NK // CHUNKS_PER_BODY) as i:
                for j in range(BODY):
                    high(j, i * BODY + U0)
                    if j % 2 == 0:
                        gelu_in_place(j // 2 - 2 + ACT_BANKS)
            for j in range(NK // CHUNKS_PER_BODY * BODY, 2 * NK):
                high(j, U0)
                if j % 2 == 0:
                    gelu_in_place(j // 2 - 2)

            def high_v(n0, j):
                act.wait_ge(raw_in[j % RAW], (n0 + (j // RAW * RAW + RAW + V0 // RAW * RAW)) * (16 // RAW))
                act.wait_ge(used, n0 + (V0 + j - SPL + 1))
                nc.scalar.activation(whi[:, (V0 + j) % SPL, :], raw[:, j % RAW, :], ACT.Copy).then_inc(hi_done, 1)

            def gated_high(k0, k):
                nc.scalar.activation(gate_hi[:, k % 2, :], W[:, k0 + k, :], ACT.Copy).then_inc(ghi_done, 1)

            assert V0 % RAW == 0
            high_v(0, 0)
            gelu_in_place(NK - 2)
            act.wait_ge(gated, TOK_PAIRS)
            gated_high(0, 0)
            gated_high(0, 1)
            high_v(0, 1)
            act.wait_ge(used, V0)
            gelu_in_place(NK - 1)
            high_v(0, 2)
            for j in range(3, BODY):
                high_v(0, j)
                if j == 4:
                    act.wait_ge(act_taken, NK)
                if j in (5, 8):
                    tb = j // 8
                    act.dma_start(x2_back[:, tb, :], x2_dram[tb * P:(tb + 1) * P, :]).then_inc(x2_in, 16)
                if j == 11:
                    act.dma_start(last_gain[:, :], last_gain_d.partition_broadcast(P)).then_inc(last_gain_in, 16)
                if j % 2 == 0:
                    gated_high(0, j // 2)
            with act.Fori(1, 2 * NK // BODY) as i:
                for j in range(BODY):
                    high_v(i * BODY, j)
                    if j % 2 == 0:
                        gated_high(i * CHUNKS_PER_BODY, j // 2)
            for j in range(2 * NK // BODY * BODY, 2 * NK):
                high_v(0, j)
                if j % 2 == 0:
                    gated_high(0, j // 2)
            act.wait_ge(glo_done, NK)
            unread = at(2 * TB * D, 1024)
            for tb in range(TB):
                for half in range(2):
                    k = 2 * tb + half
                    act.wait_ge(x3_ready, k + 1)
                    nc.scalar.activation(unread, x2_back[:, tb, half * 1024:(half + 1) * 1024], ACT.Square,
                                         accum_out=stats[:, LAST_SS + k:LAST_SS + k + 1]).then_inc(squares, 1)
                    act.wait_ge(squares, 8 + k + 1)
                root(7 + tb, VAR + N_LAST + tb, ROOT + N_LAST + tb, 1)
            for tb in range(TB):
                act.wait_ge(last_r, tb + 1)
                act.wait_ge(gained_right, tb + 1)
                nc.scalar.activation(x2_back[:, tb, 1024:D], FINAL[:, tb, 1024:D], ACT.Copy,
                                     scale=stats[:, R + N_LAST + tb:R + N_LAST + tb + 1]).then_inc(y_out[1], 1)

        @block.vector
        def _(dve):
            n = [0]

            def step(ins):
                n[0] += 1
                ins.then_inc(dve_step, 1)
                dve.wait_ge(dve_step, n[0])

            def inverse_root(count, var, rt, to, cols, ready=None):
                v, t, r = stats[:, var:var + cols], stats[:, rt:rt + cols], stats[:, to:to + cols]
                dve.wait_ge(root_ready, count)
                step(nc.vector.reciprocal(r, t))
                step(nc.vector.tensor_tensor(t, r, r, ALU.mult))
                step(nc.vector.tensor_tensor(t, t, v, ALU.mult))
                step(nc.vector.tensor_scalar(t, t, -0.5, 1.5, ALU.mult, ALU.add))
                ins = nc.vector.tensor_tensor(r, r, t, ALU.mult)
                if ready is None:
                    step(ins)
                else:
                    ins.then_inc(ready, 1)

            def variances(which):
                dve.wait_ge(squares, which + 2)
                nc.vector.tensor_scalar(stats[:, VAR + which:VAR + which + 2], stats[:, SS + which:SS + which + 2], 1.0 / D, EPS,
                                        ALU.mult, ALU.add).then_inc(var_ready, 1)

            def inverse_rms(count, which):
                inverse_root(count, VAR + which, ROOT + which, R + which, 2)

            def split_low(v, b):
                dve.wait_ge(xh_ready, v + b + 1)
                for m in (2 * b, 2 * b + 1):
                    if v == A_NORMED:
                        ins = nc.vector.tensor_tensor(xl[:, m, :], TMP[:, m, :], xh[:, m, :], ALU.subtract)
                    else:
                        ins = nc.vector.scalar_tensor_tensor(xl[:, m, :], act_source(v, m), GAIN[:, gain_of[v], m:m + 1],
                                                             xh[:, m, :], ALU.mult, ALU.subtract)
                ins.then_inc(xl_ready, 1)

            def diagonal(which):
                for tb in range(TB):
                    ins = nc.vector.tensor_scalar(DIAG[:, tb, :], ident, stats[:, R + which + tb:R + which + tb + 1], None, ALU.mult)
                ins.then_inc(diag_ready, 1)

            def inverse_by_token(count, bank):
                dve.wait_ge(rb_ready, count)
                nc.vector.tensor_copy(RB, ps[:, bank, 0:T]).then_inc(rb_out, 1)
                dve.wait_ge(rb_out, count)

            dve.wait_ge(gain_in, 16)
            for b in range(8):
                split_low(A_X, b)
            variances(N_X)
            inverse_rms(1, N_X)
            dve.wait_ge(const_in, 7 * 16)
            step(nc.vector.tensor_copy(iota[:, :], IOTA_F32))
            TF = at(ANG_AT + 1920, 2, TB * 160)
            step(nc.vector.tensor_copy(POSF, POSI))
            for tb in range(TB):
                step(nc.vector.tensor_scalar(ANG[:, 2, tb * 160:(tb + 1) * 160], INV, POSF[:, tb:tb + 1], None, ALU.mult))
            for k, shift in ((0, 0.0), (1, 0.25)):
                step(nc.vector.tensor_scalar(TF[:, k, :], ANG[:, 2, :], 0.15915494309189535, shift, ALU.mult, ALU.add))
                step(nc.vector.tensor_copy(TURN[:, k, :], TF[:, k, :]))
                step(nc.vector.tensor_copy(TF[:, k, :], TURN[:, k, :]))
                step(nc.vector.scalar_tensor_tensor(ANG[:, k, :], TF[:, k, :], -C1, ANG[:, 2, :], ALU.mult, ALU.add))
                step(nc.vector.scalar_tensor_tensor(ANG[:, k, :], TF[:, k, :], -C2, ANG[:, k, :], ALU.mult, ALU.add))
                step(nc.vector.scalar_tensor_tensor(ANG[:, k, :], TF[:, k, :], -C3, ANG[:, k, :], ALU.mult, ALU.add))
                if k:
                    step(nc.vector.tensor_scalar(ANG[:, k, :], ANG[:, k, :], PI / 2, None, ALU.add))
            nc.vector.tensor_scalar(ANG[:, 0:2, :], ANG[:, 0:2, :], PI, -PI, ALU.min, ALU.max).then_inc(angles, 1)
            variances(N_MEM)
            inverse_rms(2, N_MEM)
            nc.vector.memset(ONES, 1.0)
            dve.wait_ge(ident_in, 16)
            diagonal(N_MEM)

            def in_tile(t):
                c0, w = IN_TILES[t]
                dve.wait_ge(used, TILE_END[t])
                for tb in range(TB):
                    ins = nc.vector.tensor_scalar(H[:, tb, c0:c0 + w], ps[:, 2 * (t % 2) + tb, 0:w],
                                                  stats[:, R + N_X + tb:R + N_X + tb + 1], None, ALU.mult)
                ins.then_inc(tile_out, 1)
                dve.wait_ge(tile_out, 1 + t)

            ropes = [0]

            def rope(tb, c0, heads, half, tab):
                v = H[:, tb, c0:c0 + heads * 2 * half].rearrange("p (n two f) -> p n two f", two=2, f=half)
                x1, x2 = v[:, :, 0, :], v[:, :, 1, :]
                m = heads * half
                t = [at(GN_AT + 576 * k, heads, half) if m > 512 else at(GN_AT + 512 * k, heads, half) for k in range(3)]
                sin, cos = (CS[:, k, tb, tab:tab + half].unsqueeze(1).broadcast_to([P, heads, half]) for k in range(2))
                nc.vector.tensor_tensor(t[0], x1, cos, ALU.mult)
                nc.vector.tensor_tensor(t[1], x2, sin, ALU.mult)
                step(nc.vector.tensor_tensor(t[2], x1, sin, ALU.mult))
                step(nc.vector.tensor_tensor(x1, t[0], t[1], ALU.subtract))
                step(nc.vector.tensor_tensor(t[0], x2, cos, ALU.mult))
                nc.vector.tensor_tensor(x2, t[0], t[2], ALU.add).then_inc(roped, 1)
                ropes[0] += 1
                dve.wait_ge(roped, ropes[0])

            def rope_a(_):
                dve.wait_ge(sincos, 1)
                for tb in range(TB):
                    rope(tb, QA, QH + KVH, HD // 2, 0)
                for tb in range(TB):
                    for g in range(KVH):
                        src = H[:, tb, KA + g * HD:KA + (g + 1) * HD].unsqueeze(1).broadcast_to([P, 2, HD])
                        nc.vector.tensor_copy(at(P_AT + (tb * KVH + g) * P, 2, HD), src).then_inc(roped_a, 1)

            def qk_copies(g):
                dve.wait_ge(qk_T, g + 1)
                b = 4 if g == 0 else 6
                if g == 0:
                    nc.vector.tensor_copy(KT, ps[:, 6, :].rearrange("p (a b) -> p a b", a=2))
                nc.vector.tensor_copy(QAT[:, 4 * g:4 * g + 4, :],
                                      ps[:, b:b + 2, :].rearrange("p a (b c) -> p (a b) c", b=2)).then_inc(qk_copied, 1)

            def softmax_in(b):
                g, tb, h0, h1, w = BATCH[b]
                m = h1 - h0
                pr = PR[:, 0:m * w].rearrange("p (a b) -> p a b", a=m)
                src = ps[:, 4:6, :].rearrange("p a b -> p (a b)")[:, 0:m * w].rearrange("p (a b) -> p a b", a=m)
                mask = MASK.rearrange("p a b -> p (a b)")[:, 2 * P - w:2 * P].unsqueeze(1).broadcast_to([P, m, w])
                dve.wait_ge(scores, b + 1)
                if b:
                    dve.wait_ge(p_T, b)
                nc.vector.scalar_tensor_tensor(pr, src, HD ** -0.5, mask, ALU.mult, ALU.add).then_inc(scores_read, 1)
                dve.wait_ge(scores_read, b + 1)
                mx = stats[:, MX:MX + m]
                step(nc.vector.reduce_max(mx, pr, AX))
                mx2 = mx.rearrange("p (b a) -> p b a", b=2)
                sink = SINK[:, h0:h1].rearrange("p (a b) -> p b a", b=2)
                step(nc.vector.tensor_tensor(mx2, mx2, sink, ALU.max))
                nc.vector.tensor_tensor(stats[:, SD:SD + m].rearrange("p (b a) -> p b a", b=2), sink, mx2, ALU.subtract)
                nc.vector.tensor_tensor(pr, pr, mx.unsqueeze(2).broadcast_to([P, m, w]), ALU.subtract).then_inc(exp_in, 1)

            def softmax_sum(b):
                g, tb, h0, h1, w = BATCH[b]
                m = h1 - h0
                dve.wait_ge(exp_out, b + 1)
                pr = PR[:, 0:m * w].rearrange("p (a b) -> p a b", a=m)
                r = stats[:, RV + 8 * (b % 2):RV + 8 * (b % 2) + m]
                step(nc.vector.reduce_sum(r, pr, AX))
                step(nc.vector.tensor_tensor(r, r, stats[:, ES:ES + m], ALU.add))
                step(nc.vector.reciprocal(r, r))

            def o_rows(b):
                g, tb, h0, h1, w = BATCH[b]
                m = h1 - h0
                dve.wait_ge(o_ready, b + 1)
                r = stats[:, RV + 8 * (b % 2):RV + 8 * (b % 2) + m]
                nc.vector.tensor_tensor(Y[:, tb, h0 * HD:h1 * HD].rearrange("p (a b d) -> p a b d", b=2, d=HD),
                                        ps[:, 6, 0:m * HD].rearrange("p (a b d) -> p a b d", b=2, d=HD),
                                        r.rearrange("p (b a) -> p a b", b=2).unsqueeze(3).broadcast_to([P, m // 2, 2, HD]),
                                        ALU.mult).then_inc(o_out, 1)

            def p_copies(b):
                dve.wait_ge(p_T, b + 1)
                nc.vector.tensor_copy(PT, ps[:, 6:8, :].rearrange("p a (b c) -> p (a b) c", b=4)).then_inc(p_copied, 1)

            def rope_r(k):
                rope(k % TB, (QR, KR)[k // TB], RH, RD // 2, 32)

            def r_copies(r):
                dve.wait_ge(r_T, r + 1)
                nc.vector.tensor_copy(QRT[:, r], ps[:, 4, :].rearrange("p (a b) -> p a b", a=2))
                nc.vector.tensor_copy(KRT[:, r % 2], ps[:, 5, :].rearrange("p (a b) -> p a b", a=2)).then_inc(r_copied, 1)

            def inner_decay(r):
                dve.wait_ge(inner, r + 1)
                nc.vector.tensor_tensor(IT[:, r], ps[:, 6, 0:T].rearrange("p (a b) -> p a b", a=TB),
                                        DEC[:, r, :].unsqueeze(1).broadcast_to([P, TB, P]), ALU.mult).then_inc(inner_out, 1)

            def kz_rows(r):
                if r >= 2:
                    dve.wait_ge(state, r - 1)
                nc.vector.tensor_scalar(KZ[:, r % 2, :], H[:, 0, KR + r * RD:KR + (r + 1) * RD], ZX[:, 0, r:r + 1],
                                        None, ALU.mult).then_inc(kz_ready, 1)

            def state_copy(r):
                dve.wait_ge(state, r + 1)
                nc.vector.tensor_copy(ST[:, r % 2], ps[:, 7, :].rearrange("p (a b) -> p a b", a=2)).then_inc(state_out, 1)

            def cross_rows(r):
                dve.wait_ge(ret_o, r + 1)
                nc.vector.tensor_copy(Y[:, :, 1024 + r * RD:1024 + (r + 1) * RD],
                                      ps[:, 6, :].rearrange("p (a b) -> p a b", a=TB)).then_inc(ret_o_out, 1)
                dve.wait_ge(ret_o_out, r + 1)
                y = Y[:, 1, 1024 + r * RD:1024 + (r + 1) * RD]
                nc.vector.scalar_tensor_tensor(y, ps[:, 7, 0:RD], ZX[:, 1, r:r + 1], y, ALU.mult, ALU.add).then_inc(ret_cross, 1)

            SQA = at(GN_AT, 2, 1024)

            def att_variances(_):
                dve.wait_ge(o_out, len(BATCH))
                step(nc.vector.tensor_tensor(SQA, Y[:, :, 0:1024], Y[:, :, 0:1024], ALU.mult))
                ms = stats[:, A_SS:A_SS + 32].rearrange("p (a b) -> p a b", a=TB)
                for tb in range(TB):
                    ins = nc.vector.reduce_sum(ms[:, tb, :], SQA[:, tb, :].rearrange("p (a b) -> p a b", a=QH), AX)
                step(ins)
                nc.vector.tensor_scalar(stats[:, A_VAR:A_VAR + 32], stats[:, A_SS:A_SS + 32], 1.0 / HD, EPS,
                                        ALU.mult, ALU.add).then_inc(var_ready, 1)

            def att_norm(_):
                inverse_root(3, A_VAR, A_ROOT, A_R, 32)
                for tb in range(TB):
                    ya = Y[:, tb, 0:1024].rearrange("p (a b) -> p a b", a=QH)
                    r = stats[:, A_R + 16 * tb:A_R + 16 * tb + 16]
                    ins = nc.vector.tensor_tensor(ya, ya, r.unsqueeze(2).broadcast_to([P, QH, HD]), ALU.mult)
                ins.then_inc(y_ready, 1)

            def ret_moments(r):
                dve.wait_ge(ret_cross, r + 1)
                for tb in range(TB):
                    ins = nc.vector.bn_stats(BN[:, r * TB + tb, :], Y[:, tb, 1024 + r * RD:1024 + (r + 1) * RD])
                step(ins)
                for tb in range(TB):
                    ins = nc.vector.bn_aggr(MV[:, r * TB + tb, :], BN[:, r * TB + tb, :])
                step(ins)

            def ret_norm(_):
                nc.vector.tensor_scalar(stats[:, R_VAR:R_VAR + 8], MV[:, :, 1], GN_EPS, None, ALU.add).then_inc(var_ready, 1)
                inverse_root(4, R_VAR, R_ROOT, R_R, 8)
                dve.wait_ge(gate_ready, TB)
                for r in range(RH):
                    cols = slice(1024 + r * RD, 1024 + (r + 1) * RD)
                    for tb in range(TB):
                        k = r * TB + tb
                        ins = nc.vector.tensor_scalar(Y[:, tb, cols], Y[:, tb, cols], MV[:, k, 0:1],
                                                      stats[:, R_R + k:R_R + k + 1], ALU.subtract, ALU.mult)
                    step(ins)
                    nc.vector.tensor_tensor(Y[:, :, cols], Y[:, :, cols], H[:, :, GR + r * RD:GR + (r + 1) * RD],
                                            ALU.mult).then_inc(y_ready, 1)

            def memory_keys(_):
                dve.wait_ge(used, W_XK + 8)
                nc.vector.tensor_tensor(KX, ps[:, 2:6, 0:T], RB.unsqueeze(1).broadcast_to([P, XH, T]), ALU.mult).then_inc(tile_out, 1)

            do = {"tile": in_tile, "rope_a": rope_a, "qk": qk_copies, "sin": softmax_in, "ssum": softmax_sum,
                  "o": o_rows, "pt": p_copies, "rope_r": rope_r, "rc": r_copies, "dec": inner_decay, "kz": kz_rows,
                  "st": state_copy, "cross": cross_rows, "att": att_variances, "att_norm": att_norm,
                  "moments": ret_moments, "ret_norm": ret_norm, "keys": memory_keys,
                  "mem": lambda b: split_low(A_MEM, b), "y": lambda b: split_low(A_Y, b),
                  "rb": lambda _: inverse_by_token(1, 7)}
            for what, k in DVE_ORDER:
                do[what](k)

            def out_tile(first, t, pieces, banks, other):
                dve.wait_ge(used, first + pieces * (t + 1))
                cols = slice(512 * t, 512 * t + 512)
                nc.vector.tensor_tensor(X1[:, :, cols], ps[:, banks:banks + 2, :], other[:, :, cols], ALU.add).then_inc(tile_out, 1)

            dve.wait_ge(xr_in[0], 16)
            dve.wait_ge(xr_in[1], 16)
            for t in range(3):
                out_tile(W_OUT, t, 8, 2 * (t % 2), XR)
            for b in range(6):
                split_low(A_X1, b)
            out_tile(W_OUT, 3, 8, 2, XR)
            for b in (6, 7):
                split_low(A_X1, b)

            for b in range(4):
                split_low(A_MEM2, b)
            variances(N_X1)
            split_low(A_MEM2, 4)
            inverse_rms(5, N_X1)
            step(nc.vector.tensor_scalar(stats[:, SC:SC + 2], stats[:, R + N_X1:R + N_X1 + 2], XD ** -0.5, None, ALU.mult))
            split_low(A_MEM2, 5)
            split_low(A_MEM2, 6)
            dve.wait_ge(used, W_XQ + 8)
            nc.vector.tensor_copy(QXT[:, 0:2, :], ps[:, 0:2, 0:T])
            nc.vector.tensor_copy(QXT[:, 2:4, :], ps[:, 4:6, 0:T]).then_inc(tile_out, 1)
            split_low(A_MEM2, 7)
            dve.wait_ge(x_scores, 1)
            sc = ps[:, 4:8, :].rearrange("p a (b c) -> p (a b) c", b=TB)
            step(nc.vector.reduce_max(stats[:, CM:CM + 8], sc, AX))
            cm = stats[:, CM:CM + 8].rearrange("p (a b) -> p a b", b=TB)
            nm = stats[:, NM:NM + 8].rearrange("p (a b) -> p a b", b=TB)
            step(nc.vector.tensor_tensor(nm, cm, stats[:, SC:SC + 2].unsqueeze(1).broadcast_to([P, XH, TB]), ALU.mult))
            nc.vector.tensor_scalar(nm, nm, -1.0, None, ALU.mult).then_inc(x_max, 1)
            dve.wait_ge(x_exp, 1)
            step(nc.vector.reciprocal(stats[:, CR:CR + 8], stats[:, SM:SM + 8]))
            for h in range(XH):
                px = PX[:, h * TB:(h + 1) * TB, :]
                nc.vector.tensor_tensor(px, px, stats[:, CR + h * TB:CR + (h + 1) * TB].unsqueeze(2).broadcast_to([P, TB, T]),
                                        ALU.mult).then_inc(x_prob, 1)
            for h in range(XH):
                dve.wait_ge(x_pT, h + 1)
                nc.vector.tensor_copy(PXT[:, h], ps[:, 4 + h, :].rearrange("p (b c) -> p b c", b=TB)).then_inc(x_pT_out, 1)
            dve.wait_ge(used, W_XV + 8)
            for mb in range(TB):
                ins = nc.vector.tensor_scalar(VX[:, mb, :], ps[:, 2 + mb, :], stats[:, R + N_MEM + mb:R + N_MEM + mb + 1], None, ALU.mult)
            ins.then_inc(tile_out, 1)
            for h in range(XH):
                dve.wait_ge(xh_ready, A_O + h + 1)
                m = DC - XH + h
                nc.vector.tensor_tensor(xl[:, m, :], ps[:, h, 0:T], xh[:, m, :], ALU.subtract).then_inc(xl_ready, 1)
            out_tile(W_XO, 0, 2, 4, X1)
            out_tile(W_XO, 1, 2, 6, X1)
            split_low(A_X2, 0)
            split_low(A_X2, 1)
            out_tile(W_XO, 2, 2, 4, X1)
            for b in range(2, 6):
                split_low(A_X2, b)
            out_tile(W_XO, 3, 2, 6, X1)
            split_low(A_X2, 6)
            split_low(A_X2, 7)

            variances(N_X2)
            inverse_rms(6, N_X2)
            diagonal(N_X2)

            def query_tile(t):
                dve.wait_ge(used, W_PQ + 8 * t + 8)
                b = 2 * (t % 2)
                nc.vector.tensor_copy(QPT[:, 4 * t:4 * t + 2, :], ps[:, b:b + 2, 0:T])
                nc.vector.tensor_copy(QPT[:, 4 * t + 2:4 * t + 4, :], ps[:, b + 4:b + 6, 0:T]).then_inc(tile_out, 1)

            query_tile(0)
            inverse_by_token(2, 0)
            query_tile(1)
            query_tile(2)
            for b in range(8):
                pair = slice(2 * b, 2 * b + 2)
                dve.wait_ge(used, U0 - 8 + b + 1)
                step(nc.vector.tensor_tensor(TMP[:, pair, :], xh[:, pair, :], xl[:, pair, :], ALU.add))
                nc.vector.tensor_tensor(TMP[:, pair, :], TMP[:, pair, :], RB.unsqueeze(1).broadcast_to([P, 2, T]),
                                        ALU.mult).then_inc(rescaled, 1)
                if b:
                    split_low(A_NORMED, b - 1)
            split_low(A_NORMED, 7)
            query_tile(3)
            for tb in range(TB):
                dve.wait_ge(key_scores, tb + 1)
                nc.vector.tensor_scalar(S[:, tb * PH:(tb + 1) * PH, :],
                                        ps[:, 4:8, :].rearrange("p a (b c) -> p (a b) c", b=2),
                                        stats[:, R + N_X2 + tb:R + N_X2 + tb + 1], None, ALU.mult).then_inc(key_scores_out, 1)
            dve.wait_ge(key_scores_out, 2)
            nc.vector.memset(W[:, C_ONES:C_FREE, :], 1.0)

            o = TK_AT
            def small(*dims):
                nonlocal o
                v = at(o, *dims)
                m = 1
                for d in dims:
                    m *= d
                o += m
                return v
            GE = small(TB * PH, TOPK)
            CH = small(2, TB * PH * TOPK)
            cur, cur2, v, ixf = small(2, NK), small(2, NK), small(2, TOPK), small(2, TOPK)
            ix = small(2, TOPK).bitcast(U32)
            cand, cand2, top = small(TOPK * TOPK), small(TOPK * TOPK), small(TOPK)
            where = small(TOPK).bitcast(U32)
            ab, abf = small(2, TOPK).bitcast(U32), small(2, TOPK)
            oh = small(2, TOPK, TOPK)
            assert o <= IOTA_AT
            LOW = -3.0e38
            with dve.Fori(0, TB * PH) as r:
                k = [0]

                def tick(ins):
                    k[0] += 1
                    ins.then_inc(topk, 1)
                    dve.wait_ge(topk, k[0])

                tick(nc.vector.tensor_copy(cur, S[:, bass.ds(r, 1), :].rearrange("p a (b c) -> p (a b) c", b=2)))
                for c, half in ((cur, 0), (cur2, 8)):
                    for p in range(2):
                        ins = nc.vector.max(v[:, p, half:half + 8], c[:, p, :])
                    tick(ins)
                    for p in range(2):
                        ins = nc.vector.max_index(ix[:, p, half:half + 8], v[:, p, half:half + 8], c[:, p, :])
                    if half == 0:
                        for p in range(2):
                            ins = nc.vector.match_replace(cur2[:, p, :], v[:, p, 0:8], cur[:, p, :], LOW)
                    tick(ins)
                tick(nc.vector.tensor_copy(ixf, ix))
                tick(nc.vector.tensor_tensor(cand.rearrange("p (a b) -> p a b", a=TOPK),
                                             v[:, 0, :].unsqueeze(2).broadcast_to([P, TOPK, TOPK]),
                                             v[:, 1, :].unsqueeze(1).broadcast_to([P, TOPK, TOPK]), ALU.add))
                tick(nc.vector.max(top[:, 0:8], cand))
                tick(nc.vector.max_index(where[:, 0:8], top[:, 0:8], cand))
                tick(nc.vector.match_replace(cand2, top[:, 0:8], cand, LOW))
                tick(nc.vector.max(top[:, 8:16], cand2))
                tick(nc.vector.max_index(where[:, 8:16], top[:, 8:16], cand2))
                tick(nc.vector.tensor_copy(GE[:, bass.ds(r, 1), :], top.unsqueeze(1)))
                tick(nc.vector.tensor_scalar(ab[:, 0, :], where, 4, None, ALU.logical_shift_right))
                tick(nc.vector.tensor_scalar(ab[:, 1, :], where, 15, None, ALU.bitwise_and))
                tick(nc.vector.tensor_copy(abf, ab))
                tick(nc.vector.tensor_tensor(oh, iota[:, 0:TOPK].unsqueeze(1).unsqueeze(1).broadcast_to([P, 2, TOPK, TOPK]),
                                             abf.unsqueeze(3).broadcast_to([P, 2, TOPK, TOPK]), ALU.is_equal))
                tick(nc.vector.tensor_tensor(oh, oh, ixf.unsqueeze(2).broadcast_to([P, 2, TOPK, TOPK]), ALU.mult))
                tick(nc.vector.reduce_sum(CH[:, :, bass.ds(r * TOPK, TOPK)], oh, AX))
                dve.sem_clear(topk)
            top1 = stats[:, TOP:TOP + 16]
            step(nc.vector.tensor_copy(top1.unsqueeze(2), GE[:, :, 0:1]))
            nc.vector.tensor_tensor(GE, GE, top1.unsqueeze(2).broadcast_to([P, 16, TOPK]), ALU.subtract).then_inc(top_ready, 1)
            dve.wait_ge(top_exp, 1)
            step(nc.vector.reduce_sum(top1, GE, AX))
            step(nc.vector.reciprocal(top1, top1))
            nc.vector.tensor_tensor(GE, GE, top1.unsqueeze(2).broadcast_to([P, 16, TOPK]), ALU.mult).then_inc(gates_ready, 1)
            dve.wait_ge(table_T, 1)
            nc.vector.tensor_copy(i1_table[:, :], ps[:, 3, 0:T])
            part, rest = at(TK_AT, 2 * T)[:, 0:T // 2].bitcast(BF16), at(TK_AT + T, T)
            step(nc.vector.tensor_copy(rest, ps[:, 5, 0:T]))
            for k in range(3):
                step(nc.vector.tensor_copy(part, rest))
                ins = nc.vector.tensor_copy(parts_table[:, k, :], part)
                if k < 2:
                    ins = nc.vector.tensor_tensor(rest, rest, part, ALU.subtract)
                step(ins)
            step(nc.vector.memset(W[:, C_FREE:NK, :], 1.0))

            def hot_i1(g, q):
                for m in range(2):
                    t = bass.ds(g * 2 + m, 1)
                    parts = parts_table[:, :, t].broadcast_to([P, 3, P])
                    ins = nc.vector.scalar_tensor_tensor(hot1_rows[:, q, m], iota[:, :].unsqueeze(1).broadcast_to([P, 3, P]),
                                                         i1_table[:, t], parts, ALU.is_equal, ALU.mult)
                ins.then_inc(hot1, 1)

            def hot_i2(g):
                nc.vector.tensor_tensor(hot2_row[:, :, :], iota[:, :].unsqueeze(1).broadcast_to([P, 2, P]),
                                        i2_table[:, bass.ds(g * 2, 2)].unsqueeze(2).broadcast_to([P, 2, P]),
                                        ALU.is_equal).then_inc(hot2, 1)

            def take_chunk(k0, c, pairs):
                dve.wait_ge(gelu_done, k0 + (c + 1 - C_ONES))
                if not (isinstance(pairs, int) and pairs == 0):
                    dve.wait_ge(gated, pairs)
                nc.vector.tensor_tensor(W[:, k0 + c, :], ps[:, c % ACT_BANKS, 0:T], W[:, k0 + c, :], ALU.mult).then_inc(act_taken, 1)

            def gate_step(i, j, last=TOK_PAIRS):
                g = i * BODY + j
                dve.wait_ge(gate_mat, g + 1)
                if last > j + 1:
                    hot_i2(g + 1)
                if j % 2 == 0:
                    take_chunk(i * CHUNKS_PER_BODY + (C_GATE - CHUNKS_PER_BODY), j // 2 - 2 + CHUNKS_PER_BODY, g)
                dve.wait_ge(act_taken, i * CHUNKS_PER_BODY + (C_ONES + 1 + j // 2))
                w = W[:, :, bass.ds(g * 2, 2)]
                nc.vector.tensor_tensor(w, ps[:, 4 + j % 2, 0:T].rearrange("p (m k) -> p k m", m=2), w, ALU.mult).then_inc(gated, 1)
                if last > j + 2:
                    hot_i1(g + 2, j % 2)

            hot_i2(0)
            hot_i1(0, 0)
            hot_i1(1, 1)
            full = TOK_PAIRS // BODY
            for j in range(BODY):
                gate_step(0, j)
            with dve.Fori(1, full) as i:
                for j in range(BODY):
                    gate_step(i, j)
            for j in range(TOK_PAIRS - full * BODY):
                gate_step(full, j, TOK_PAIRS - full * BODY)
            def v_step(n0, k0, j, split=True):
                if split:
                    dve.wait_ge(hi_done, n0 + (V0 + j + 1))
                    s = (V0 + j) % SPL
                    nc.vector.tensor_tensor(wlo[:, s, :], raw[:, j % RAW, :], whi[:, s, :], ALU.subtract).then_inc(lo_v_done, 1)
                if j % 2 == 0:
                    dve.wait_ge(ghi_done, k0 + (j // 2 + 1))
                    nc.vector.tensor_tensor(gate_lo[:, j // 2 % 2, :], W[:, k0 + j // 2, :],
                                            gate_hi[:, j // 2 % 2, :], ALU.subtract).then_inc(glo_done, 1)

            for k in range(C_ONES + TOK_PAIRS // 2, NK - 1):
                take_chunk(0, k, TOK_PAIRS)
            v_step(0, 0, 0, split=False)
            v_step(0, 0, 2, split=False)
            take_chunk(0, NK - 1, TOK_PAIRS)
            for j in range(4, BODY):
                v_step(0, 0, j, split=V0 + j >= POOL_END)
            with dve.Fori(1, 2 * NK // BODY) as i:
                for j in range(BODY):
                    v_step(i * BODY, i * CHUNKS_PER_BODY, j)
            for j in range(2 * NK // BODY * BODY, 2 * NK):
                v_step(0, 0, j)

            dve.wait_ge(x2_in, 32)
            dve.wait_ge(last_gain_in, 16)

            def residual(tb):
                dve.wait_ge(rows_done, tb + 1)
                for half in range(2):
                    cols = slice(half * 1024, (half + 1) * 1024)
                    b = 4 * tb + 2 * half
                    nc.vector.tensor_tensor(x2_back[:, tb, cols], ps[:, b:b + 2, :].rearrange("p a b -> p (a b)"),
                                            x2_back[:, tb, cols], ALU.add).then_inc(x3_ready, 1)
                dve.wait_ge(x3_ready, 2 * tb + 2)

            def gained(tb):
                step(nc.vector.tensor_tensor(FINAL[:, tb, 0:1024], x2_back[:, tb, 0:1024], last_gain[:, 0:1024], ALU.mult))

            def last_variance(tb):
                dve.wait_ge(squares, 8 + 2 * tb + 2)
                k = LAST_SS + 2 * tb
                v = stats[:, VAR + N_LAST + tb:VAR + N_LAST + tb + 1]
                step(nc.vector.tensor_tensor(v, stats[:, k:k + 1], stats[:, k + 1:k + 2], ALU.add))
                nc.vector.tensor_scalar(v, v, 1.0 / D, EPS, ALU.mult, ALU.add).then_inc(var_ready, 1)

            def last_norm(tb):
                inverse_root(7 + tb, VAR + N_LAST + tb, ROOT + N_LAST + tb, R + N_LAST + tb, 1, last_r)
                dve.wait_ge(last_r, tb + 1)
                nc.vector.tensor_scalar(x2_back[:, tb, 0:1024], FINAL[:, tb, 0:1024],
                                        stats[:, R + N_LAST + tb:R + N_LAST + tb + 1], None, ALU.mult).then_inc(y_out[0], 1)

            residual(0)
            gained(0)
            last_variance(0)
            residual(1)
            last_norm(0)
            gained(1)
            last_variance(1)
            last_norm(1)

        @block.tensor
        def _(pe):
            def transpose_pair(v, b, rows, counts):
                for ready, count in counts:
                    pe.wait_ge(ready, count)
                for c in range(2):
                    for tb in range(TB):
                        m = 2 * b + c
                        ins = nc.tensor.transpose(ps[:, pair_bank(v, b), (c * TB + tb) * P:(c * TB + tb + 1) * P],
                                                  rows[:, tb, m * P:(m + 1) * P], ident)
                ins.then_inc(xT_ready, 1)

            def three(out_ap, sh, sl, mh, ml, start, stop):
                nc.tensor.matmul(out_ap, sh, mh, start=start, stop=False)
                nc.tensor.matmul(out_ap, sh, ml, start=False, stop=False)
                return nc.tensor.matmul(out_ap, sl, mh, start=False, stop=stop)

            def rows_piece(n, c0, width, last_chunk, banks, at_chunk=0):
                pe.wait_ge(lo_done, n + 1)
                s = n % SPL
                for tb in range(TB):
                    for c in range(PW // width):
                        m = c0 + c
                        t = slice(tb * P, (tb + 1) * P)
                        cols = slice(c * width, (c + 1) * width)
                        ins = three(ps[:, banks + tb, 0:width], xh[:, at_chunk + m, t], xl[:, at_chunk + m, t],
                                    whi[:, s, cols], wlo[:, s, cols], m == 0, m == last_chunk)
                ins.then_inc(used, 1)

            def cols_piece(n, c0, last_chunk, banks):
                pe.wait_ge(lo_done, n + 1)
                s = n % SPL
                for c in range(2):
                    for b in range(4):
                        m = c0 + c
                        cols = slice(c * 512 + b * P, c * 512 + (b + 1) * P)
                        ins = three(ps[:, banks[b], 0:T], whi[:, s, cols], wlo[:, s, cols], xh[:, m, :], xl[:, m, :],
                                    m == 0, m == last_chunk)
                ins.then_inc(used, 1)

            def inverse_by_token(count, bank):
                pe.wait_ge(diag_ready, count)
                nc.tensor.matmul(ps[:, bank, 0:T], ONES, DIAG.rearrange("p a b -> p (a b)"), start=True, stop=True).then_inc(rb_ready, 1)

            def qk_transposes(g):
                if g == 0:
                    pe.wait_ge(ident_in, 16)
                    pe.wait_ge(roped_a, 4)
                    for k in range(KVH):
                        for tb in range(TB):
                            nc.tensor.transpose(ps[:, 6, (k * TB + tb) * P:(k * TB + tb + 1) * P],
                                                at(P_AT + (tb * KVH + k) * P, P), ident)
                else:
                    pe.wait_ge(qk_copied, 1)
                    pe.wait_ge(rb_out, 1)
                for c in range(4):
                    for tb in range(TB):
                        m = c * TB + tb
                        ins = nc.tensor.transpose(ps[:, (4 if g == 0 else 6) + m // 4, (m % 4) * P:(m % 4 + 1) * P],
                                                  H[:, tb, (4 * g + c) * P:(4 * g + c + 1) * P], ident)
                ins.then_inc(qk_T, 1)

            def head_scores(b):
                g, tb, h0, h1, w = BATCH[b]
                pe.wait_ge(qk_copied, 1 + g)
                if b:
                    pe.wait_ge(scores_read, b)
                for h in range(h0, h1):
                    lo = h % 2 * HD
                    col = (h - h0) // 2 * w
                    ins = nc.tensor.matmul(ps[:, 4 + h % 2, col:col + w],
                                           QAT[lo:lo + HD, h // 2, tb * P:(tb + 1) * P],
                                           KT[lo:lo + HD, g, 0:w], start=True, stop=True)
                ins.then_inc(scores, 1)

            def p_transposes(b):
                g, tb, h0, h1, w = BATCH[b]
                pe.wait_ge(exp_out, b + 1)
                pe.wait_ge(qk_copied, 2)
                if b:
                    pe.wait_ge(o_out, b)
                for m in range(8):
                    ins = nc.tensor.transpose(ps[:, 6 + m // 4, (m % 4) * P:(m % 4 + 1) * P], PR[:, m * P:(m + 1) * P],
                                              ident)
                ins.then_inc(p_T, 1)

            def head_outputs(b):
                g, tb, h0, h1, w = BATCH[b]
                pe.wait_ge(p_copied, b + 1)
                nk = w // P
                for k in range(h1 - h0):
                    for kc in range(nk):
                        q = k % 2 * ((h1 - h0) // 2) + k // 2
                        ins = nc.tensor.matmul(ps[:, 6, k * HD:(k + 1) * HD], PT[:, q * nk + kc, :],
                                               H[:, kc, VA + g * HD:VA + (g + 1) * HD], start=kc == 0, stop=kc == nk - 1)
                ins.then_inc(o_ready, 1)

            def r_transposes(r):
                pe.wait_ge(roped, 6)
                if r == 0:
                    pe.wait_ge(scores_read, len(BATCH))
                else:
                    pe.wait_ge(r_copied, r)
                for k, c0 in ((0, QR), (1, KR)):
                    for dc in range(2):
                        for tb in range(TB):
                            ins = nc.tensor.transpose(ps[:, 4 + k, (dc * TB + tb) * P:(dc * TB + tb + 1) * P],
                                                      H[:, tb, c0 + r * RD + dc * P:c0 + r * RD + (dc + 1) * P], ident)
                ins.then_inc(r_T, 1)

            def r_inner(r):
                pe.wait_ge(r_copied, r + 1)
                if r == 0:
                    pe.wait_ge(o_out, len(BATCH))
                else:
                    pe.wait_ge(ret_o_out, r)
                for tb in range(TB):
                    for dc in range(2):
                        ins = nc.tensor.matmul(ps[:, 6, tb * P:(tb + 1) * P], KRT[:, r % 2, dc, tb * P:(tb + 1) * P],
                                               QRT[:, r, dc, tb * P:(tb + 1) * P], start=dc == 0, stop=dc == 1)
                ins.then_inc(inner, 1)

            def r_state(r):
                pe.wait_ge(kz_ready, r + 1)
                pe.wait_ge(tile_out, 9)
                if r:
                    pe.wait_ge(ret_cross, r)
                for dc in range(2):
                    ins = nc.tensor.matmul(ps[:, 7, dc * RD:(dc + 1) * RD], KZ[:, r % 2, dc * P:(dc + 1) * P],
                                           H[:, 0, VR + r * RD:VR + (r + 1) * RD], start=True, stop=True)
                ins.then_inc(state, 1)

            def r_out(r):
                pe.wait_ge(inner_out, r + 1)
                pe.wait_ge(state_out, r + 1)
                for tb in range(TB):
                    nc.tensor.matmul(ps[:, 6, tb * RD:(tb + 1) * RD], IT[:, r, tb, :], H[:, tb, VR + r * RD:VR + (r + 1) * RD],
                                     start=True, stop=True)
                for dc in range(2):
                    ins = nc.tensor.matmul(ps[:, 7, 0:RD], QRT[:, r, dc, P:T], ST[:, r % 2, dc, :], start=dc == 0, stop=dc == 1)
                ins.then_inc(ret_o, 1)

            do = {"qk": qk_transposes, "s": head_scores, "pt": p_transposes, "o": head_outputs, "rt": r_transposes,
                  "ri": r_inner, "rs": r_state, "ro": r_out, "rb": lambda _: inverse_by_token(1, 7)}
            n = W_IN
            for t, (c0, w) in enumerate(IN_TILES):
                if t >= 2:
                    pe.wait_ge(tile_out, t - 1)
                per = PW // w
                for j in range(DC // per):
                    if t == 0:
                        pe.wait_ge(xl_ready, A_X + j + 1)
                    rows_piece(n, j * per, w, DC - 1, 2 * (t % 2))
                    for what, k in PE_POINTS.get(n, ()):
                        do[what](k)
                    n += 1
            assert n == W_XK
            do["ro"](RH - 1)

            pe.wait_ge(tile_out, 10)
            pe.wait_ge(r_copied, RH)
            for j in range(8):
                pe.wait_ge(xl_ready, A_MEM + j + 1)
                cols_piece(W_XK + j, 2 * j, DC - 1, (2, 3, 4, 5))
                if j == 4:
                    for b in (0, 1):
                        transpose_pair(A_Y, b, Y, [(y_ready, 1), (ret_cross, RH)])

            pe.wait_ge(tile_out, N_IN)
            for t in range(4):
                if t == 1:
                    pe.wait_ge(tile_out, N_XK)
                if t >= 2:
                    pe.wait_ge(tile_out, N_XK + t - 1)
                if t == 3:
                    for b in range(4):
                        transpose_pair(A_X1, b, X1, [(tile_out, N_XK + 1 + b // 2)])
                for j in range(8):
                    if t == 0:
                        pe.wait_ge(xl_ready, A_Y + j + 1)
                    rows_piece(W_OUT + 8 * t + j, 2 * j, 512, DC - 1, 2 * (t % 2))
                    if t == 0:
                        for b in {0: (2, 3), 1: (4, 5), 3: (6, 7)}.get(j, ()):
                            free = (tile_out, N_XK) if b < 4 else (xl_ready, A_Y + b - 3)
                            transpose_pair(A_Y, b, Y, [(y_ready, max(1, b - 2)), free])
                    if t == 3 and j == 3:
                        for b in (4, 5):
                            transpose_pair(A_X1, b, X1, [(tile_out, N_XK + 3), (xl_ready, A_X1 + b - 3)])

            pe.wait_ge(xl_ready, A_X1 + 6)
            for j in range(8):
                pe.wait_ge(xl_ready, A_X1 + j + 1)
                cols_piece(W_XQ + j, 2 * j, DC - 1, (0, 1, 4, 5))
                if j == 1:
                    for b in (6, 7):
                        transpose_pair(A_X1, b, X1, [(tile_out, N_OUT), (xl_ready, A_X1 + b - 3)])
            for j in range(8):
                pe.wait_ge(xl_ready, A_MEM2 + j + 1)
                rows_piece(W_XV + j, 2 * j, 512, DC - 1, 2)
                if j == 0:
                    pe.wait_ge(tile_out, N_XQ)
                    for h in range(XH):
                        for tb in range(TB):
                            ins = nc.tensor.matmul(ps[:, 4 + h, tb * T:(tb + 1) * T], QXT[:, h, tb * P:(tb + 1) * P], KX[:, h, :],
                                                   start=True, stop=True)
                    ins.then_inc(x_scores, 1)
                if j == 5:
                    for h in range(XH):
                        pe.wait_ge(x_prob, h + 1)
                        for mb in range(TB):
                            for tb in range(TB):
                                ins = nc.tensor.transpose(ps[:, 4 + h, mb * T + tb * P:mb * T + (tb + 1) * P],
                                                          PX[:, h * TB + tb, mb * P:(mb + 1) * P], ident)
                        ins.then_inc(x_pT, 1)
            pe.wait_ge(tile_out, N_XV)
            for h in range(XH):
                pe.wait_ge(x_pT_out, h + 1)
                for mb in range(TB):
                    ins = nc.tensor.matmul(ps[:, h, 0:T], VX[:, mb, h * XD:(h + 1) * XD], PXT[:, h, mb, :],
                                           start=mb == 0, stop=mb == 1)
                ins.then_inc(x_oT, 1)
            pe.wait_ge(x_pT_out, XH)
            for t in range(4):
                if t >= 2:
                    pe.wait_ge(tile_out, N_XV + t - 1)
                for j in range(2):
                    if t == 0:
                        pe.wait_ge(xl_ready, A_O + 2 * j + 2)
                    n = 2 * t + j
                    rows_piece(W_XO + n, 2 * j, 512, XH - 1, 4 + 2 * (t % 2), DC - XH)
                    for b in {3: (0, 1), 5: (2, 3), 6: (4, 5)}.get(n, ()):
                        free = A_O + b + 1 if b < 4 else A_X2 + b - 3
                        transpose_pair(A_X2, b, X1, [(tile_out, N_XV + 1 + b // 2), (xl_ready, free)])

            pe.wait_ge(tile_out, N_XV + 3)
            pe.wait_ge(xl_ready, A_X2 + 6)
            for t in range(4):
                if t == 1:
                    pe.wait_ge(xl_ready, A_NORMED)
                if t >= 2:
                    pe.wait_ge(tile_out, N_XO + t - 1)
                for j in range(8):
                    if t == 0:
                        pe.wait_ge(xl_ready, A_X2 + j + 1)
                    cols_piece(W_PQ + 8 * t + j, 2 * j, DC - 1, (2, 3, 6, 7) if t % 2 else (0, 1, 4, 5))
                    if t == 0 and j == 1:
                        for b in (6, 7):
                            transpose_pair(A_X2, b, X1, [(tile_out, N_XO), (xl_ready, A_X2 + b - 3)])
                    if t == 1 and j == 6:
                        pe.wait_ge(tile_out, N_XO + 1)
                        inverse_by_token(2, 0)
                if t == 1:
                    pe.wait_ge(rb_out, 2)

            def key_products(tb):
                for hp in range(HP):
                    ins = nc.tensor.matmul(ps[:, 4 + hp // 4, hp % 4 * NK:(hp % 4 + 1) * NK],
                                           QPT[:, hp, tb * P:(tb + 1) * P], SK[:, hp, :], start=True, stop=True)
                ins.then_inc(key_scores, 1)

            def u_piece(i, j):
                if j % 2 == 0 and not (isinstance(i, int) and i == 0 and j < 2 * ACT_BANKS):
                    pe.wait_ge(act_taken, i * CHUNKS_PER_BODY + (j // 2 - ACT_BANKS + 1))
                pe.wait_ge(lo_done, i * BODY + (U0 + j + 1))
                s = j % SPL
                for c in range(8):
                    m = j % 2 * 8 + c
                    cols = slice(c * P, (c + 1) * P)
                    ins = three(ps[:, j // 2 % ACT_BANKS, 0:T], whi[:, s, cols], wlo[:, s, cols], xh[:, m, :], xl[:, m, :],
                                m == 0, m == DC - 1)
                ins.then_inc(used, 1)

            def gate_products(i, j):
                pe.wait_ge(hot1, i * BODY + (j + 1))
                pe.wait_ge(hot2, i * BODY + (j + 1))
                if not (isinstance(i, int) and i == 0 and j < 2):
                    pe.wait_ge(gated, i * BODY + (j - 1))
                for m in range(2):
                    for part in range(3):
                        ins = nc.tensor.matmul(ps[:, 4 + j % 2, m * P:(m + 1) * P], hot1_rows[:, j % 2, m, part, :],
                                               hot2_row[:, m, :], start=part == 0, stop=part == 2)
                ins.then_inc(gate_mat, 1)

            pe.wait_ge(tile_out, N_PQ - 1)
            pe.wait_ge(keys_in, 16)
            for j in range(BODY):
                if j < 2:
                    pe.wait_ge(xl_ready, A_NORMED + 4 * j + 4)
                u_piece(0, j)
                if j == 2:
                    pe.wait_ge(tile_out, N_PQ)
                    key_products(0)
                if j == 5:
                    pe.wait_ge(key_scores_out, 1)
                    key_products(1)
            pe.wait_ge(key_scores_out, 2)
            with pe.Fori(1, C_TABLES // CHUNKS_PER_BODY) as i:
                for j in range(BODY):
                    u_piece(i, j)
            pe.wait_ge(gates_ready, 1)
            CH = at(TK_AT + 256, 2, T)
            GE = at(TK_AT, T)
            for k in range(3):
                for tb in range(TB):
                    src = (CH[:, k, :] if k < 2 else GE)[:, tb * P:(tb + 1) * P]
                    ins = nc.tensor.transpose(ps[:, 3 + k // 2 * 2, (k % 2 * TB + tb) * P:(k % 2 * TB + tb + 1) * P], src, ident)
            ins.then_inc(table_T, 1)
            with pe.Fori(C_TABLES // CHUNKS_PER_BODY, C_GATE // CHUNKS_PER_BODY) as i:
                for j in range(BODY):
                    u_piece(i, j)
            first = C_GATE // CHUNKS_PER_BODY
            full = TOK_PAIRS // BODY
            for j in range(BODY):
                u_piece(first, j)
                gate_products(0, j)
            with pe.Fori(1, full) as i:
                for j in range(BODY):
                    u_piece(i + first, j)
                    gate_products(i, j)
            for j in range(2 * NK - (first + full) * BODY):
                u_piece(first + full, j)
                if full * BODY + j < TOK_PAIRS:
                    gate_products(full, j)

            def v_products(s, g, half, tb, first=False, last=False):
                for c in range(2):
                    t = slice(tb * P, (tb + 1) * P)
                    cols = slice(c * 512, (c + 1) * 512)
                    ins = three(ps[:, 4 * tb + 2 * half + c, :], gate_hi[:, g, t], gate_lo[:, g, t], whi[:, s, cols],
                                wlo[:, s, cols], first, last)
                return ins

            def v_piece(n0, k0, j, first=False):
                if j % 2 == 0:
                    pe.wait_ge(glo_done, k0 + (j // 2 + 1))
                if isinstance(n0, int) and n0 + V0 + j < POOL_END:
                    pe.wait_ge(lo_done, V0 + j + 1)
                else:
                    pe.wait_ge(lo_v_done, n0 + (V0 - POOL_END + j + 1))
                for tb in (1, 0):
                    if first and j == 0 and tb == 0:
                        pe.wait_ge(act_taken, NK)
                    ins = v_products((V0 + j) % SPL, j // 2 % 2, j % 2, tb, first)
                ins.then_inc(used, 1)

            pe.wait_ge(gated, TOK_PAIRS)
            pe.wait_ge(act_taken, NK - 2)
            for j in range(BODY):
                v_piece(0, 0, j, first=j < 2)
            with pe.Fori(1, 2 * NK // BODY) as i:
                for j in range(BODY):
                    v_piece(i * BODY, i * CHUNKS_PER_BODY, j)
            for j in range(2 * NK // BODY * BODY, 2 * NK - 2):
                v_piece(0, 0, j)
            pe.wait_ge(glo_done, NK)
            for tb in range(TB):
                for half in range(2):
                    if tb == 0:
                        pe.wait_ge(lo_v_done, END - POOL_END - 1 + half)
                    ins = v_products((END - 2 + half) % SPL, (NK - 1) % 2, half, tb, last=True)
                ins.then_inc(rows_done, 1)


BATCH = [(g, tb, h0, h1, w) for g in range(KVH) for tb, h0, h1, w in
         ((0, 8 * g, 8 * g + 8, P), (1, 8 * g, 8 * g + 4, 2 * P), (1, 8 * g + 4, 8 * g + 8, 2 * P))]
TILE_END = []
for _c, _w in IN_TILES:
    TILE_END.append((TILE_END[-1] if TILE_END else W_IN) + DC * _w // PW)


def _half(t, h):
    return TILE_END[t] - 8 + 4 * h + 3


PE_POINTS = {_half(3, 0): [("qk", 0)], _half(3, 1): [("qk", 1), ("s", 0)]}
for _b in range(7):
    _steps = ([("o", _b - 1)] if _b else []) + ([("s", _b + 1)] if _b < 5 else []) + ([("pt", _b)] if _b < 6 else [])
    PE_POINTS[_half(4 + _b // 2, _b % 2)] = _steps
PE_POINTS[_half(7, 1)] = [("rt", 0)]
for _r, _at in enumerate((_half(8, 1), _half(9, 0), _half(9, 1), _half(10, 0))):
    PE_POINTS[_at] = ([("ro", _r - 1)] if _r else []) + ([("rt", _r + 1)] if _r < 3 else []) + [("ri", _r), ("rs", _r)]
PE_POINTS[TILE_END[2] - 1] = [("rb", 0)]

ACT_POINTS = {}


def _act(n, *steps):
    ACT_POINTS.setdefault(n, []).extend(steps)


for _b in range(8):
    _act(_b // 2, ("x", _b))
for _b in range(4):
    _act(2 + _b, ("load_rows", _b))
    _act(7 + _b, ("load_memory_rows", _b))
for _n, _s in ((6, ("load_ident", 0)), (6, ("square_x", 0)), (7, ("square_x", 1)), (9, ("root_x", 0)),
               (11, ("square_mem", 0)), (12, ("square_mem", 1)), (14, ("root_mem", 0)), (15, ("sines", 0))):
    _act(_n, _s)
for _b in range(6):
    _act(_half(4 + _b // 2, _b % 2), ("exp", _b))
_act(_half(8, 0), ("load_memory", 0))
_act(_half(8, 0) + 2, ("load_memory", 1))
_act(_half(8, 1), ("root_att", 0))
for _b in range(8):
    _act(W_XK - 8 + _b + 3, ("mem", _b))
_act(W_XK + 3, ("gates", 0), ("gates", 1))
_act(W_XK + 5, ("root_ret", 0), ("load_x", 0))
_act(W_OUT, ("load_x", 1))
_act(W_XK + 7, ("y", 0), ("y", 1))
_act(W_OUT + 3, ("y", 2), ("y", 3))
_act(W_OUT + 4, ("y", 4), ("y", 5))
_act(W_OUT + 6, ("y", 6), ("y", 7))
for _b in range(6):
    _act(W_XQ - 8 + _b + 3, ("x1", _b))
_act(W_XQ + 4, ("x1", 6), ("x1", 7), ("mem2", 0), ("mem2", 1))
_act(W_XQ + 5, ("square_x1", 0), ("mem2", 2), ("load_keys", 0))
_act(W_XQ + 6, ("square_x1", 1), ("mem2", 3))
_act(W_XQ + 7, ("mem2", 4))
_act(W_XQ + 8, ("root_x1", 0), ("mem2", 5))
_act(W_XQ + 9, ("mem2", 6))
_act(W_XQ + 10, ("mem2", 7))
_act(W_XV + 5, ("cross_exps", 0))
_act(W_XO + 2, ("o", 0), ("o", 1), ("o", 2), ("o", 3))
_act(W_XO + 6, ("x2", 0), ("x2", 1))
_act(W_PQ, ("x2", 2), ("x2", 3))
_act(W_PQ + 1, ("x2", 4), ("x2", 5))
_act(W_PQ + 4, ("x2", 6), ("x2", 7))
_act(W_PQ + 5, ("square_x2", 0), ("store_x2", 0))
_act(W_PQ + 6, ("square_x2", 1))
_act(W_PQ + 7, ("root_x2", 0))
_act(W_PQ + 8, ("store_x2", 1))
for _b in range(8):
    _act(U0 - 8 + min(_b + 4, 10), ("normed", _b))

DVE_ORDER = [("tile", 0), ("tile", 1), ("tile", 2), ("rb", 0), ("rope_a", 0), ("qk", 0), ("tile", 3), ("qk", 1), ("sin", 0)]
for _b in range(7):
    if _b < 6:
        DVE_ORDER.append(("ssum", _b))
    if _b:
        DVE_ORDER.append(("o", _b - 1))
    if _b < 6:
        DVE_ORDER.append(("pt", _b))
    if _b < 5:
        DVE_ORDER.append(("sin", _b + 1))
    if _b in (1, 3):
        DVE_ORDER.append(("tile", 4 + _b // 2))
    if _b in (2, 4):
        DVE_ORDER.append(("rope_r", _b // 4))
    if _b == 5:
        DVE_ORDER.append(("tile", 6))
DVE_ORDER += [("rope_r", 2), ("rope_r", 3), ("kz", 0), ("tile", 7), ("rc", 0), ("att", 0), ("tile", 8)]
for _r in range(4):
    DVE_ORDER += ([("cross", _r - 1)] if _r else []) + [("dec", _r), ("st", _r)] + ([("moments", _r - 1)] if _r else []) + \
                 ([("rc", _r + 1), ("kz", _r + 1)] if _r < 3 else [])
    if _r == 0:
        DVE_ORDER.append(("att_norm", 0))
    if _r == 2:
        DVE_ORDER.append(("tile", 9))
DVE_ORDER += [("mem", _b) for _b in range(8)] + [("tile", 10), ("cross", 3), ("moments", 3), ("ret_norm", 0),
                                                 ("y", 0), ("y", 1), ("keys", 0)]
DVE_ORDER += [("y", _b) for _b in range(2, 8)]


def pair_bank(v, b):
    return b % 4 if v == A_X2 else 4 + (b + 2) % 4 if v == A_Y else 4 + b % 4



def _pieces(w, width):
    per = PW // width
    k = w.shape[0] // P // per
    return w.reshape(k, per, P, width).transpose(0, 2, 1, 3).reshape(k, P, PW)


def kernel(**inputs):
    import numpy as np
    import concourse.bacc as bacc
    from concourse.bass_utils import run_bass_kernel_spmd

    a = {k: np.asarray(v) for k, v in inputs.items()}

    def tiles(w):
        return [_pieces(w[:, c:c + 512], 512) for c in range(0, w.shape[1], 512)]

    w_in = a["w_in"][0]
    front = [_pieces(w_in[:, c:c + w], w) for c, w in IN_TILES]
    for name in ("w_xk", "w_out", "w_xq", "w_xv", "w_xo", "w_peer_q"):
        front += tiles(a[name][0])
    u = a["peer_u"][0].reshape(NK, NK, 2, 8, P).transpose(1, 2, 4, 3, 0).reshape(2 * NK, P, PW)
    v = a["peer_v"][0].reshape(NK, NK, 2, PW).transpose(1, 2, 0, 3).reshape(2 * NK, P, PW)
    lg = np.log1p(-np.exp2(-5.0 - np.arange(RH)))
    i = np.arange(P)
    diff = i[None, :] - i[:, None]
    decay = np.where(diff[None] >= 0, np.exp(np.maximum(diff, 0)[None] * lg[:, None, None]), 0.0) * RD ** -0.5
    zeta = np.exp((P - 1 - i)[:, None] * lg[None, :]) * RD ** -0.5
    xi = np.exp((i + 1)[:, None] * lg[None, :])
    mask = np.stack([i[None, :] > i[:, None], i[None, :] <= i[:, None]], 1)
    theta = np.float32(10000.0)
    inv = np.concatenate([theta ** (-np.arange(0, d, 2, dtype=np.float32) / np.float32(d)) for d in (HD, RD)])
    by_chunk = [g.reshape(DC, P).T for g in (a["mix_norm_gain"][0], a["mem_norm_gain"][0],
                                             np.concatenate([a["att_out_gain"][0], a["ret_out_gain"][0]]),
                                             a["cross_norm_gain"][0], a["ffn_norm_gain"][0])]
    arrays = {
        "x": a["x"], "mem": a["mem"],
        "x_t": a["x"][0].reshape(T, DC, P).transpose(2, 1, 0), "mem_t": a["mem"][0].reshape(T, DC, P).transpose(2, 1, 0),
        "pos": a["positions"].astype(np.int32).reshape(TB, P).T,
        "gains": np.concatenate(by_chunk, 1), "last_gain": a["final_norm_gain"][None],
        "w_front": np.concatenate(front), "w_u": u, "w_v": v,
        "sub_keys": a["peer_sub_keys"][0].reshape(HP, NK, P).transpose(2, 0, 1).reshape(P, HP * NK),
        "sinks": a["att_sinks"].reshape(1, QH),
        "c_ident": np.eye(P, dtype=np.float32), "c_iota": np.tile(i.astype(np.float32), (P, 1)),
        "c_mask": np.where(mask, 0.0, -1e30).astype(np.float32).reshape(P, 2 * P),
        "c_decay": decay.astype(np.float32).transpose(1, 0, 2).reshape(P, RH * P),
        "c_zx": np.concatenate([zeta, xi], 1).astype(np.float32), "c_inv": inv.astype(np.float32)[None],
    }
    arrays = {k: np.ascontiguousarray(v) for k, v in arrays.items()}
    nc = bacc.Bacc("TRN2", target_bir_lowering=False, num_devices=1)
    args = [nc.dram_tensor(f"in_{k}", v.shape, mybir.dt.from_np(v.dtype), kind="ExternalInput").ap()
            for k, v in arrays.items()]
    x2_dram = nc.dram_tensor("x2_scratch", (T, D), F32, kind="Internal").ap()
    out = nc.dram_tensor("out_0", (1, T, D), F32, kind="ExternalOutput").ap()
    hymba_layer(nc, *args, x2_dram, out)
    r = run_bass_kernel_spmd(nc, [{f"in_{k}": v for k, v in arrays.items()}], core_ids=[0])
    return r.results[0]["out_0"]
```
